# Optimizing a Trainium2 kernel written in Bass

```python
import math
import jax
import jax.numpy as jnp
from jax import lax
import numpy as np

D_MODEL = 1024
BATCH = 1
SEQ = 256
DEPTH = 1

A_HEADS = 8
A_HEAD_DIM = 64
A_WIDTH = A_HEADS * A_HEAD_DIM
DILATED_PATTERNS = ((128, 1), (512, 4), (2048, 16))
BAND_BLOCK = 128

B_HEADS = 4
QK_NOPE_DIM = 128
QK_ROPE_DIM = 64
QK_HEAD_DIM = QK_NOPE_DIM + QK_ROPE_DIM
V_HEAD_DIM = 128
Q_LORA_RANK = 256
KV_LORA_RANK = 256
B_WIDTH = B_HEADS * V_HEAD_DIM
ROPE_THETA = 10000.0
Q_BLOCK = 128

MIX_WIDTH = A_WIDTH + B_WIDTH
IN_PROJ_WIDTH = 3 * A_WIDTH + Q_LORA_RANK + KV_LORA_RANK + QK_ROPE_DIM

NUM_BUCKETS = 32
MAX_DISTANCE = 2048

N_EXPERTS = 32
TOP_K = 4
D_FF = D_MODEL
SWIGLU_LIMIT = 7.0
SWIGLU_ALPHA = 1.702
EXPERT_BLOCK = 256

RMS_EPS = 1e-6

kernel_name = 'hybrid_dilated_mla_moe_block'

def rms_norm(x, g):
    xf = x.astype(jnp.float32)
    y = xf * lax.rsqrt(jnp.mean(xf * xf, axis=-1, keepdims=True) + RMS_EPS)
    return (y * g.astype(jnp.float32)).astype(x.dtype)

def t5_bucket(dist):
    max_exact = NUM_BUCKETS // 2
    df = jnp.maximum(dist, 1).astype(jnp.float32)
    log_bucket = max_exact + (jnp.log(df / max_exact) / math.log(MAX_DISTANCE / max_exact)
                              * (NUM_BUCKETS - max_exact)).astype(jnp.int32)
    log_bucket = jnp.minimum(log_bucket, NUM_BUCKETS - 1)
    return jnp.where(dist < max_exact, dist, log_bucket)

def apply_rope(x, cos, sin):
    x1, x2 = jnp.split(x, 2, axis=-1)
    c = cos[None, :, None, :].astype(x.dtype)
    s = sin[None, :, None, :].astype(x.dtype)
    return jnp.concatenate([x1 * c - x2 * s, x1 * s + x2 * c], axis=-1)

def dilated_branch(q, k, v, rel_bias, window, dilation):
    b, s, h, dh = q.shape
    steps = window // dilation
    n = b * dilation
    length = s // dilation
    nb = -(-length // BAND_BLOCK)
    lp = nb * BAND_BLOCK

    def to_classes(t):
        return t.reshape(b, length, dilation, h, dh).transpose(0, 2, 1, 3, 4).reshape(n, length, h, dh)

    def band(t):
        tp = jnp.pad(to_classes(t), ((0, 0), (BAND_BLOCK, lp - length), (0, 0), (0, 0)))
        tp = tp.reshape(n, nb + 1, BAND_BLOCK, h, dh)
        return jnp.concatenate([tp[:, :-1], tp[:, 1:]], axis=2)

    qb = jnp.pad(to_classes(q), ((0, 0), (0, lp - length), (0, 0), (0, 0))).reshape(n, nb, BAND_BLOCK, h, dh)
    kb = band(k)
    vb = band(v)

    qi = jnp.arange(BAND_BLOCK)[:, None]
    kj = jnp.arange(2 * BAND_BLOCK)[None, :]
    back = qi - kj + BAND_BLOCK
    blk = jnp.arange(nb)[:, None, None]
    valid = (back >= 0) & (back <= steps) & (blk * BAND_BLOCK + kj >= BAND_BLOCK)
    bias = rel_bias[t5_bucket(jnp.maximum(back, 0) * dilation)].astype(jnp.float32).transpose(2, 0, 1)

    scores = jnp.einsum('nbqhd,nbkhd->nbhqk', qb, kb).astype(jnp.float32) * (dh ** -0.5) + bias
    scores = jnp.where(valid[None, :, None], scores, -jnp.inf)
    m = jnp.max(scores, axis=-1, keepdims=True)
    p = jnp.exp(scores - m)
    den = jnp.sum(p, axis=-1)
    out = jnp.einsum('nbhqk,nbkhd->nbqhd', p, vb.astype(jnp.float32)) / den.transpose(0, 1, 3, 2)[..., None]
    lse = (m[..., 0] + jnp.log(den)).transpose(0, 1, 3, 2)

    def from_classes(t):
        t = t.reshape((n, lp) + t.shape[3:])[:, :length]
        t = t.reshape((b, dilation, length) + t.shape[2:])
        return jnp.swapaxes(t, 1, 2).reshape((b, s) + t.shape[3:])

    return from_classes(out), from_classes(lse)

def dilated_attention(q, k, v, rel_bias):
    results = [dilated_branch(q, k, v, rel_bias, w, d) for (w, d) in DILATED_PATTERNS]
    outs = jnp.stack([r[0] for r in results])
    lses = jnp.stack([r[1] for r in results])
    weights = jax.nn.softmax(lses, axis=0)
    return jnp.einsum('pbsh,pbshd->bshd', weights, outs).astype(q.dtype)

def causal_block_attention(q, k, v, scale):
    b, s, h, dqk = q.shape
    nq = s // Q_BLOCK
    qb = q.reshape(b, nq, Q_BLOCK, h, dqk).transpose(1, 0, 2, 3, 4)
    kpos = jnp.arange(s)

    def one_block(args):
        i, qblk = args
        qpos = i * Q_BLOCK + jnp.arange(Q_BLOCK)
        sc = jnp.einsum('bqhd,bkhd->bhqk', qblk, k).astype(jnp.float32) * scale
        sc = jnp.where(kpos[None, :] <= qpos[:, None], sc, -jnp.inf)
        p = jax.nn.softmax(sc, axis=-1)
        return jnp.einsum('bhqk,bkhd->bqhd', p.astype(v.dtype), v)

    out = lax.map(one_block, (jnp.arange(nq, dtype=jnp.int32), qb))
    return out.transpose(1, 0, 2, 3, 4).reshape(b, s, h, v.shape[-1])

def routed_experts(h, router_w, router_b, w_gate_up, b_gate_up, w_down, b_down):
    t, d = h.shape
    logits = (h @ router_w).astype(jnp.float32) + router_b.astype(jnp.float32)
    top_val, top_idx = lax.top_k(logits, TOP_K)
    gates = jax.nn.softmax(top_val, axis=-1)

    n_assign = t * TOP_K
    flat_e = top_idx.reshape(-1)
    order = jnp.argsort(flat_e)
    sorted_e = flat_e[order]
    tok = (order // TOP_K).astype(jnp.int32)
    counts = jnp.bincount(flat_e, length=N_EXPERTS)
    padded = (counts + EXPERT_BLOCK - 1) // EXPERT_BLOCK * EXPERT_BLOCK
    pad_end = jnp.cumsum(padded)
    pad_start = pad_end - padded
    start = jnp.cumsum(counts) - counts
    dest = pad_start[sorted_e] + (jnp.arange(n_assign) - start[sorted_e])

    n_blocks = -(-n_assign // EXPERT_BLOCK) + N_EXPERTS
    n_slots = n_blocks * EXPERT_BLOCK
    slot_tok = jnp.zeros((n_slots,), jnp.int32).at[dest].set(tok)
    slot_gate = jnp.zeros((n_slots,), jnp.float32).at[dest].set(gates.reshape(-1)[order])
    block_expert = jnp.clip(jnp.searchsorted(pad_end, jnp.arange(n_blocks) * EXPERT_BLOCK, side='right'),
                            0, N_EXPERTS - 1).astype(jnp.int32)
    xs = h[slot_tok].reshape(n_blocks, EXPERT_BLOCK, d)

    def expert_block(args):
        xb, e = args
        gu = xb @ w_gate_up[e] + b_gate_up[e]
        gate = jnp.minimum(gu[:, :D_FF], SWIGLU_LIMIT)
        up = jnp.clip(gu[:, D_FF:], -SWIGLU_LIMIT, SWIGLU_LIMIT)
        glu = gate * jax.nn.sigmoid(SWIGLU_ALPHA * gate)
        return ((up + 1.0) * glu) @ w_down[e] + b_down[e]

    ys = lax.map(expert_block, (xs, block_expert)).reshape(n_slots, d)
    ys = ys * slot_gate[:, None].astype(ys.dtype)
    return jax.ops.segment_sum(ys, slot_tok, num_segments=t)

def setup_inputs(seed: int = 0) -> dict:
    key = jax.random.key(seed)
    ks = jax.random.split(key, 20)
    f32 = jnp.float32

    def nrm(k, shape, scale):
        return jax.random.normal(k, shape, f32) * scale

    def gain(k, shape):
        return 1.0 + 0.02 * jax.random.normal(k, shape, f32)

    L = DEPTH
    return {
        'x': nrm(ks[0], (BATCH, SEQ, D_MODEL), 1.0),
        'attn_norm_g': gain(ks[1], (L, D_MODEL)),
        'w_in': nrm(ks[2], (L, D_MODEL, IN_PROJ_WIDTH), D_MODEL ** -0.5),
        'a_q_norm_g': gain(ks[3], (L, A_HEAD_DIM)),
        'a_k_norm_g': gain(ks[4], (L, A_HEAD_DIM)),
        'rel_bias': nrm(ks[5], (NUM_BUCKETS, A_HEADS), 0.5),
        'q_a_norm_g': gain(ks[6], (L, Q_LORA_RANK)),
        'w_q_b': nrm(ks[7], (L, Q_LORA_RANK, B_HEADS * QK_HEAD_DIM), Q_LORA_RANK ** -0.5),
        'kv_a_norm_g': gain(ks[8], (L, KV_LORA_RANK)),
        'w_kv_b': nrm(ks[9], (L, KV_LORA_RANK, B_HEADS * (QK_NOPE_DIM + V_HEAD_DIM)), KV_LORA_RANK ** -0.5),
        'b_q_norm_g': gain(ks[10], (L, QK_HEAD_DIM)),
        'b_k_norm_g': gain(ks[11], (L, QK_HEAD_DIM)),
        'w_out': nrm(ks[12], (L, MIX_WIDTH, D_MODEL), MIX_WIDTH ** -0.5),
        'ffn_norm_g': gain(ks[13], (L, D_MODEL)),
        'router_w': nrm(ks[14], (L, D_MODEL, N_EXPERTS), D_MODEL ** -0.5),
        'router_b': nrm(ks[15], (L, N_EXPERTS), 0.01),
        'w_gate_up': nrm(ks[16], (L, N_EXPERTS, D_MODEL, 2 * D_FF), D_MODEL ** -0.5),
        'b_gate_up': nrm(ks[17], (L, N_EXPERTS, 2 * D_FF), 0.02),
        'w_down': nrm(ks[18], (L, N_EXPERTS, D_FF, D_MODEL), D_FF ** -0.5),
        'b_down': nrm(ks[19], (L, N_EXPERTS, D_MODEL), 0.02),
    }

def reference(x, attn_norm_g, w_in, a_q_norm_g, a_k_norm_g, rel_bias, q_a_norm_g, w_q_b,
              kv_a_norm_g, w_kv_b, b_q_norm_g, b_k_norm_g, w_out, ffn_norm_g, router_w,
              router_b, w_gate_up, b_gate_up, w_down, b_down):
    b, s, d = x.shape
    pos = jnp.arange(s, dtype=jnp.float32)
    inv_freq = ROPE_THETA ** (-jnp.arange(0, QK_ROPE_DIM, 2, dtype=jnp.float32) / QK_ROPE_DIM)
    ang = pos[:, None] * inv_freq[None, :]
    cos, sin = jnp.cos(ang), jnp.sin(ang)
    splits = [A_WIDTH, 2 * A_WIDTH, 3 * A_WIDTH, 3 * A_WIDTH + Q_LORA_RANK,
              3 * A_WIDTH + Q_LORA_RANK + KV_LORA_RANK]

    for layer in range(DEPTH):
        h = rms_norm(x, attn_norm_g[layer])
        proj = h @ w_in[layer]
        qa, ka, va, cq, ckv, kpe = jnp.split(proj, splits, axis=-1)

        qa = rms_norm(qa.reshape(b, s, A_HEADS, A_HEAD_DIM), a_q_norm_g[layer])
        ka = rms_norm(ka.reshape(b, s, A_HEADS, A_HEAD_DIM), a_k_norm_g[layer])
        va = va.reshape(b, s, A_HEADS, A_HEAD_DIM)
        out_a = dilated_attention(qa, ka, va, rel_bias).reshape(b, s, A_WIDTH)

        qb = (rms_norm(cq, q_a_norm_g[layer]) @ w_q_b[layer]).reshape(b, s, B_HEADS, QK_HEAD_DIM)
        kv = (rms_norm(ckv, kv_a_norm_g[layer]) @ w_kv_b[layer]).reshape(b, s, B_HEADS, QK_NOPE_DIM + V_HEAD_DIM)
        k_nope, vb = kv[..., :QK_NOPE_DIM], kv[..., QK_NOPE_DIM:]
        k_pe = jnp.broadcast_to(kpe[:, :, None, :], (b, s, B_HEADS, QK_ROPE_DIM))
        kb = jnp.concatenate([k_nope, k_pe], axis=-1)
        qb = rms_norm(qb, b_q_norm_g[layer])
        kb = rms_norm(kb, b_k_norm_g[layer])
        qb = jnp.concatenate([qb[..., :QK_NOPE_DIM], apply_rope(qb[..., QK_NOPE_DIM:], cos, sin)], axis=-1)
        kb = jnp.concatenate([kb[..., :QK_NOPE_DIM], apply_rope(kb[..., QK_NOPE_DIM:], cos, sin)], axis=-1)
        out_b = causal_block_attention(qb, kb, vb, QK_HEAD_DIM ** -0.5).reshape(b, s, B_WIDTH)

        x = x + jnp.concatenate([out_a, out_b], axis=-1) @ w_out[layer]

        h2 = rms_norm(x, ffn_norm_g[layer]).reshape(b * s, d)
        y = routed_experts(h2, router_w[layer], router_b[layer], w_gate_up[layer], b_gate_up[layer],
                           w_down[layer], b_down[layer])
        x = x + y.reshape(b, s, d)
    return x


_drawn_inputs = setup_inputs


def setup_inputs(seed=0):
    import zlib

    import numpy as np

    out = dict(_drawn_inputs(seed))
    spreads = {}
    factors = {'attn_norm_g': 3.108,
     'a_q_norm_g': 2.935,
     'a_k_norm_g': 6.662,
     'q_a_norm_g': 4.427,
     'b_q_norm_g': 3.984,
     'b_k_norm_g': 4.424,
     'b_gate_up': 5.194,
     'b_down': 21.341,
     'kv_a_norm_g': 3.209,
     'ffn_norm_g': 2.863,
     'router_b': 10.185}
    for name, (base, spread) in spreads.items():
        noise = np.random.default_rng([zlib.crc32(name.encode()), seed]).standard_normal(out[name].shape)
        drawn = base * np.exp(spread * noise) if base else spread * noise
        out[name] = jnp.asarray(drawn.astype(out[name].dtype))
    for name, factor in factors.items():
        out[name] = (out[name] * factor).astype(out[name].dtype)
    return out
```

```python
from contextlib import ExitStack

import numpy as np

import concourse.bass as bass
from concourse import mybir

F32 = mybir.dt.float32
I32 = mybir.dt.int32
ALU = mybir.AluOpType
ACT = mybir.ActivationFunctionType
AX = mybir.AxisListType.X

P = 128
SEQ, D = 256, 1024
TT = SEQ // P
KD = D // P
HALF = 512
A_HEADS, A_DIM, A_WIDTH = 8, 64, 512
B_HEADS, NOPE, ROPE, V_DIM = 4, 128, 64, 128
QK_DIM = NOPE + ROPE
LORA = 256
C_COL = 3 * A_WIDTH
KPE_COL = C_COL + 2 * LORA
IN_W = KPE_COL + ROPE
EXPERTS, TOP_K, FF = 32, 4, 1024
LIMIT, ALPHA = 7.0, 1.702
EPS = 1e-6
BUCKETS, MAX_DIST = 32, 2048
NEG = -1e30
LOW = -3e38
SLOT = 64
MAX_MORE = 16
MORE = MAX_MORE + 2
SLOTS = EXPERTS + MORE
GAIN_DMAS = 13
NCHUNK, DCHUNK = 4, 2


def constants():
    eye = np.eye(P, dtype=np.float32)
    iota = np.tile(np.arange(64, dtype=np.float32), (P, 1))
    before = np.triu(np.ones((P, P), np.float32), 1)
    ones = np.ones((P, P), np.float32)
    q, k = np.arange(P)[:, None], np.arange(P)[None, :]
    causal = np.concatenate([np.zeros((P, P)), np.where(k <= q, 0.0, NEG)], 1).astype(np.float32)
    inv = (np.float32(10000.0) ** (-np.arange(0, ROPE, 2, dtype=np.float32) / np.float32(ROPE))).astype(np.float32)
    ang = np.arange(SEQ, dtype=np.float32)[:, None] * inv[None, :]
    cos, sin = np.cos(ang).astype(np.float32), np.sin(ang).astype(np.float32)
    cc = np.concatenate([cos, cos], 1).reshape(TT, P, ROPE).transpose(1, 0, 2).reshape(P, TT * ROPE)
    ss = np.concatenate([-sin, sin], 1).reshape(TT, P, ROPE).transpose(1, 0, 2).reshape(P, TT * ROPE)
    row = np.arange(P, dtype=np.float32)[:, None]
    slot_expert = np.tile(np.arange(EXPERTS, dtype=np.float32), (P, 1))
    c_all = np.concatenate([eye, eye[:, ::-1], iota, before, ones, causal, cc, ss, row, slot_expert], 1)
    d = 255 - np.arange(384)
    df = np.maximum(d, 1).astype(np.float32)
    half = BUCKETS // 2
    log_b = half + (np.log(df / half) / np.float32(np.log(MAX_DIST / half)) * half).astype(np.int32)
    bucket = np.where(d < half, np.maximum(d, 0), np.minimum(log_b, BUCKETS - 1))
    count = sum(((d >= 0) & (d <= w) & (d % r == 0)).astype(np.float32) for w, r in ((128, 1), (512, 4), (2048, 16)))
    onehot = (bucket[None, :] == np.arange(BUCKETS)[:, None]).astype(np.float32)
    lnc = np.where(count > 0, np.log(np.maximum(count, 1)), NEG).astype(np.float32)
    c_rel = np.concatenate([onehot, np.tile(lnc, (BUCKETS, 1))], 1)
    return np.ascontiguousarray(c_all, np.float32), np.ascontiguousarray(c_rel, np.float32)


C_ALL_W = 2 * P + 64 + P + P + 2 * P + TT * ROPE * 2 + 1 + EXPERTS


class Steps:

    def __init__(self, sem, names):
        self.sem, self.names, self.next = sem, list(names), 0
        assert len(set(self.names)) == len(self.names)

    def at(self, name):
        return self.names.index(name) + 1

    def done(self, name, instruction):
        assert self.names[self.next] == name, (self.names[self.next], name)
        self.next += 1
        instruction.then_inc(self.sem, 1)


def layer_kernel(nc, x, attn_norm_g, w_in, a_q_norm_g, a_k_norm_g, rel_bias, q_a_norm_g, w_q_b, kv_a_norm_g,
                 w_kv_b, b_q_norm_g, b_k_norm_g, w_out, ffn_norm_g, router_w, router_b, w_gate_up, b_gate_up,
                 w_down, b_down, c_all, c_rel, out):
    with ExitStack() as ctx:
        def sb(name, shape, dt=F32):
            return ctx.enter_context(nc.sbuf_tensor(name, shape, dt))

        def sem(name):
            return ctx.enter_context(nc.semaphore(name))

        ring = sb("ring", [P, 2 * KD * 2 * FF])
        dring = sb("dring", [P, KD * D])
        GU = [ring[:, b * KD * 2 * FF:(b + 1) * KD * 2 * FF].rearrange("p (k n) -> p k n", k=KD) for b in range(2)]
        DN = dring[:, :].rearrange("p (k n) -> p k n", k=KD)
        xs = sb("xs", [P, TT, D])
        hn = sb("hn", [P, TT, D])
        mt = sb("mt", [P, 7040])
        ca = sb("ca", [P, C_ALL_W])
        st = sb("st", [P, 256])
        rt = sb("rt", [P, 320])
        gains = sb("gains", [P, 24])
        gr = sb("gr", [24, P])
        gq_rope = sb("gq_rope", [P, ROPE])
        gk_rope = sb("gk_rope", [P, ROPE])
        router_bias = sb("router_bias", [P, EXPERTS])
        sqw = sb("sqw", [P, 1280])
        k_rot = sb("k_rot", [P, TT, ROPE])
        rs0 = sb("rs0", [P, B_HEADS, ROPE])
        rs1 = sb("rs1", [P, B_HEADS, ROPE])
        w_kpe = sb("w_kpe", [P, KD, ROPE])
        w_router = sb("w_router", [P, KD, EXPERTS])
        minus_half = sb("minus_half", [P, 1])
        slot_e = sb("slot_e", [1, SLOTS], I32)
        turns = sb("turns", [1, 1], I32)
        dram_bias = nc.dram_tensor("dram_bias", (A_HEADS, 384), F32)

        def cut(t, at, n):
            return t[:, at:at + n]

        c0 = 0
        ident = cut(ca, c0, P); c0 += P
        flip = cut(ca, c0, P); c0 += P
        iota = cut(ca, c0, 64); c0 += 64
        before = cut(ca, c0, P); c0 += P
        ones = cut(ca, c0, P); c0 += P
        causal = cut(ca, c0, 2 * P); c0 += 2 * P
        cos2 = cut(ca, c0, TT * ROPE).rearrange("p (t r) -> p t r", t=TT); c0 += TT * ROPE
        sin2 = cut(ca, c0, TT * ROPE).rearrange("p (t r) -> p t r", t=TT); c0 += TT * ROPE
        row_id = cut(ca, c0, 1); c0 += 1
        expert_id = cut(ca, c0, EXPERTS); c0 += EXPERTS
        assert c0 == C_ALL_W

        w_in_sb, w_out_sb = GU[0], DN
        T = ring[:, KD * 2 * FF:]
        t0 = 0

        def tcut(n):
            nonlocal t0
            t0 += n
            return T[:, t0 - n:t0]

        pr = tcut(TT * IN_W).rearrange("p (t n) -> p t n", t=TT)
        qb = tcut(TT * B_HEADS * QK_DIM).rearrange("p (t h n) -> p t h n", t=TT, h=B_HEADS)
        kvb = tcut(TT * B_HEADS * 256).rearrange("p (t h n) -> p t h n", t=TT, h=B_HEADS)
        qTa_at = t0
        qTa = tcut(4 * SEQ).rearrange("p (h t) -> p h t", h=4)
        kTa = tcut(4 * SEQ).rearrange("p (h t) -> p h t", h=4)
        hankel = T[:, t0:t0 + 8 * SEQ]
        qTn = tcut(4 * SEQ).rearrange("p (h t) -> p h t", h=4)
        kTn = tcut(4 * SEQ).rearrange("p (h t) -> p h t", h=4)
        qTr = tcut(4 * SEQ)[0:ROPE].rearrange("p (h t) -> p h t", h=4)
        kTr = tcut(4 * SEQ)[0:ROPE].rearrange("p (h t) -> p h t", h=4)
        bias_a = tcut(A_HEADS * SEQ).rearrange("p (h t) -> p h t", h=A_HEADS)
        assert t0 <= KD * 2 * FF
        rel_tab = T[0:BUCKETS, qTa_at:qTa_at + 768]
        rel_rev = T[0:A_HEADS, qTa_at + 768:qTa_at + 1152]
        rel_sb = T[0:BUCKETS, qTa_at + 1152:qTa_at + 1160]
        xT = mt[:, 0:2048].rearrange("p (k t) -> p k t", k=KD)
        wqb = mt[:, 2048:3584].rearrange("p (k n) -> p k n", k=2)
        wkvb = mt[:, 3584:5632].rearrange("p (k n) -> p k n", k=2)
        cT = mt[:, 5632:6656].rearrange("p (k t) -> p k t", k=4)
        prob = [mt[:, 0:1536].rearrange("p (h k) -> p h k", h=12), mt[:, 1536:4608].rearrange("p (h k) -> p h k", h=12)]
        mixed = mt[:, 4608:6656].rearrange("p (t n) -> p t n", t=TT)
        mixT = mt[:, 0:2048].rearrange("p (k t) -> p k t", k=KD)
        h2T = mt[:, 2048:4096].rearrange("p (k t) -> p k t", k=KD)
        sq = hn[:, :, :].rearrange("p t n -> p (t n)")
        probT0 = hn[:, :, :].rearrange("p t n -> p (t n)")
        probT1 = [pr[:, 0, 0:512], pr[:, 0, 512:1024], pr[:, 1, 0:512], pr[:, 1, 512:1024],
                  sq[:, 1536:2048], qb[:, 0].rearrange("p h n -> p (h n)")[:, 0:512]]
        s0 = 0

        def scut(n):
            nonlocal s0
            s0 += n
            return st[:, s0 - n:s0]

        r_x, r_2 = scut(TT), scut(TT)
        r_a = scut(TT * 16).rearrange("p (t n) -> p t n", t=TT)
        r_c = scut(TT * 2).rearrange("p (t n) -> p t n", t=TT)
        r_q = scut(TT * 4).rearrange("p (t n) -> p t n", t=TT)
        s_kpe = scut(TT)
        r_k = scut(TT * 4).rearrange("p (t n) -> p t n", t=TT)
        n_max = scut(TT * 12).rearrange("p (t n) -> p t n", t=TT)
        den = scut(TT * 12).rearrange("p (t n) -> p t n", t=TT)
        g_den = scut(TT)
        n_m1 = scut(TT)
        gain_a, gain_b = scut(1), scut(1)
        cnt, extra, cum = scut(1), scut(1), scut(1)
        assert s0 <= 256
        r0 = 0

        def rcut(n):
            nonlocal r0
            r0 += n
            return rt[:, r0 - n:r0]

        pos = rcut(TT * EXPERTS).rearrange("p (t e) -> p t e", t=TT)
        gate = rcut(TT * EXPERTS).rearrange("p (t e) -> p t e", t=TT)
        slot_first = rcut(SLOTS)
        rel_pos = [rcut(TT) for _ in range(2)]
        slot_gate = [rcut(TT) for _ in range(2)]
        R = mt[:, 0:1024]
        lg = R[:, 0:80].rearrange("p (t e) -> p t e", t=TT)
        rep = R[:, 80:160].rearrange("p (t e) -> p t e", t=TT)
        m8 = R[:, 160:176].rearrange("p (t e) -> p t e", t=TT)
        top4 = R[:, 176:192].rearrange("p (t e) -> p t e", t=TT)
        mask = R[:, 192:256].rearrange("p (t e) -> p t e", t=TT)
        ex = R[:, 256:320].rearrange("p (t e) -> p t e", t=TT)
        table_in = R[0:EXPERTS, 320:320 + 3 * MORE]
        tdist = R[0:EXPERTS, 400:400 + MORE]
        tlow = R[0:EXPERTS, 440:440 + MORE]
        table = R[:, 480:480 + 3 * MORE]
        pairs = R[:, 560:561]
        gateT = R[0:EXPERTS, 576:576 + SEQ]
        xeT = [mt[:, 0:512], mt[:, 512:1024]]
        g_sb, u_sb, h_sb = mt[:, 1024:1536], mt[:, 1536:2048], mt[:, 2048:2560]
        hT = mt[:, 2560:3072]
        y_sb = mt[:, 3072:4096].rearrange("p (h n) -> p h n", h=2)
        GT = mt[:, 4608:4864]
        sel = [mt[:, 4096 + 128 * b:4224 + 128 * b].rearrange("p (t j) -> p t j", t=TT) for b in range(2)]
        selG = mt[:, 4352:4608].rearrange("p (t b j) -> p t b j", t=TT, b=2)
        onehot = [mt[:, 4864 + 64 * b:4928 + 64 * b] for b in range(2)]
        b_gu = mt[:, 4992:7040]
        b_dn = mt[0:EXPERTS, 1024:2048]
        y_out = hn

        bank = [ctx.enter_context(nc.psum_tensor(f"bank{i}", [P, HALF], F32)) for i in range(8)]
        y_acc = [[bank[0], bank[1]], [bank[2], bank[3]]]
        ps_gate, ps_up, ps_a, ps_b = bank[4], bank[5], bank[6], bank[7]

        jobs = [("gains", "dve", "gains"), ("rel", "dve", "rel")]
        jobs += [(f"xT{t}{g}", "dve", f"xT{t}{g}") for t in range(2) for g in range(2)]
        jobs += [(f"{n}{t}", "act", f"{n}{t}") for t in range(2) for n in ("pC", "pE")]
        jobs += [("pK0", "act", "pK0"), ("cT0", "dve", "cT0"), ("cT1", "dve", "cT1"), ("pK1", "act", "pK1")]
        jobs += [(f"band{g}", "act", f"band{g}") for g in range(4)]
        jobs += [(f"{n}0", "act", f"{n}0") for n in ("qba", "qbb", "kva", "kvb", "pQ")]
        jobs += [(f"{n}1", "act", f"{n}1") for n in ("qba", "qbb", "kva", "kvb", "pQ")]
        jobs += [("pV0", "act", "pV0"), ("pV1", "act", "pV1")]
        for t in range(2):
            jobs += [(f"tnq{t}", "dve", f"tnq{t}"), (f"tnk{t}", "act", f"tnk{t}"),
                     (f"trq{t}", "act", f"trq{t}"), (f"trk{t}", "act", f"trk{t}"),
                     (f"taq{t}", "dve", f"taq{t}"), (f"tak{t}", "act", f"tak{t}")]
        heads_of = {"s0e": (0, [0, 2, 4, 6]), "s0o": (0, [1, 3, 5, 7]), "s0b": (0, [8, 9, 10, 11]),
                    "s1a": (1, [0, 2]), "s1b": (1, [1, 3]), "s1c": (1, [4, 6]), "s1d": (1, [5, 7]),
                    "s1e": (1, [8, 9]), "s1f": (1, [10, 11])}
        jobs += [(n, "dve", f"{n}{hs[-1]}") for n, (_, hs) in heads_of.items()]
        jobs += [(f"P0{g}", "dve", f"P0{g}") for g in range(3)]
        jobs += [("vA0", "dve", "vA0"), ("vB0", "dve", "vB0")]
        jobs += [(f"P1{g}", "dve" if g % 2 else "act", f"P1{g}") for g in range(6)]
        jobs += [("vA1", "dve", "vA1"), ("vB1", "dve", "vB1")]
        jobs += [(f"mT{t}{g}", "act", f"mT{t}{g}") for t in range(2) for g in range(2)]
        jobs += [(f"oP{t}{g}", "dve", f"oP{t}{g}") for t in range(2) for g in range(2)]
        jobs += [(f"hT{t}{g}", "dve", f"hT{t}{g}") for t in range(2) for g in range(2)]
        jobs += [("lg0", "dve", "lg0"), ("lg1", "dve", "lg1")]
        jobs += [("rank0", "dve", "pos0"), ("rank1", "dve", "pos1"), ("cnt", "dve", "cnt"), ("cum", "dve", "cum"),
                 ("table", "dve", "table"), ("gateT", "act", "gateT")]
        job_at = {n: i for i, (n, _, _) in enumerate(jobs)}

        pe_steps, dve_steps, act_steps, pool_steps = sem("pe_steps"), sem("dve_steps"), sem("act_steps"), sem("pool_steps")
        PE = Steps(pe_steps, [n for n, _, _ in jobs] + ["y_start"])
        ACTS = Steps(act_steps,
                     ["sqx0", "sqx1"]
                     + [f"{n}{t}" for t in range(2) for n in ("pC", "pE", "sqc", "sqc_b", "sqe")]
                     + ["pK0", "pK1"] + [f"band{g}" for g in range(4)]
                     + [f"{n}{t}" for t in range(2) for n in ("qba", "qbb", "kva", "kvb", "sqq", "sqk", "pQ", "sqa")]
                     + ["pV0", "pV1"]
                     + [f"{n}{t}" for t in range(2) for n in ("tnk", "trq", "trk", "tak")]
                     + [f"e{t}{h}" for t in range(2) for h in range(12)]
                     + [f"P1{g}" for g in range(0, 6, 2)]
                     + [f"mT{t}{g}" for t in range(2) for g in range(2)]
                     + ["sq2_0", "sq2_1", "exp0", "exp1", "gateT"])
        DVE = Steps(dve_steps,
                    ["rx0", "rx1", "gains", "ga", "gb", "rel"]
                    + [f"xT{t}{g}" for t in range(2) for g in range(2)]
                    + ["rc0", "rc1"]
                    + ["cT0", "cT1"]
                    + [f"{n}{t}" for t in range(2) for n in ("sumq", "rq", "sumk", "addk", "rk", "sumA", "rAq", "rAk", "nscale", "kpe", "kscale")]
                    + [f"{n}{t}" for t in range(2) for n in ("tnq", "taq")]
                    + [x for n, (t, hs) in heads_of.items() if t == 0 for x in [f"{n}{h}" for h in hs]] + ["max0"]
                    + [x for n, (t, hs) in heads_of.items() if t == 1 for x in [f"{n}{h}" for h in hs]] + ["max1"]
                    + ["rden0", "P00", "P01", "P02", "vA0", "vB0", "rden1", "P11", "P13", "P15", "vA1", "vB1"]
                    + ["oP00", "oP01", "r20", "hn0", "oP10", "oP11", "r21", "hn1"]
                    + [f"hT{t}{g}" for t in range(2) for g in range(2)]
                    + ["low", "low4", "first0"]
                    + [f"{n}{t}" for t in range(2) for n in ("lg", "max8_", "top", "nm1_", "rep", "mask")]
                    + ["cnt", "x1", "x2", "x3", "cum", "td", "tge", "tlt", "tA", "tR", "tE", "table", "first_m", "first", "slots_e", "main_e", "pairsum", "turns"]
                    + [f"{n}{t}" for t in range(2) for n in ("gm", "gden", "grd", "gate")]
                    + ["posr0", "pos0", "posr1", "pos1"])
        POOL = Steps(pool_steps,
                     ["half", "px0", "px1", "pc0", "pc1"]
                     + [f"{n}{t}" for t in range(2) for n in ("gk", "kc", "ks1", "ks2", "kadd")]
                     + [f"{n}{t}" for t in range(2) for n in ("gq", "qc", "qs1", "qs2", "qadd", "pq", "pk", "pa")]
                     + ["p20", "p21", "zero_G", "zero_b"])

        ld = {n: sem("ld_" + n) for n in ("x0", "x1", "gains", "const", "wC", "wK", "wQ", "wV", "lora", "rel", "small", "wout",
                                          "bias_a", "b_gu", "b_dn")}
        st_bias = sem("st_bias")
        st_out = sem("st_out")
        gu_loaded = [[sem(f"gu_loaded{b}{c}") for c in range(NCHUNK)] for b in range(2)]
        dn_loaded = [sem(f"dn_loaded{c}") for c in range(DCHUNK)]
        gu_used, dn_used = sem("gu_used"), sem("dn_used")
        select_steps, sel_ready = sem("select_steps"), sem("sel_ready")
        xet_done, xet_ready = sem("xet_done"), sem("xet_ready")
        gt_done, gt_ready = sem("gt_done"), sem("gt_ready")
        gate_ready, up_ready, upgate_ready = sem("gate_ready"), sem("up_ready"), sem("upgate_ready")
        sig_ready, h_ready = sem("sig_ready"), sem("h_ready")
        t_done, hT_ready = sem("t_done"), sem("hT_ready")
        y_ready, y_final, out_ready = sem("y_ready"), sem("y_final"), sem("out_ready")
        SEL_OPS = 3

        def fill(t, c):
            return t[:, c * (KD // NCHUNK):(c + 1) * (KD // NCHUNK), :]

        def gu_dram(e, c):
            rows = D // NCHUNK
            w = w_gate_up[e] if isinstance(e, int) else w_gate_up[bass.ds(e, 1)].rearrange("a d f -> (a d) f")
            return w[c * rows:(c + 1) * rows, :].rearrange("(k p) f -> p k f", p=P)

        def dn_dram(e, c):
            rows = FF // DCHUNK
            w = w_down[e] if isinstance(e, int) else w_down[bass.ds(e, 1)].rearrange("a d f -> (a d) f")
            return w[c * rows:(c + 1) * rows, :].rearrange("(k p) f -> p k f", p=P)

        def dn_fill(c):
            return DN[:, c * (KD // DCHUNK):(c + 1) * (KD // DCHUNK), :]

        block = ctx.enter_context(nc.Block())

        @block.sync
        def _(sp):
            w_rows = w_in[0].rearrange("(k p) n -> p k n", p=P)
            sp.dma_start(xs[:, 0, :], x[0, 0:P, :]).then_inc(ld["x0"], 16)
            sp.dma_start(ca[:, :], c_all[:, :]).then_inc(ld["const"], 16)
            sp.dma_start(xs[:, 1, :], x[0, P:SEQ, :]).then_inc(ld["x1"], 16)
            sp.dma_start(w_in_sb[:, :, C_COL:C_COL + 512], w_rows[:, :, C_COL:C_COL + 512]).then_inc(ld["wC"], 16)
            sp.dma_start(w_kpe[:, :, :], w_rows[:, :, KPE_COL:KPE_COL + ROPE]).then_inc(ld["wC"], 16)
            sp.dma_start(w_in_sb[:, :, 512:1024], w_rows[:, :, 512:1024]).then_inc(ld["wK"], 16)
            sp.dma_start(wqb, w_q_b[0].rearrange("(k p) n -> p k n", p=P)).then_inc(ld["lora"], 16)
            sp.dma_start(wkvb, w_kv_b[0].rearrange("(k p) n -> p k n", p=P)).then_inc(ld["lora"], 16)
            sp.dma_start(w_in_sb[:, :, 0:512], w_rows[:, :, 0:512]).then_inc(ld["wQ"], 16)
            sp.dma_start(w_in_sb[:, :, 1024:1536], w_rows[:, :, 1024:1536]).then_inc(ld["wV"], 16)
            sp.dma_start(w_out_sb[:, :, :], w_out[0].rearrange("(k p) n -> p k n", p=P)).then_inc(ld["wout"], 16)
            sp.wait_ge(pe_steps, PE.at("pV1"))
            for c in range(NCHUNK):
                sp.dma_start(fill(GU[0], c), gu_dram(0, c)).then_inc(gu_loaded[0][c], 16)
            sp.wait_ge(pe_steps, PE.at("oP11"))
            for c in range(DCHUNK):
                sp.dma_start(dn_fill(c), dn_dram(0, c)).then_inc(dn_loaded[c], 16)
            for c in range(NCHUNK):
                sp.dma_start(fill(GU[1], c), gu_dram(1, c)).then_inc(gu_loaded[1][c], 16)
            for c in range(DCHUNK):
                sp.wait_ge(dn_used, c + 1)
                sp.dma_start(dn_fill(c), dn_dram(1, c)).then_inc(dn_loaded[c], 16)
            sp.wait_ge(dve_steps, DVE.at("turns"))
            n_turns = sp.value_load(turns[0:1, 0:1], min_val=EXPERTS // 2, max_val=(EXPERTS + MAX_MORE) // 2)
            with sp.Fori(0, n_turns - 1) as i:
                for b in range(2):
                    e = sp.value_load(slot_e[0:1, bass.ds(i * 2 + (b + 2), 1)], min_val=0, max_val=EXPERTS - 1)
                    for c in range(NCHUNK):
                        sp.wait_ge(gu_used, i * (2 * NCHUNK) + (b * NCHUNK + c + 1))
                        sp.dma_start(fill(GU[b], c), gu_dram(e, c)).then_inc(gu_loaded[b][c], 16)
                    for c in range(DCHUNK):
                        sp.wait_ge(dn_used, i * (2 * DCHUNK) + ((b + 1) * DCHUNK + c + 1))
                        sp.dma_start(dn_fill(c), dn_dram(e, c)).then_inc(dn_loaded[c], 16)
            for t in range(TT):
                sp.wait_ge(out_ready, 2 * t + 2)
                sp.dma_start(out[0, t * P:(t + 1) * P, :], y_out[:, t, :]).then_inc(st_out, 16)
            sp.wait_ge(st_out, 32)

        @block.tensor
        def _(pe):
            def begin(name):
                n = job_at[name]
                if n >= 8:
                    _, engine, step = jobs[n - 8]
                    if engine == "dve":
                        pe.wait_ge(dve_steps, DVE.at(step))
                    else:
                        pe.wait_ge(act_steps, ACTS.at(step))
                return bank[n % 8]

            pe.wait_ge(ld["gains"], 16 * GAIN_DMAS)
            pe.wait_ge(ld["const"], 16)
            b = begin("gains")
            PE.done("gains", nc.tensor.transpose(b[:, 0:24], gr[:, :], ident[0:24, 0:24]))
            b = begin("rel")
            pe.wait_ge(ld["rel"], 32)
            PE.done("rel", nc.tensor.matmul(b[0:A_HEADS, 0:384], rel_sb, rel_tab[:, 0:384], start=True, stop=True))
            for t in range(TT):
                pe.wait_ge(ld[f"x{t}"], 16)
                for g in range(2):
                    b = begin(f"xT{t}{g}")
                    for j in range(4):
                        last = nc.tensor.transpose(b[:, j * P:(j + 1) * P], xs[:, t, (4 * g + j) * P:(4 * g + j + 1) * P], ident)
                    PE.done(f"xT{t}{g}", last)

            def project(name, t, w, n):
                b = begin(name)
                pe.wait_ge(dve_steps, DVE.at(f"xT{t}1"))
                for k in range(KD):
                    last = nc.tensor.matmul(b[:, 0:n], xT[:, k, t * P:(t + 1) * P], w[:, k, :], start=k == 0, stop=k == KD - 1)
                PE.done(name, last)

            def latent(t):
                pe.wait_ge(dve_steps, DVE.at(f"cT{t}"))
                for name, k0, w, n0, n in (("qba", 0, wqb, 0, 384), ("qbb", 0, wqb, 384, 384), ("kva", 2, wkvb, 0, 512), ("kvb", 2, wkvb, 512, 512)):
                    b = begin(f"{name}{t}")
                    for k in range(2):
                        last = nc.tensor.matmul(b[:, 0:n], cT[:, k0 + k, t * P:(t + 1) * P], w[:, k, n0:n0 + n], start=k == 0, stop=k == 1)
                    PE.done(f"{name}{t}", last)

            pe.wait_ge(ld["wC"], 32)
            for t in range(TT):
                project(f"pC{t}", t, w_in_sb[:, :, C_COL:C_COL + 512], 512)
                project(f"pE{t}", t, w_kpe, ROPE)
            pe.wait_ge(ld["wK"], 16)
            project("pK0", 0, w_in_sb[:, :, 512:1024], 512)
            for t in range(TT):
                b = begin(f"cT{t}")
                pe.wait_ge(act_steps, ACTS.at(f"pC{t}"))
                for j in range(4):
                    last = nc.tensor.transpose(b[:, j * P:(j + 1) * P], pr[:, t, C_COL + j * P:C_COL + (j + 1) * P], ident)
                PE.done(f"cT{t}", last)
            project("pK1", 1, w_in_sb[:, :, 512:1024], 512)
            pe.wait_ge(ld["bias_a"], 16)
            for g in range(4):
                b = begin(f"band{g}")
                PE.done(f"band{g}", nc.tensor.matmul(b[:, :], flip, hankel[:, g * 512:(g + 1) * 512], start=True, stop=True))
            pe.wait_ge(ld["lora"], 32)
            latent(0)
            pe.wait_ge(ld["wQ"], 16)
            project("pQ0", 0, w_in_sb[:, :, 0:512], 512)
            latent(1)
            project("pQ1", 1, w_in_sb[:, :, 0:512], 512)
            pe.wait_ge(ld["wV"], 16)
            project("pV0", 0, w_in_sb[:, :, 1024:1536], 512)
            project("pV1", 1, w_in_sb[:, :, 1024:1536], 512)

            def turn(name, blocks, rows=P):
                b = begin(name)
                for j, src in enumerate(blocks):
                    last = nc.tensor.transpose(b[0:rows, j * P:(j + 1) * P], src, ident)
                PE.done(name, last)

            for t in range(TT):
                pe.wait_ge(act_steps, ACTS.at(f"qbb{t}"))
                turn(f"tnq{t}", [qb[:, t, h, 0:NOPE] for h in range(B_HEADS)])
                pe.wait_ge(dve_steps, DVE.at(f"nscale{t}"))
                turn(f"tnk{t}", [kvb[:, t, h, 0:NOPE] for h in range(B_HEADS)])
                pe.wait_ge(pool_steps, POOL.at(f"qadd{t}"))
                turn(f"trq{t}", [sq[:, 1024 + t * 512:1024 + t * 512 + 256].rearrange("p (h r) -> p h r", h=4)[:, h, :] for h in range(4)], ROPE)
                pe.wait_ge(dve_steps, DVE.at(f"kscale{t}"))
                turn(f"trk{t}", [sq[:, 1280 + t * 512:1536 + t * 512].rearrange("p (h r) -> p h r", h=4)[:, h, :] for h in range(4)], ROPE)
                turn(f"taq{t}", [pr[:, t, j * P:(j + 1) * P] for j in range(4)])
                turn(f"tak{t}", [pr[:, t, 512 + j * P:512 + (j + 1) * P] for j in range(4)])

            for name, (t, heads) in heads_of.items():
                b = begin(name)
                nk = (t + 1) * P
                pe.wait_ge(act_steps, ACTS.at(f"tak{t}"))
                pe.wait_ge(dve_steps, DVE.at(f"taq{t}"))
                for j, h in enumerate(heads):
                    o = b[:, j * nk:(j + 1) * nk]
                    if h < A_HEADS:
                        r = slice(64 * (h % 2), 64 * (h % 2) + 64)
                        last = nc.tensor.matmul(o, qTa[r, h // 2, t * P:(t + 1) * P], kTa[r, h // 2, 0:nk], start=True, stop=True)
                    else:
                        g = h - A_HEADS
                        nc.tensor.matmul(o, qTn[:, g, t * P:(t + 1) * P], kTn[:, g, 0:nk], start=True, stop=False)
                        last = nc.tensor.matmul(o, qTr[:, g, t * P:(t + 1) * P], kTr[:, g, 0:nk], start=False, stop=True)
                PE.done(name, last)

            def value(h, key_tile):
                if h < A_HEADS:
                    return pr[:, key_tile, 1024 + h * A_DIM:1024 + (h + 1) * A_DIM]
                return kvb[:, key_tile, h - A_HEADS, NOPE:NOPE + V_DIM]

            for g in range(3):
                pe.wait_ge(act_steps, ACTS.at(f"e0{4 * g + 3}"))
                turn(f"P0{g}", [prob[0][:, 4 * g + j, :] for j in range(4)])
            for name, heads, w in (("vA0", range(8), A_DIM), ("vB0", range(8, 12), V_DIM)):
                b = begin(name)
                for j, h in enumerate(heads):
                    pe.wait_ge(dve_steps, DVE.at(f"P0{h // 4}"))
                    last = nc.tensor.matmul(b[:, j * w:(j + 1) * w], probT0[:, (h // 4) * 512 + (h % 4) * P:(h // 4) * 512 + (h % 4 + 1) * P],
                                            value(h, 0), start=True, stop=True)
                PE.done(name, last)
            for g in range(6):
                pe.wait_ge(act_steps, ACTS.at(f"e1{2 * g + 1}"))
                turn(f"P1{g}", [prob[1][:, 2 * g + j // 2, (j % 2) * P:(j % 2 + 1) * P] for j in range(4)])
            for name, heads, w in (("vA1", range(8), A_DIM), ("vB1", range(8, 12), V_DIM)):
                b = begin(name)
                for j, h in enumerate(heads):
                    g = h // 2
                    if g % 2:
                        pe.wait_ge(dve_steps, DVE.at(f"P1{g}"))
                    else:
                        pe.wait_ge(act_steps, ACTS.at(f"P1{g}"))
                    for kt in range(2):
                        o = (h % 2) * 256 + kt * P
                        last = nc.tensor.matmul(b[:, j * w:(j + 1) * w], probT1[g][:, o:o + P], value(h, kt), start=kt == 0, stop=kt == 1)
                PE.done(name, last)
            for t in range(TT):
                pe.wait_ge(dve_steps, DVE.at(f"vB{t}"))
                for g in range(2):
                    turn(f"mT{t}{g}", [mixed[:, t, (4 * g + j) * P:(4 * g + j + 1) * P] for j in range(4)])
            pe.wait_ge(ld["wout"], 16)
            for t in range(TT):
                pe.wait_ge(act_steps, ACTS.at(f"mT{t}1"))
                for g in range(2):
                    b = begin(f"oP{t}{g}")
                    for k in range(KD):
                        last = nc.tensor.matmul(b[:, :], mixT[:, k, t * P:(t + 1) * P], w_out_sb[:, k, g * HALF:(g + 1) * HALF],
                                                start=k == 0, stop=k == KD - 1)
                    PE.done(f"oP{t}{g}", last)
            for t in range(TT):
                pe.wait_ge(dve_steps, DVE.at(f"hn{t}"))
                for g in range(2):
                    turn(f"hT{t}{g}", [hn[:, t, (4 * g + j) * P:(4 * g + j + 1) * P] for j in range(4)])
            pe.wait_ge(ld["small"], 16)
            for t in range(TT):
                b = begin(f"lg{t}")
                pe.wait_ge(dve_steps, DVE.at(f"hT{t}1"))
                for k in range(KD):
                    last = nc.tensor.matmul(b[:, 0:EXPERTS], h2T[:, k, t * P:(t + 1) * P], w_router[:, k, :], start=k == 0, stop=k == KD - 1)
                PE.done(f"lg{t}", last)
            pe.wait_ge(dve_steps, DVE.at("mask0"))
            b = begin("rank0")
            PE.done("rank0", nc.tensor.matmul(b[:, 0:EXPERTS], before, mask[:, 0, :], start=True, stop=True))
            b = begin("rank1")
            pe.wait_ge(dve_steps, DVE.at("mask1"))
            nc.tensor.matmul(b[:, 0:EXPERTS], ones, mask[:, 0, :], start=True, stop=False)
            PE.done("rank1", nc.tensor.matmul(b[:, 0:EXPERTS], before, mask[:, 1, :], start=False, stop=True))
            b = begin("cnt")
            nc.tensor.matmul(b[0:EXPERTS, 0:1], mask[:, 0, :], ones[:, 0:1], start=True, stop=False)
            PE.done("cnt", nc.tensor.matmul(b[0:EXPERTS, 0:1], mask[:, 1, :], ones[:, 0:1], start=False, stop=True))
            b = begin("cum")
            pe.wait_ge(dve_steps, DVE.at("x3"))
            PE.done("cum", nc.tensor.matmul(b[0:EXPERTS, 0:1], before[0:EXPERTS, 0:EXPERTS], extra[0:EXPERTS, :], start=True, stop=True))
            b = begin("table")
            pe.wait_ge(dve_steps, DVE.at("tE"))
            PE.done("table", nc.tensor.matmul(b[:, 0:3 * MORE], ones[0:EXPERTS, :], table_in, start=True, stop=True))
            b = begin("gateT")
            pe.wait_ge(dve_steps, DVE.at("gate1"))
            for t in range(TT):
                last = nc.tensor.transpose(b[0:EXPERTS, t * P:(t + 1) * P], gate[:, t, :], ident)
            PE.done("gateT", last)

            pe.wait_ge(dve_steps, DVE.at("pos1"))
            pe.wait_ge(act_steps, ACTS.at("gateT"))
            pe.wait_ge(ld["b_dn"], 16)
            for t in range(TT):
                for h in range(2):
                    last = nc.tensor.matmul(y_acc[t][h][:, :], gateT[:, t * P:(t + 1) * P], b_dn[:, h * HALF:(h + 1) * HALF],
                                            start=True, stop=False, skip_group_check=True)
            PE.done("y_start", last)

            def gather(b, ready):
                pe.wait_ge(sel_ready, ready)
                for k in range(KD):
                    for t in range(TT):
                        last = nc.tensor.matmul(ps_a[:, k * SLOT:(k + 1) * SLOT], hn[:, t, k * P:(k + 1) * P], sel[b][:, t, :],
                                                start=t == 0, stop=t == TT - 1)
                last.then_inc(xet_done, 1)

            def scatter(stop):
                for t in range(TT):
                    for h in range(2):
                        last = nc.tensor.matmul(y_acc[t][h][:, :], GT[:, t * P:(t + 1) * P], y_sb[:, h, :],
                                                start=False, stop=stop, skip_group_check=True)
                return last

            gather(0, 1)
            pe.wait_ge(pool_steps, POOL.at("zero_b"))
            pe.wait_ge(ld["b_gu"], 16)
            n_turns = pe.value_load(turns[0:1, 0:1], min_val=EXPERTS // 2, max_val=(EXPERTS + MAX_MORE) // 2)
            with pe.Fori(0, n_turns) as i:
                for b in range(2):
                    n = i * 2 + b
                    pe.wait_ge(xet_ready, n + 1)
                    for u, ps in enumerate((ps_gate, ps_up)):
                        for h in range(2):
                            nc.tensor.matmul(ps[64 * h:64 * h + 64, :], onehot[b], b_gu[:, u * FF + h * HALF:u * FF + (h + 1) * HALF],
                                             start=True, stop=False)
                    for c in range(NCHUNK):
                        pe.wait_ge(gu_loaded[b][c], (i + 1) * 16)
                        for k in range(c * KD // NCHUNK, (c + 1) * KD // NCHUNK):
                            for u, ps in enumerate((ps_gate, ps_up)):
                                for h in range(2):
                                    last = nc.tensor.matmul(ps[64 * h:64 * h + 64, :], xeT[b][:, k * SLOT:(k + 1) * SLOT],
                                                            GU[b][:, k, u * FF + h * HALF:u * FF + (h + 1) * HALF],
                                                            start=False, stop=k == KD - 1)
                        last.then_inc(gu_used, 1)
                        if c == 1 and b == 0:
                            pe.wait_ge(y_ready, n + 1)
                            scatter(False)
                        if c == 1 and b == 1:
                            for t in range(TT):
                                last = nc.tensor.transpose(ps_b[:, t * P:(t + 1) * P], selG[:, t].rearrange("p b j -> p (b j)"), ident)
                            last.then_inc(gt_done, 1)
                    pe.wait_ge(y_ready, n + 1)
                    gather(1 - b, n + 2)
                    pe.wait_ge(h_ready, n + 1)
                    if b == 1:
                        pe.wait_ge(gt_ready, i + 1)
                    for c in range(4):
                        last = nc.tensor.transpose(ps_b[:, c * P:(c + 1) * P], h_sb[:, c * P:(c + 1) * P], ident)
                    last.then_inc(t_done, 1)
                    pe.wait_ge(hT_ready, n + 1)
                    pe.wait_ge(xet_ready, n + 2)
                    for c in range(DCHUNK):
                        pe.wait_ge(dn_loaded[c], (n + 1) * 16)
                        for k in range(c * KD // DCHUNK, (c + 1) * KD // DCHUNK):
                            o = (k % 4) * P + (k // 4) * SLOT
                            for h in range(2):
                                last = nc.tensor.matmul(ps_a[64 * h:64 * h + 64, :], hT[:, o:o + SLOT], DN[:, k, h * HALF:(h + 1) * HALF],
                                                        start=k == 0, stop=k == KD - 1)
                        last.then_inc(dn_used, 1)
            pe.wait_ge(y_ready, n_turns * 2 + 1)
            scatter(True).then_inc(y_final, 1)

        @block.scalar
        def _(act):
            def own(name):
                act.wait_ge(act_steps, ACTS.at(name))

            for r, (g, n) in enumerate(((attn_norm_g, 8), (ffn_norm_g, 8), (q_a_norm_g, 2), (kv_a_norm_g, 2))):
                at = (0, 8, 16, 18)[r]
                act.dma_start(gr[at:at + n, :], g[0].rearrange("(k p) -> k p", p=P)).then_inc(ld["gains"], 16)
            act.dma_start(gr[20:21, 0:64], a_q_norm_g[0:1, :]).then_inc(ld["gains"], 16)
            act.dma_start(gr[20:21, 64:128], a_q_norm_g[0:1, :]).then_inc(ld["gains"], 16)
            act.dma_start(gr[21:22, 0:64], a_k_norm_g[0:1, :]).then_inc(ld["gains"], 16)
            act.dma_start(gr[21:22, 64:128], a_k_norm_g[0:1, :]).then_inc(ld["gains"], 16)
            act.dma_start(gr[22:23, :], b_q_norm_g[0:1, 0:NOPE]).then_inc(ld["gains"], 16)
            act.dma_start(gr[23:24, :], b_k_norm_g[0:1, 0:NOPE]).then_inc(ld["gains"], 16)
            act.dma_start(gq_rope[:, :], b_q_norm_g[0:1, NOPE:QK_DIM].to_broadcast([P, ROPE])).then_inc(ld["gains"], 16)
            act.dma_start(gk_rope[:, :], b_k_norm_g[0:1, NOPE:QK_DIM].to_broadcast([P, ROPE])).then_inc(ld["gains"], 16)
            act.dma_start(router_bias[:, :], router_b[0:1, :].to_broadcast([P, EXPERTS])).then_inc(ld["gains"], 16)
            act.dma_start(w_router[:, :, :], router_w[0].rearrange("(k p) e -> p k e", p=P)).then_inc(ld["small"], 16)
            act.dma_start(rel_tab, c_rel[:, :]).then_inc(ld["rel"], 16)
            act.dma_start(rel_sb, rel_bias[:, :]).then_inc(ld["rel"], 16)

            for t in range(TT):
                act.wait_ge(ld[f"x{t}"], 16)
                ACTS.done(f"sqx{t}", nc.scalar.activation(sq[:, 0:D], xs[:, t, :], ACT.Square, scale=float(D) ** -0.5, accum_out=r_x[:, t:t + 1]))
                own(f"sqx{t}")

            act.wait_ge(dve_steps, DVE.at("rel"))
            act.dma_start(dram_bias[:, :], rel_rev).then_inc(st_bias, 16)

            def scaled(name, o, n, r):
                act.wait_ge(pe_steps, PE.at(name))
                ACTS.done(name, nc.scalar.activation(o, bank[job_at[name] % 8][:, 0:n], ACT.Copy, scale=r))

            for t in range(TT):
                act.wait_ge(pool_steps, POOL.at(f"px{t}"))
                scaled(f"pC{t}", pr[:, t, C_COL:C_COL + 512], 512, r_x[:, t:t + 1])
                scaled(f"pE{t}", pr[:, t, KPE_COL:IN_W], ROPE, r_x[:, t:t + 1])
                own(f"pE{t}")
                for g, n in ((0, "sqc"), (1, "sqc_b")):
                    ACTS.done(f"{n}{t}", nc.scalar.activation(sq[:, 0:LORA], pr[:, t, C_COL + g * LORA:C_COL + (g + 1) * LORA], ACT.Square,
                                                              scale=float(LORA) ** -0.5, accum_out=r_c[:, t, g:g + 1]))
                    own(f"{n}{t}")
                ACTS.done(f"sqe{t}", nc.scalar.activation(sq[:, 0:ROPE], pr[:, t, KPE_COL:IN_W], ACT.Square, accum_out=s_kpe[:, t:t + 1]))
                own(f"sqe{t}")
            act.wait_ge(st_bias, 16)
            act.dma_start(hankel.rearrange("p (h k) -> p h k", h=A_HEADS), bass.AP(dram_bias, 0, [[1, P], [384, A_HEADS], [1, SEQ]])).then_inc(ld["bias_a"], 16)
            for t in range(TT):
                scaled(f"pK{t}", pr[:, t, 512:1024], 512, r_x[:, t:t + 1])
            for g in range(4):
                act.wait_ge(pe_steps, PE.at(f"band{g}"))
                ACTS.done(f"band{g}", nc.scalar.activation(bias_a[:, 2 * g:2 * g + 2, :].rearrange("p h k -> p (h k)"),
                                                           bank[job_at[f"band{g}"] % 8][:, :], ACT.Copy))
            for t in range(TT):
                act.wait_ge(pool_steps, POOL.at(f"pc{t}"))
                q_flat = qb[:, t].rearrange("p h n -> p (h n)")
                k_flat = kvb[:, t].rearrange("p h n -> p (h n)")
                scaled(f"qba{t}", q_flat[:, 0:384], 384, r_c[:, t, 0:1])
                scaled(f"qbb{t}", q_flat[:, 384:768], 384, r_c[:, t, 0:1])
                scaled(f"kva{t}", k_flat[:, 0:512], 512, r_c[:, t, 1:2])
                scaled(f"kvb{t}", k_flat[:, 512:1024], 512, r_c[:, t, 1:2])
                own(f"qbb{t}")
                if t:
                    act.wait_ge(dve_steps, DVE.at(f"sumk{t - 1}"))
                    act.wait_ge(dve_steps, DVE.at(f"sumA{t - 1}"))
                ACTS.done(f"sqq{t}", nc.scalar.activation(sqw[:, 0:768], q_flat, ACT.Square))
                own(f"kvb{t}")
                ACTS.done(f"sqk{t}", nc.scalar.activation(sqw[:, 768:1280].rearrange("p (h n) -> p h n", h=4), kvb[:, t, :, 0:NOPE], ACT.Square))
                scaled(f"pQ{t}", pr[:, t, 0:512], 512, r_x[:, t:t + 1])
                own(f"pQ{t}")
                if t:
                    act.wait_ge(dve_steps, DVE.at(f"sumA{t - 1}"))
                ACTS.done(f"sqa{t}", nc.scalar.activation(sq[:, 0:1024], pr[:, t, 0:1024], ACT.Square))
            for t in range(TT):
                scaled(f"pV{t}", pr[:, t, 1024:1536], 512, r_x[:, t:t + 1])

            def copied(name, o, i):
                act.wait_ge(pe_steps, PE.at(name))
                ACTS.done(name, nc.scalar.activation(o, i, ACT.Copy))

            def of(name, rows=P):
                return bank[job_at[name] % 8][0:rows, :].rearrange("p (h t) -> p h t", h=4)

            for t in range(TT):
                cols = slice(t * P, (t + 1) * P)
                copied(f"tnk{t}", kTn[:, :, cols], of(f"tnk{t}"))
                copied(f"trq{t}", qTr[:, :, cols], of(f"trq{t}", ROPE))
                copied(f"trk{t}", kTr[:, :, cols], of(f"trk{t}", ROPE))
                copied(f"tak{t}", kTa[:, :, cols], of(f"tak{t}"))
            for t in range(TT):
                act.wait_ge(dve_steps, DVE.at(f"max{t}"))
                for h in range(12):
                    ACTS.done(f"e{t}{h}", nc.scalar.activation(prob[t][:, h, :], prob[t][:, h, :], ACT.Exp, bias=n_max[:, t, h:h + 1],
                                                               accum_out=den[:, t, h:h + 1]))
            for g in range(0, 6, 2):
                copied(f"P1{g}", probT1[g], bank[job_at[f"P1{g}"] % 8][:, :])
            for t in range(TT):
                for g in range(2):
                    copied(f"mT{t}{g}", mixT[:, 4 * g:4 * g + 4, t * P:(t + 1) * P], of(f"mT{t}{g}"))
            for t in range(TT):
                act.wait_ge(dve_steps, DVE.at(f"oP{t}1"))
                ACTS.done(f"sq2_{t}", nc.scalar.activation(sqw[:, 0:D], xs[:, t, :], ACT.Square, scale=float(D) ** -0.5, accum_out=r_2[:, t:t + 1]))
                own(f"sq2_{t}")
            act.dma_start(b_dn, b_down[0]).then_inc(ld["b_dn"], 16)
            for t in range(TT):
                act.wait_ge(dve_steps, DVE.at(f"nm1_{t}"))
                ACTS.done(f"exp{t}", nc.scalar.activation(ex[:, t, :], lg[:, t, 0:EXPERTS], ACT.Exp, bias=n_m1[:, t:t + 1]))
            copied("gateT", gateT, bank[job_at["gateT"] % 8][0:EXPERTS, 0:SEQ])

            act.wait_ge(pool_steps, POOL.at("zero_b"))
            act.dma_start(b_gu[0:EXPERTS, :], b_gate_up[0]).then_inc(ld["b_gu"], 16)

            n_turns = act.value_load(turns[0:1, 0:1], min_val=EXPERTS // 2, max_val=(EXPERTS + MAX_MORE) // 2)
            with act.Fori(0, n_turns) as i:
                for b in range(2):
                    n = i * 2 + b
                    if b == 1:
                        act.wait_ge(gt_done, i + 1)
                        nc.scalar.activation(GT, ps_b[:, 0:SEQ], ACT.Copy).then_inc(gt_ready, 1)
                    act.wait_ge(gate_ready, n + 1)
                    nc.scalar.activation(h_sb, g_sb, ACT.Sigmoid, scale=ALPHA).then_inc(sig_ready, 1)
                    act.wait_ge(t_done, n + 1)
                    nc.scalar.activation(hT, ps_b[:, :], ACT.Copy).then_inc(hT_ready, 1)
                    act.wait_ge(dn_used, (n + 1) * DCHUNK)
                    for h in range(2):
                        last = nc.scalar.activation(y_sb[64 * b:64 * b + 64, h, :], ps_a[64 * h:64 * h + 64, :], ACT.Copy)
                    last.then_inc(y_ready, 1)

        @block.vector
        def _(dve):
            V = nc.vector

            def own(name):
                dve.wait_ge(dve_steps, DVE.at(name))

            def ps(name, rows=P):
                dve.wait_ge(pe_steps, PE.at(name))
                return bank[job_at[name] % 8][0:rows, :]

            def mean(name, r, add, times):
                DVE.done(name, V.tensor_scalar(r, r, add, times, ALU.add, ALU.mult))

            for t in range(TT):
                dve.wait_ge(act_steps, ACTS.at(f"sqx{t}"))
                mean(f"rx{t}", r_x[:, t:t + 1], EPS, 1.0)
            DVE.done("gains", V.tensor_copy(gains[:, :], ps("gains")[:, 0:24]))
            own("gains")
            DVE.done("ga", V.tensor_tensor(gain_a, gains[:, 20:21], gains[:, 21:22], ALU.mult))
            DVE.done("gb", V.tensor_tensor(gain_b, gains[:, 22:23], gains[:, 23:24], ALU.mult))
            DVE.done("rel", V.tensor_tensor(rel_rev, ps("rel", A_HEADS)[:, 0:384], rel_tab[0:A_HEADS, 384:768], ALU.add))

            def with_gain(name, o, at, n=4):
                src = ps(name)[:, 0:512].rearrange("p (k t) -> p k t", k=4)
                g = gains[:, at:at + 4].unsqueeze(2).to_broadcast([P, 4, P])
                DVE.done(name, V.tensor_tensor(o, src, g, ALU.mult))

            for t in range(TT):
                for g in range(2):
                    with_gain(f"xT{t}{g}", xT[:, 4 * g:4 * g + 4, t * P:(t + 1) * P], 4 * g)
            for t in range(TT):
                dve.wait_ge(act_steps, ACTS.at(f"sqc_b{t}"))
                mean(f"rc{t}", r_c[:, t, :], EPS, 1.0)
            for t in range(TT):
                with_gain(f"cT{t}", cT[:, :, t * P:(t + 1) * P], 16)

            for t in range(TT):
                dve.wait_ge(act_steps, ACTS.at(f"sqk{t}"))
                DVE.done(f"sumq{t}", V.tensor_reduce(r_q[:, t, :], sqw[:, 0:768].rearrange("p (h n) -> p h n", h=4), AX, ALU.add))
                own(f"sumq{t}")
                mean(f"rq{t}", r_q[:, t, :], QK_DIM * EPS, 1.0)
                DVE.done(f"sumk{t}", V.tensor_reduce(r_k[:, t, :], sqw[:, 768:1280].rearrange("p (h n) -> p h n", h=4), AX, ALU.add))
                own(f"sumk{t}")
                DVE.done(f"addk{t}", V.tensor_scalar(r_k[:, t, :], r_k[:, t, :], s_kpe[:, t:t + 1], 1.0 / QK_DIM, ALU.add, ALU.mult))
                own(f"addk{t}")
                mean(f"rk{t}", r_k[:, t, :], EPS, 1.0)
                dve.wait_ge(act_steps, ACTS.at(f"sqa{t}"))
                DVE.done(f"sumA{t}", V.tensor_reduce(r_a[:, t, :], sq[:, 0:1024].rearrange("p (h n) -> p h n", h=16), AX, ALU.add))
                own(f"sumA{t}")
                mean(f"rAq{t}", r_a[:, t, 0:8], A_DIM * EPS, 1.0)
                mean(f"rAk{t}", r_a[:, t, 8:16], A_DIM * EPS, 1.0 / A_DIM)
                kn = kvb[:, t, :, 0:NOPE]
                dve.wait_ge(pool_steps, POOL.at(f"pk{t}"))
                DVE.done(f"nscale{t}", V.tensor_tensor(kn, kn, r_k[:, t, :].unsqueeze(2).to_broadcast([P, 4, NOPE]), ALU.mult))
                dve.wait_ge(pool_steps, POOL.at(f"kadd{t}"))
                kr = sq[:, 1280 + t * 512:1536 + t * 512].rearrange("p (h r) -> p h r", h=4)
                DVE.done(f"kpe{t}", V.tensor_tensor(kr, k_rot[:, t, :].unsqueeze(1).to_broadcast([P, 4, ROPE]),
                                                    r_k[:, t, :].unsqueeze(2).to_broadcast([P, 4, ROPE]), ALU.mult))
                kk = pr[:, t, 512:1024].rearrange("p (h n) -> p h n", h=8)
                dve.wait_ge(pool_steps, POOL.at(f"pa{t}"))
                DVE.done(f"kscale{t}", V.tensor_tensor(kk, kk, r_a[:, t, 8:16].unsqueeze(2).to_broadcast([P, 8, A_DIM]), ALU.mult))
            for t in range(TT):
                cols = slice(t * P, (t + 1) * P)
                DVE.done(f"tnq{t}", V.tensor_scalar(qTn[:, :, cols], ps(f"tnq{t}").rearrange("p (h t) -> p h t", h=4), gain_b, None, ALU.mult))
                DVE.done(f"taq{t}", V.tensor_scalar(qTa[:, :, cols], ps(f"taq{t}").rearrange("p (h t) -> p h t", h=4), gain_a, None, ALU.mult))
            for t in range(TT):
                nk = (t + 1) * P
                for name, (tt, heads) in heads_of.items():
                    if tt != t:
                        continue
                    src = ps(name)
                    for j, h in enumerate(heads):
                        r = r_a[:, t, h:h + 1] if h < 8 else r_q[:, t, h - 8:h - 7]
                        add = bias_a[:, h, SEQ - nk:SEQ] if h < 8 else causal[:, SEQ - nk:SEQ]
                        dve.wait_ge(act_steps, ACTS.at("band3"))
                        DVE.done(f"{name}{h}", V.scalar_tensor_tensor(prob[t][:, h, :], src[:, j * nk:(j + 1) * nk], r, add, ALU.mult, ALU.add))
                own(("s0b", "s1f")[t] + "11")
                DVE.done(f"max{t}", V.tensor_reduce(n_max[:, t, :], prob[t], AX, ALU.max, negate=True))

            def copied(name, o):
                DVE.done(name, V.tensor_copy(o, ps(name)))

            def outputs(t):
                for name, h0, nh, w, c0 in ((f"vA{t}", 0, 8, A_DIM, 0), (f"vB{t}", 8, 4, V_DIM, A_WIDTH)):
                    DVE.done(name, V.tensor_tensor(mixed[:, t, c0:c0 + 512].rearrange("p (h n) -> p h n", h=nh),
                                                   ps(name).rearrange("p (h n) -> p h n", h=nh),
                                                   den[:, t, h0:h0 + nh].unsqueeze(2).to_broadcast([P, nh, w]), ALU.mult))

            dve.wait_ge(act_steps, ACTS.at("e011"))
            DVE.done("rden0", V.reciprocal(den[:, 0, :], den[:, 0, :]))
            for g in range(3):
                copied(f"P0{g}", probT0[:, g * 512:(g + 1) * 512])
            own("rden0")
            outputs(0)
            dve.wait_ge(act_steps, ACTS.at("e111"))
            DVE.done("rden1", V.reciprocal(den[:, 1, :], den[:, 1, :]))
            for g in range(1, 6, 2):
                copied(f"P1{g}", probT1[g])
            own("rden1")
            outputs(1)
            for t in range(TT):
                for g in range(2):
                    part = xs[:, t, g * HALF:(g + 1) * HALF]
                    DVE.done(f"oP{t}{g}", V.tensor_tensor(part, ps(f"oP{t}{g}"), part, ALU.add))
                dve.wait_ge(act_steps, ACTS.at(f"sq2_{t}"))
                mean(f"r2{t}", r_2[:, t:t + 1], EPS, 1.0)
                dve.wait_ge(pool_steps, POOL.at(f"p2{t}"))
                DVE.done(f"hn{t}", V.tensor_scalar(hn[:, t, :], xs[:, t, :], r_2[:, t:t + 1], None, ALU.mult))
            for t in range(TT):
                for g in range(2):
                    with_gain(f"hT{t}{g}", h2T[:, 4 * g:4 * g + 4, t * P:(t + 1) * P], 8 + 4 * g)
            DVE.done("low", V.memset(lg[:, :, EXPERTS:EXPERTS + 4], LOW))
            DVE.done("low4", V.memset(top4[:, :, TOP_K:8], LOW))
            DVE.done("first0", V.memset(slot_first[:, 0:EXPERTS], 0.0))
            for t in range(TT):
                src = ps(f"lg{t}")
                DVE.done(f"lg{t}", V.tensor_tensor(lg[:, t, 0:EXPERTS], src[:, 0:EXPERTS], router_bias[:, :], ALU.add))
                own(f"lg{t}")
                DVE.done(f"max8_{t}", V.max(m8[:, t, :], lg[:, t, 0:EXPERTS]))
                own(f"max8_{t}")
                DVE.done(f"top{t}", V.tensor_copy(top4[:, t, 0:TOP_K], m8[:, t, 0:TOP_K]))
                DVE.done(f"nm1_{t}", V.tensor_scalar(n_m1[:, t:t + 1], m8[:, t, 0:1], -1.0, None, ALU.mult))
                own(f"top{t}")
                DVE.done(f"rep{t}", V.match_replace(rep[:, t, 0:36], top4[:, t, :], lg[:, t, 0:36], -LOW))
                own(f"rep{t}")
                DVE.done(f"mask{t}", V.tensor_tensor(mask[:, t, :], rep[:, t, 0:EXPERTS], lg[:, t, 0:EXPERTS], ALU.not_equal))
            E = EXPERTS
            DVE.done("cnt", V.tensor_copy(cnt[0:E], ps("cnt", E)[:, 0:1]))
            own("cnt")
            DVE.done("x1", V.tensor_scalar(extra[0:E], cnt[0:E], float(SLOT), None, ALU.is_gt))
            own("x1")
            DVE.done("x2", V.scalar_tensor_tensor(extra[0:E], cnt[0:E], 2.0 * SLOT, extra[0:E], ALU.is_gt, ALU.add))
            own("x2")
            DVE.done("x3", V.scalar_tensor_tensor(extra[0:E], cnt[0:E], 3.0 * SLOT, extra[0:E], ALU.is_gt, ALU.add))
            DVE.done("cum", V.tensor_copy(cum[0:E], ps("cum", E)[:, 0:1]))
            own("cum")
            DVE.done("td", V.tensor_scalar(tdist, iota[0:E, 0:MORE], cum[0:E], None, ALU.subtract))
            own("td")
            DVE.done("tge", V.tensor_scalar(tlow, tdist, 0.0, None, ALU.is_ge))
            own("tge")
            DVE.done("tlt", V.tensor_scalar(table_in[:, 0:MORE], tdist, extra[0:E], None, ALU.is_lt))
            own("tlt")
            DVE.done("tA", V.tensor_tensor(table_in[:, 0:MORE], table_in[:, 0:MORE], tlow, ALU.mult))
            own("tA")
            DVE.done("tR", V.scalar_tensor_tensor(table_in[:, MORE:2 * MORE], tdist, 1.0, table_in[:, 0:MORE], ALU.add, ALU.mult))
            DVE.done("tE", V.tensor_scalar(table_in[:, 2 * MORE:3 * MORE], table_in[:, 0:MORE], row_id[0:E], None, ALU.mult))
            DVE.done("table", V.tensor_copy(table, ps("table")[:, 0:3 * MORE]))
            own("table")
            DVE.done("first_m", V.tensor_scalar(slot_first[:, EXPERTS:SLOTS], table[:, 0:MORE], -8.0 * SLOT, 8.0 * SLOT, ALU.mult, ALU.add))
            own("first_m")
            DVE.done("first", V.scalar_tensor_tensor(slot_first[:, EXPERTS:SLOTS], table[:, MORE:2 * MORE], float(SLOT), slot_first[:, EXPERTS:SLOTS], ALU.mult, ALU.add))
            DVE.done("slots_e", V.tensor_copy(slot_e[0:1, EXPERTS:SLOTS], table[0:1, 2 * MORE:3 * MORE]))
            DVE.done("main_e", V.tensor_copy(slot_e[0:1, 0:EXPERTS], expert_id[0:1, :]))
            DVE.done("pairsum", V.tensor_reduce(pairs[0:1], table[0:1, 0:MORE].rearrange("p (s two) -> p two s", two=2)[:, 0, :], AX, ALU.add))
            own("pairsum")
            DVE.done("turns", V.tensor_scalar(turns[0:1, 0:1], pairs[0:1], float(EXPERTS // 2), None, ALU.add))
            for t in range(TT):
                dve.wait_ge(act_steps, ACTS.at(f"exp{t}"))
                DVE.done(f"gm{t}", V.tensor_tensor(ex[:, t, :], ex[:, t, :], mask[:, t, :], ALU.mult))
                own(f"gm{t}")
                DVE.done(f"gden{t}", V.tensor_reduce(g_den[:, t:t + 1], ex[:, t, :], AX, ALU.add))
                own(f"gden{t}")
                DVE.done(f"grd{t}", V.reciprocal(g_den[:, t:t + 1], g_den[:, t:t + 1]))
                own(f"grd{t}")
                DVE.done(f"gate{t}", V.tensor_scalar(gate[:, t, :], ex[:, t, :], g_den[:, t:t + 1], None, ALU.mult))
            for t in range(TT):
                src = ps(f"rank{t}")
                DVE.done(f"posr{t}", V.scalar_tensor_tensor(pos[:, t, :], src[:, 0:EXPERTS], 1.0, mask[:, t, :], ALU.add, ALU.mult))
                own(f"posr{t}")
                DVE.done(f"pos{t}", V.tensor_scalar(pos[:, t, :], pos[:, t, :], -1.0, None, ALU.add))

            ffn_gain = gains[:, 8:16].unsqueeze(2).to_broadcast([P, KD, SLOT])

            def select(b, steps, pair_read=None):
                dve.wait_ge(select_steps, steps)
                if pair_read is not None:
                    dve.wait_ge(gt_done, pair_read)
                for t in range(TT):
                    V.tensor_scalar(sel[b][:, t, :], iota, rel_pos[b][:, t:t + 1], None, ALU.is_equal)
                    last = V.tensor_scalar(selG[:, t, b, :], iota, rel_pos[b][:, t:t + 1], slot_gate[b][:, t:t + 1],
                                           ALU.is_equal, ALU.mult)
                last.then_inc(sel_ready, 1)

            def take_tokens(b):
                V.tensor_tensor(xeT[b].rearrange("p (k j) -> p k j", k=KD), ps_a[:, :].rearrange("p (k j) -> p k j", k=KD),
                                ffn_gain, ALU.mult).then_inc(xet_ready, 1)

            dve.wait_ge(pe_steps, PE.at("y_start"))
            select(0, SEL_OPS)
            dve.wait_ge(xet_done, 1)
            take_tokens(0)
            n_turns = dve.value_load(turns[0:1, 0:1], min_val=EXPERTS // 2, max_val=(EXPERTS + MAX_MORE) // 2)
            with dve.Fori(0, n_turns) as i:
                for b in range(2):
                    n = i * 2 + b
                    select(1 - b, (n + 2) * SEL_OPS, pair_read=i + 1 if b == 1 else None)
                    dve.wait_ge(gu_used, (n + 1) * NCHUNK)
                    V.tensor_scalar(g_sb, ps_gate[:, :], LIMIT, None, ALU.min).then_inc(gate_ready, 1)
                    V.tensor_scalar(u_sb, ps_up[:, :], LIMIT, -LIMIT, ALU.min, ALU.max).then_inc(up_ready, 1)
                    dve.wait_ge(gate_ready, n + 1)
                    dve.wait_ge(up_ready, n + 1)
                    V.scalar_tensor_tensor(u_sb, u_sb, 1.0, g_sb, ALU.add, ALU.mult).then_inc(upgate_ready, 1)
                    dve.wait_ge(upgate_ready, n + 1)
                    dve.wait_ge(sig_ready, n + 1)
                    V.tensor_tensor(h_sb, h_sb, u_sb, ALU.mult).then_inc(h_ready, 1)
                    dve.wait_ge(xet_done, n + 2)
                    take_tokens(1 - b)
            dve.wait_ge(y_final, 1)
            for t in range(TT):
                for h in range(2):
                    V.tensor_tensor(y_out[:, t, h * HALF:(h + 1) * HALF], y_acc[t][h][:, :], xs[:, t, h * HALF:(h + 1) * HALF],
                                    ALU.add).then_inc(out_ready, 1)

        @block.gpsimd
        def _(pool):
            G = nc.gpsimd

            def own(name):
                pool.wait_ge(pool_steps, POOL.at(name))

            def rotate(kind, t, o, scratch, cos, sin):
                POOL.done(f"{kind}c{t}", G.tensor_tensor(scratch[0], o, cos, ALU.mult))
                POOL.done(f"{kind}s1{t}", G.tensor_tensor(scratch[1][..., 0:32], o[..., 32:64], sin[..., 0:32], ALU.mult))
                POOL.done(f"{kind}s2{t}", G.tensor_tensor(scratch[1][..., 32:64], o[..., 0:32], sin[..., 32:64], ALU.mult))
                own(f"{kind}s2{t}")
                return G.tensor_tensor(o, scratch[0], scratch[1], ALU.add)

            def root(name, r, n, made):
                pool.wait_ge(dve_steps, DVE.at(made))
                POOL.done(name, G.tensor_tensor(r, r, minus_half[:, :].to_broadcast([P, n]), ALU.pow))

            POOL.done("half", G.memset(minus_half[:, :], -0.5))
            own("half")
            for t in range(TT):
                root(f"px{t}", r_x[:, t:t + 1], 1, f"rx{t}")
            for t in range(TT):
                root(f"pc{t}", r_c[:, t, :], 2, f"rc{t}")
            pool.wait_ge(ld["const"], 16)
            pool.wait_ge(ld["gains"], 16 * GAIN_DMAS)
            for t in range(TT):
                k = k_rot[:, t, :]
                pool.wait_ge(act_steps, ACTS.at(f"pE{t}"))
                POOL.done(f"gk{t}", G.tensor_tensor(k, pr[:, t, KPE_COL:IN_W], gk_rope[:, :], ALU.mult))
                own(f"gk{t}")
                last = rotate("k", t, k, (rs0[:, 0, :], rs1[:, 0, :]), cos2[:, t, :], sin2[:, t, :])
                POOL.done(f"kadd{t}", last)
                own(f"kadd{t}")
            for t in range(TT):
                q = sq[:, 1024 + t * 512:1280 + t * 512].rearrange("p (h r) -> p h r", h=4)
                pool.wait_ge(act_steps, ACTS.at(f"qbb{t}"))
                POOL.done(f"gq{t}", G.tensor_tensor(q, qb[:, t, :, NOPE:QK_DIM], gq_rope[:, :].unsqueeze(1).to_broadcast([P, 4, ROPE]), ALU.mult))
                own(f"gq{t}")
                last = rotate("q", t, q, (rs0[:, :, :], rs1[:, :, :]), cos2[:, t, :].unsqueeze(1).to_broadcast([P, 4, ROPE]),
                              sin2[:, t, :].unsqueeze(1).to_broadcast([P, 4, ROPE]))
                POOL.done(f"qadd{t}", last)
                own(f"qadd{t}")
                root(f"pq{t}", r_q[:, t, :], 4, f"rq{t}")
                root(f"pk{t}", r_k[:, t, :], 4, f"rk{t}")
                root(f"pa{t}", r_a[:, t, :], 16, f"rAk{t}")
            for t in range(TT):
                root(f"p2{t}", r_2[:, t:t + 1], 1, f"r2{t}")
            pool.wait_ge(dve_steps, DVE.at("lg1"))
            G.memset(y_sb, 0.0).then_inc(y_ready, 1)
            POOL.done("zero_G", G.memset(GT, 0.0))
            POOL.done("zero_b", G.memset(b_gu, 0.0))

            def select(b, n):
                e = pool.value_load(slot_e[0:1, bass.ds(n, 1)] if not isinstance(n, int) else slot_e[0:1, n:n + 1], min_val=0, max_val=EXPERTS - 1)
                first = slot_first[:, bass.ds(n, 1)] if not isinstance(n, int) else slot_first[:, n:n + 1]
                G.tensor_tensor(rel_pos[b].unsqueeze(2), pos[:, :, bass.ds(e, 1)], first.unsqueeze(1).to_broadcast([P, TT, 1]),
                                ALU.subtract).then_inc(select_steps, 1)
                G.tensor_copy(slot_gate[b].unsqueeze(2), gate[:, :, bass.ds(e, 1)]).then_inc(select_steps, 1)
                G.tensor_copy(onehot[b], ident[:, bass.ds(e, 1)].to_broadcast([P, SLOT])).then_inc(select_steps, 1)

            pool.wait_ge(dve_steps, DVE.at("pos1"))
            select(0, 0)
            n_turns = pool.value_load(turns[0:1, 0:1], min_val=EXPERTS // 2, max_val=(EXPERTS + MAX_MORE) // 2)
            with pool.Fori(0, n_turns) as i:
                for b in range(2):
                    pool.wait_ge(xet_done, i * 2 + b + 1)
                    select(1 - b, i * 2 + b + 1)


_INS = ['x', 'attn_norm_g', 'w_in', 'a_q_norm_g', 'a_k_norm_g', 'rel_bias', 'q_a_norm_g', 'w_q_b', 'kv_a_norm_g', 'w_kv_b',
        'b_q_norm_g', 'b_k_norm_g', 'w_out', 'ffn_norm_g', 'router_w', 'router_b', 'w_gate_up', 'b_gate_up', 'w_down', 'b_down']


def kernel(**inputs):
    import numpy as _np
    import concourse.bacc as _bacc
    from concourse import mybir as _mybir
    from concourse.bass_utils import run_bass_kernel_spmd as _run

    nc = _bacc.Bacc("TRN2", target_bir_lowering=False, num_devices=1, dynamic_dma_scratch_size=1024)
    c_all, c_rel = constants()
    arrays, args = {}, []
    for name, a in [(n, inputs[n]) for n in _INS] + [("c_all", c_all), ("c_rel", c_rel)]:
        a = _np.ascontiguousarray(a)
        arrays[f"in_{name}_dram"] = a
        args.append(nc.dram_tensor(f"in_{name}_dram", a.shape, _mybir.dt.from_np(a.dtype), kind="ExternalInput").ap())
    args.append(nc.dram_tensor("out_0_dram", (1, SEQ, D), _mybir.dt.float32, kind="ExternalOutput").ap())
    for i, name in enumerate(_INS):
        if name in ("w_gate_up", "w_down"):
            args[i] = args[i][0]
    layer_kernel(nc, *args)
    r = _run(nc, [arrays], core_ids=[0])
    return r.results[0]["out_0_dram"]
```

```python
from contextlib import ExitStack

import numpy as np

import concourse.bass as bass
from concourse import mybir

F32 = mybir.dt.float32
I32 = mybir.dt.int32
ALU = mybir.AluOpType
ACT = mybir.ActivationFunctionType
AX = mybir.AxisListType.X

P = 128
SEQ, D = 256, 1024
TT = SEQ // P
KD = D // P
HALF = 512
A_HEADS, A_DIM, A_WIDTH = 8, 64, 512
B_HEADS, NOPE, ROPE, V_DIM = 4, 128, 64, 128
QK_DIM = NOPE + ROPE
LORA = 256
C_COL = 3 * A_WIDTH
KPE_COL = C_COL + 2 * LORA
IN_W = KPE_COL + ROPE
EXPERTS, TOP_K, FF = 32, 4, 1024
LIMIT, ALPHA = 7.0, 1.702
EPS = 1e-6
BUCKETS, MAX_DIST = 32, 2048
NEG = -1e30
LOW = -3e38
SLOT = 64
MAX_MORE = 16
MORE = MAX_MORE + 2
SLOTS = EXPERTS + MORE
GAIN_DMAS = 11
NCHUNK, DCHUNK = 4, 2


def constants():
    eye = np.eye(P, dtype=np.float32)
    iota = np.tile(np.arange(64, dtype=np.float32), (P, 1))
    before = np.triu(np.ones((P, P), np.float32), 1)
    ones = np.ones((P, P), np.float32)
    q, k = np.arange(P)[:, None], np.arange(P)[None, :]
    causal = np.concatenate([np.zeros((P, P)), np.where(k <= q, 0.0, NEG)], 1).astype(np.float32)
    inv = (np.float32(10000.0) ** (-np.arange(0, ROPE, 2, dtype=np.float32) / np.float32(ROPE))).astype(np.float32)
    ang = np.arange(SEQ, dtype=np.float32)[:, None] * inv[None, :]
    cos, sin = np.cos(ang).astype(np.float32), np.sin(ang).astype(np.float32)
    cc = np.concatenate([cos, cos], 1).reshape(TT, P, ROPE).transpose(1, 0, 2).reshape(P, TT * ROPE)
    ss = np.concatenate([-sin, sin], 1).reshape(TT, P, ROPE).transpose(1, 0, 2).reshape(P, TT * ROPE)
    row = np.arange(P, dtype=np.float32)[:, None]
    slot_expert = np.tile(np.arange(EXPERTS, dtype=np.float32), (P, 1))
    c_all = np.concatenate([eye, eye[:, ::-1], iota, before, ones, causal, cc, ss, row, slot_expert], 1)
    d = 255 - np.arange(384)
    df = np.maximum(d, 1).astype(np.float32)
    half = BUCKETS // 2
    log_b = half + (np.log(df / half) / np.float32(np.log(MAX_DIST / half)) * half).astype(np.int32)
    bucket = np.where(d < half, np.maximum(d, 0), np.minimum(log_b, BUCKETS - 1))
    count = sum(((d >= 0) & (d <= w) & (d % r == 0)).astype(np.float32) for w, r in ((128, 1), (512, 4), (2048, 16)))
    onehot = (bucket[None, :] == np.arange(BUCKETS)[:, None]).astype(np.float32)
    lnc = np.where(count > 0, np.log(np.maximum(count, 1)), NEG).astype(np.float32)
    c_rel = np.concatenate([onehot, np.tile(lnc, (BUCKETS, 1))], 1)
    return np.ascontiguousarray(c_all, np.float32), np.ascontiguousarray(c_rel, np.float32)


C_ALL_W = 2 * P + 64 + P + P + 2 * P + TT * ROPE * 2 + 1 + EXPERTS


class Steps:

    def __init__(self, sem, names):
        self.sem, self.names, self.next = sem, list(names), 0
        assert len(set(self.names)) == len(self.names)

    def at(self, name):
        return self.names.index(name) + 1

    def done(self, name, instruction):
        assert self.names[self.next] == name, (self.names[self.next], name)
        self.next += 1
        instruction.then_inc(self.sem, 1)


def layer_kernel(nc, x, attn_norm_g, w_in, a_q_norm_g, a_k_norm_g, rel_bias, q_a_norm_g, w_q_b, kv_a_norm_g,
                 w_kv_b, b_q_norm_g, b_k_norm_g, w_out, ffn_norm_g, router_w, router_b, w_gate_up, b_gate_up,
                 w_down, b_down, c_all, c_rel, out):
    with ExitStack() as ctx:
        def sb(name, shape, dt=F32):
            return ctx.enter_context(nc.sbuf_tensor(name, shape, dt))

        def sem(name):
            return ctx.enter_context(nc.semaphore(name))

        ring = sb("ring", [P, 2 * KD * 2 * FF])
        dring = sb("dring", [P, KD * D])
        GU = [ring[:, b * KD * 2 * FF:(b + 1) * KD * 2 * FF].rearrange("p (k n) -> p k n", k=KD) for b in range(2)]
        DN = dring[:, :].rearrange("p (k n) -> p k n", k=KD)
        xs = sb("xs", [P, TT, D])
        hn = sb("hn", [P, TT, D])
        mt = sb("mt", [P, 7040])
        ca = sb("ca", [P, C_ALL_W])
        st = sb("st", [P, 256])
        rt = sb("rt", [P, 320])
        gains = sb("gains", [P, 24])
        gr_a = sb("gr_a", [8, P])
        gr = sb("gr", [16, P])
        gq_rope = sb("gq_rope", [P, ROPE])
        gk_rope = sb("gk_rope", [P, ROPE])
        router_bias = sb("router_bias", [P, EXPERTS])
        sqw = sb("sqw", [P, 1280])
        k_rot = sb("k_rot", [P, TT, ROPE])
        short = sb("short", [P, KD * ROPE + 2 * B_HEADS * ROPE])
        w_kpe = short[:, 0:512].rearrange("p (k n) -> p k n", k=KD)
        rs0 = short[:, 512:768].rearrange("p (h r) -> p h r", h=B_HEADS)
        rs1 = short[:, 768:1024].rearrange("p (h r) -> p h r", h=B_HEADS)
        b_dn = short[0:EXPERTS, :]
        w_router = sb("w_router", [P, KD, EXPERTS])
        minus_half = sb("minus_half", [P, 1])
        slot_e = sb("slot_e", [1, SLOTS], I32)
        turns = sb("turns", [1, 1], I32)
        dram_bias = nc.dram_tensor("dram_bias", (A_HEADS, 384), F32)

        def cut(t, at, n):
            return t[:, at:at + n]

        c0 = 0
        ident = cut(ca, c0, P); c0 += P
        flip = cut(ca, c0, P); c0 += P
        iota = cut(ca, c0, 64); c0 += 64
        before = cut(ca, c0, P); c0 += P
        ones = cut(ca, c0, P); c0 += P
        causal = cut(ca, c0, 2 * P); c0 += 2 * P
        cos2 = cut(ca, c0, TT * ROPE).rearrange("p (t r) -> p t r", t=TT); c0 += TT * ROPE
        sin2 = cut(ca, c0, TT * ROPE).rearrange("p (t r) -> p t r", t=TT); c0 += TT * ROPE
        row_id = cut(ca, c0, 1); c0 += 1
        expert_id = cut(ca, c0, EXPERTS); c0 += EXPERTS
        assert c0 == C_ALL_W

        CHUNK = KD * 2 * FF // NCHUNK

        def group(t, g):
            return t[:, g * CHUNK:(g + 1) * CHUNK].rearrange("p (k n) -> p k n", k=KD)

        w_c, w_k, w_q, w_v = (group(ring, g) for g in range(4))
        w_out_sb = [group(dring, g) for g in range(2)]
        T = ring[:, KD * 2 * FF:]
        t0 = 0

        def tcut(n):
            nonlocal t0
            t0 += n
            return T[:, t0 - n:t0]

        qTa_at = t0
        qTa = tcut(4 * SEQ).rearrange("p (h t) -> p h t", h=4)
        kTa = tcut(4 * SEQ).rearrange("p (h t) -> p h t", h=4)
        hankel = T[:, t0:t0 + 8 * SEQ]
        qTn = tcut(4 * SEQ).rearrange("p (h t) -> p h t", h=4)
        kTn = tcut(4 * SEQ).rearrange("p (h t) -> p h t", h=4)
        qTr = tcut(4 * SEQ)[0:ROPE].rearrange("p (h t) -> p h t", h=4)
        kTr = tcut(4 * SEQ)[0:ROPE].rearrange("p (h t) -> p h t", h=4)
        bias_a = tcut(A_HEADS * SEQ).rearrange("p (h t) -> p h t", h=A_HEADS)
        assert t0 <= 2 * CHUNK
        pr = tcut(TT * IN_W).rearrange("p (t n) -> p t n", t=TT)
        qb = tcut(TT * B_HEADS * QK_DIM).rearrange("p (t h n) -> p t h n", t=TT, h=B_HEADS)
        kvb = tcut(TT * B_HEADS * 256).rearrange("p (t h n) -> p t h n", t=TT, h=B_HEADS)
        assert t0 <= KD * 2 * FF
        rel_tab = T[0:BUCKETS, qTa_at:qTa_at + 768]
        rel_rev = T[0:A_HEADS, qTa_at + 768:qTa_at + 1152]
        rel_sb = T[0:BUCKETS, qTa_at + 1152:qTa_at + 1160]
        xT = mt[:, 0:2048].rearrange("p (k t) -> p k t", k=KD)
        wqb = mt[:, 2048:3584].rearrange("p (k n) -> p k n", k=2)
        wkvb = mt[:, 3584:5632].rearrange("p (k n) -> p k n", k=2)
        cT = mt[:, 5632:6656].rearrange("p (k t) -> p k t", k=4)
        prob = [mt[:, 0:1536].rearrange("p (h k) -> p h k", h=12), mt[:, 1536:4608].rearrange("p (h k) -> p h k", h=12)]
        mixed = mt[:, 4608:6656].rearrange("p (t n) -> p t n", t=TT)
        mixT = mt[:, 0:2048].rearrange("p (k t) -> p k t", k=KD)
        h2T = mt[:, 2048:4096].rearrange("p (k t) -> p k t", k=KD)
        sq = hn[:, :, :].rearrange("p t n -> p (t n)")
        probT0 = hn[:, :, :].rearrange("p t n -> p (t n)")
        probT1 = [pr[:, 0, 0:512], pr[:, 0, 512:1024], pr[:, 1, 0:512], pr[:, 1, 512:1024],
                  sq[:, 1536:2048], qb[:, 0].rearrange("p h n -> p (h n)")[:, 0:512]]
        s0 = 0

        def scut(n):
            nonlocal s0
            s0 += n
            return st[:, s0 - n:s0]

        r_x, r_2 = scut(TT), scut(TT)
        ss_2 = scut(2 * TT).rearrange("p (t g) -> p t g", t=TT)
        r_a = scut(TT * 16).rearrange("p (t n) -> p t n", t=TT)
        r_c = scut(TT * 2).rearrange("p (t n) -> p t n", t=TT)
        r_q = scut(TT * 4).rearrange("p (t n) -> p t n", t=TT)
        s_kpe = scut(TT)
        r_k = scut(TT * 4).rearrange("p (t n) -> p t n", t=TT)
        n_max = scut(TT * 12).rearrange("p (t n) -> p t n", t=TT)
        den = scut(TT * 12).rearrange("p (t n) -> p t n", t=TT)
        g_den = scut(TT)
        n_m1 = scut(TT)
        gain_a, gain_b = scut(1), scut(1)
        cnt, extra, cum = scut(1), scut(1), scut(1)
        assert s0 <= 256
        r0 = 0

        def rcut(n):
            nonlocal r0
            r0 += n
            return rt[:, r0 - n:r0]

        pos = rcut(TT * EXPERTS).rearrange("p (t e) -> p t e", t=TT)
        gate = rcut(TT * EXPERTS).rearrange("p (t e) -> p t e", t=TT)
        slot_first = rcut(SLOTS)
        rel_pos = [rcut(TT) for _ in range(2)]
        slot_gate = [rcut(TT) for _ in range(2)]
        R = sqw
        lg = R[:, 0:80].rearrange("p (t e) -> p t e", t=TT)
        rep = R[:, 80:160].rearrange("p (t e) -> p t e", t=TT)
        m8 = R[:, 160:176].rearrange("p (t e) -> p t e", t=TT)
        top4 = R[:, 176:192].rearrange("p (t e) -> p t e", t=TT)
        mask = R[:, 192:256].rearrange("p (t e) -> p t e", t=TT)
        ex = R[:, 256:320].rearrange("p (t e) -> p t e", t=TT)
        table_in = R[0:EXPERTS, 320:320 + 3 * MORE]
        tdist = R[0:EXPERTS, 400:400 + MORE]
        tlow = R[0:EXPERTS, 440:440 + MORE]
        table = R[:, 480:480 + 3 * MORE]
        pairs = R[:, 560:561]
        gateT = R[0:EXPERTS, 576:576 + SEQ]
        xeT = [mt[:, 0:512], mt[:, 512:1024]]
        g_sb, u_sb, h_sb = mt[:, 1024:1536], mt[:, 1536:2048], mt[:, 2048:2560]
        hT = mt[:, 2560:3072]
        y_sb = mt[:, 3072:4096].rearrange("p (h n) -> p h n", h=2)
        GT = mt[:, 4608:4864]
        sel = [mt[:, 4096 + 128 * b:4224 + 128 * b].rearrange("p (t j) -> p t j", t=TT) for b in range(2)]
        selG = mt[:, 4352:4608].rearrange("p (t b j) -> p t b j", t=TT, b=2)
        onehot = [mt[:, 4864 + 64 * b:4928 + 64 * b] for b in range(2)]
        b_gu = mt[:, 4992:7040]
        y_out = xs

        bank = [ctx.enter_context(nc.psum_tensor(f"bank{i}", [P, HALF], F32)) for i in range(8)]
        y_acc = [[bank[0], bank[1]], [bank[2], bank[3]]]
        ps_gate, ps_up, ps_a, ps_b = bank[4], bank[5], bank[6], bank[7]

        jobs = [("gA", "dve", "gA")]
        jobs += [(f"xT{t}{g}", "dve", f"xT{t}{g}") for t in range(2) for g in range(2)]
        jobs += [(f"{n}{t}", "act", f"{n}{t}") for t in range(2) for n in ("pC", "pE")]
        jobs += [("gB", "dve", "gB"), ("pK0", "act", "pK0"), ("cT0", "dve", "cT0"), ("cT1", "dve", "cT1"), ("rel", "dve", "rel"),
                 ("pK1", "act", "pK1")]
        jobs += [(f"{n}0", "act", f"{n}0") for n in ("qba", "qbb", "kva", "kvb", "pQ")]
        jobs += [(f"band{g}", "act", f"band{g}") for g in range(4)]
        jobs += [(f"{n}1", "act", f"{n}1") for n in ("qba", "qbb", "kva", "kvb", "pQ")]
        jobs += [("pV0", "act", "pV0"), ("pV1", "act", "pV1")]
        for t in range(2):
            jobs += [(f"tnq{t}", "dve", f"tnq{t}"), (f"tnk{t}", "act", f"tnk{t}"),
                     (f"trq{t}", "act", f"trq{t}"), (f"trk{t}", "act", f"trk{t}"),
                     (f"taq{t}", "dve", f"taq{t}"), (f"tak{t}", "act", f"tak{t}")]
        heads_of = {"s0e": (0, [0, 2, 4, 6]), "s0o": (0, [1, 3, 5, 7]), "s0b": (0, [8, 9, 10, 11]),
                    "s1a": (1, [0, 2]), "s1b": (1, [1, 3]), "s1c": (1, [4, 6]), "s1d": (1, [5, 7]),
                    "s1e": (1, [8, 9]), "s1f": (1, [10, 11])}
        jobs += [(n, "dve", f"{n}{hs[-1]}") for n, (_, hs) in heads_of.items()]
        jobs += [(f"P0{g}", "dve", f"P0{g}") for g in range(3)]
        jobs += [("vA0", "dve", "vA0"), ("vB0", "dve", "vB0")]
        jobs += [(f"P1{g}", "dve" if g % 2 else "act", f"P1{g}") for g in range(6)]
        jobs += [("vA1", "dve", "vA1"), ("vB1", "dve", "vB1")]
        jobs += [(f"mT{t}{g}", "act", f"mT{t}{g}") for t in range(2) for g in range(2)]
        jobs += [(f"oP{t}{g}", "dve", f"oP{t}{g}") for t, g in ((0, 0), (1, 0), (0, 1))]
        jobs += [(f"hT{t}{g}", "dve", f"hT{t}{g}") for t, g in ((0, 0), (1, 0), (0, 1))]
        jobs += [("oP11", "dve", "oP11"), ("lg0", "dve", "lg0"), ("hT11", "dve", "hT11"), ("lg1", "dve", "lg1")]
        jobs += [("rank0", "dve", "posr0"), ("rank1", "dve", "posr1"), ("cnt", "dve", "cnt")]
        jobs += [("gather0", "", ""), ("cum", "dve", "cum"), ("table", "dve", "table"), ("gateT", "act", "gateT")]
        job_at = {n: i for i, (n, _, _) in enumerate(jobs)}

        pe_steps, dve_steps, act_steps, pool_steps = sem("pe_steps"), sem("dve_steps"), sem("act_steps"), sem("pool_steps")
        PE = Steps(pe_steps, [n for n, _, _ in jobs if n != "gather0"] + ["y_start"])
        ACTS = Steps(act_steps,
                     ["sqx0", "sqx1"]
                     + [f"{n}{t}" for t in range(2) for n in ("pC", "pE", "sqc", "sqc_b", "sqe")]
                     + ["pK0", "pK1"]
                     + [f"{n}0" for n in ("qba", "qbb", "kva", "kvb", "sqq", "sqk", "pQ", "sqa")]
                     + [f"band{g}" for g in range(4)]
                     + [f"{n}1" for n in ("qba", "qbb", "kva", "kvb", "sqq", "sqk", "pQ", "sqa")]
                     + ["pV0", "pV1"]
                     + [f"{n}{t}" for t in range(2) for n in ("tnk", "trq", "trk", "tak")]
                     + [f"e{t}{h}" for t in range(2) for h in range(12)]
                     + [f"P1{g}" for g in range(0, 6, 2)]
                     + [f"mT{t}{g}" for t in range(2) for g in range(2)]
                     + ["sq2_00", "sq2_10", "sq2_01", "hn0", "sq2_11", "hn1", "exp0", "exp1", "gateT"])
        DVE = Steps(dve_steps,
                    ["rx0", "gA", "xT00", "xT01", "rx1", "xT10", "xT11", "rc0", "rc1", "gB", "ga", "gb", "cT0", "cT1", "rel"]
                    + [f"{n}{t}" for t in range(2) for n in ("sumq", "rq", "sumk", "addk", "rk", "sumA", "rAq", "rAk", "nscale", "kpe", "kscale")]
                    + [f"{n}{t}" for t in range(2) for n in ("tnq", "taq")]
                    + [x for n, (t, hs) in heads_of.items() if t == 0 for x in [f"{n}{h}" for h in hs]] + ["max0"]
                    + [x for n, (t, hs) in heads_of.items() if t == 1 for x in [f"{n}{h}" for h in hs]] + ["max1"]
                    + ["rden0", "P00", "P01", "P02", "vA0", "vB0", "rden1", "P11", "P13", "P15", "vA1", "vB1"]
                    + ["oP00", "oP10", "oP01", "r20", "hT00", "hT10", "hT01", "oP11", "r21", "low", "low4", "first0", "lg0", "hT11"]
                    + [f"{n}0" for n in ("max8_", "top", "nm1_", "rep", "mask")] + ["lg1"]
                    + [f"{n}1" for n in ("max8_", "top", "nm1_", "rep", "mask")]
                    + ["posr0", "pos0", "posr1", "pos1", "sel00", "sel01", "cnt", "x1", "x2", "x3"]
                    + [f"{n}{t}" for t in range(2) for n in ("gm", "gden", "grd", "gate")]
                    + ["cum", "td", "tge", "tlt", "tA", "tR", "tE", "selG0", "selG1", "table", "pairsum", "turns",
                       "slots_e", "main_e", "first_m", "first"])
        POOL = Steps(pool_steps,
                     ["half", "px0", "px1", "pc0", "pc1"]
                     + [f"{n}{t}" for t in range(2) for n in ("gk", "kc", "ks1", "ks2", "kadd")]
                     + [f"{n}{t}" for t in range(2) for n in ("gq", "qc", "qs1", "qs2", "qadd", "pq", "pk", "pa")]
                     + ["zero_b", "zero_G", "onehot0", "p20", "p21"])

        ld = {n: sem("ld_" + n) for n in ("x0", "x1", "g_attn", "gains", "ident", "const", "wC", "wK", "wQ", "wV", "lora", "rel", "small", "wout0", "wout1",
                                          "bias_a", "b_gu", "b_dn")}
        st_bias = sem("st_bias")
        st_out = sem("st_out")
        gu_loaded = [[sem(f"gu_loaded{b}{c}") for c in range(NCHUNK)] for b in range(2)]
        dn_loaded = [sem(f"dn_loaded{c}") for c in range(DCHUNK)]
        gu_used, dn_used = sem("gu_used"), sem("dn_used")
        select_steps, sel_ready = sem("select_steps"), sem("sel_ready")
        xet_done, xet_ready = sem("xet_done"), sem("xet_ready")
        gt_done, gt_ready = sem("gt_done"), sem("gt_ready")
        gate_ready, up_ready, upgate_ready = sem("gate_ready"), sem("up_ready"), sem("upgate_ready")
        sig_ready, h_ready = sem("sig_ready"), sem("h_ready")
        t_done, hT_ready = sem("t_done"), sem("hT_ready")
        y_ready, y_final, out_ready = sem("y_ready"), sem("y_final"), sem("out_ready")
        SEL_OPS = 3

        def fill(t, c):
            return t[:, c * (KD // NCHUNK):(c + 1) * (KD // NCHUNK), :]

        def gu_dram(e, c):
            rows = D // NCHUNK
            w = w_gate_up[e] if isinstance(e, int) else w_gate_up[bass.ds(e, 1)].rearrange("a d f -> (a d) f")
            return w[c * rows:(c + 1) * rows, :].rearrange("(k p) f -> p k f", p=P)

        def dn_dram(e, c):
            rows = FF // DCHUNK
            w = w_down[e] if isinstance(e, int) else w_down[bass.ds(e, 1)].rearrange("a d f -> (a d) f")
            return w[c * rows:(c + 1) * rows, :].rearrange("(k p) f -> p k f", p=P)

        def dn_fill(c):
            return DN[:, c * (KD // DCHUNK):(c + 1) * (KD // DCHUNK), :]

        block = ctx.enter_context(nc.Block())

        @block.sync
        def _(sp):
            w_rows = w_in[0].rearrange("(k p) n -> p k n", p=P)
            w_out_rows = w_out[0].rearrange("(k p) n -> p k n", p=P)
            sp.dma_start(xs[:, 0, :], x[0, 0:P, :]).then_inc(ld["x0"], 16)
            sp.dma_start(ca[:, 0:P], c_all[:, 0:P]).then_inc(ld["ident"], 16)
            sp.dma_start(xs[:, 1, :], x[0, P:SEQ, :]).then_inc(ld["x1"], 16)
            sp.dma_start(w_c, w_rows[:, :, C_COL:C_COL + 512]).then_inc(ld["wC"], 16)
            sp.dma_start(w_kpe, w_rows[:, :, KPE_COL:KPE_COL + ROPE]).then_inc(ld["wC"], 16)
            sp.dma_start(w_k, w_rows[:, :, 512:1024]).then_inc(ld["wK"], 16)
            sp.dma_start(ca[:, P:], c_all[:, P:]).then_inc(ld["const"], 16)
            sp.dma_start(wqb, w_q_b[0].rearrange("(k p) n -> p k n", p=P)).then_inc(ld["lora"], 16)
            sp.dma_start(wkvb, w_kv_b[0].rearrange("(k p) n -> p k n", p=P)).then_inc(ld["lora"], 16)
            sp.dma_start(w_q, w_rows[:, :, 0:512]).then_inc(ld["wQ"], 16)
            sp.dma_start(w_v, w_rows[:, :, 1024:1536]).then_inc(ld["wV"], 16)
            for g in range(2):
                sp.dma_start(w_out_sb[g], w_out_rows[:, :, g * HALF:(g + 1) * HALF]).then_inc(ld[f"wout{g}"], 16)
            for c, done in enumerate(("pE1", "pK1", "pQ1", "pV1")):
                sp.wait_ge(pe_steps, PE.at(done))
                sp.dma_start(fill(GU[0], c), gu_dram(0, c)).then_inc(gu_loaded[0][c], 16)
            sp.wait_ge(dve_steps, DVE.at("max1"))
            for c in range(NCHUNK):
                if c == 2:
                    sp.wait_ge(pe_steps, PE.at("vB1"))
                sp.dma_start(fill(GU[1], c), gu_dram(1, c)).then_inc(gu_loaded[1][c], 16)
            for c, done in enumerate(("oP10", "oP11")):
                sp.wait_ge(pe_steps, PE.at(done))
                sp.dma_start(dn_fill(c), dn_dram(0, c)).then_inc(dn_loaded[c], 16)
            for c in range(DCHUNK):
                sp.wait_ge(dn_used, c + 1)
                sp.dma_start(dn_fill(c), dn_dram(1, c)).then_inc(dn_loaded[c], 16)
            sp.wait_ge(dve_steps, DVE.at("main_e"))
            n_turns = sp.value_load(turns[0:1, 0:1], min_val=EXPERTS // 2, max_val=(EXPERTS + MAX_MORE) // 2)
            with sp.Fori(0, n_turns - 1) as i:
                for b in range(2):
                    e = sp.value_load(slot_e[0:1, bass.ds(i * 2 + (b + 2), 1)], min_val=0, max_val=EXPERTS - 1)
                    for c in range(NCHUNK):
                        sp.wait_ge(gu_used, i * (2 * NCHUNK) + (b * NCHUNK + c + 1))
                        sp.dma_start(fill(GU[b], c), gu_dram(e, c)).then_inc(gu_loaded[b][c], 16)
                    for c in range(DCHUNK):
                        sp.wait_ge(dn_used, i * (2 * DCHUNK) + ((b + 1) * DCHUNK + c + 1))
                        sp.dma_start(dn_fill(c), dn_dram(e, c)).then_inc(dn_loaded[c], 16)
            for t in range(TT):
                sp.wait_ge(out_ready, 2 * t + 2)
                sp.dma_start(out[0, t * P:(t + 1) * P, :], y_out[:, t, :]).then_inc(st_out, 16)
            sp.wait_ge(st_out, 32)

        @block.tensor
        def _(pe):
            def begin(name):
                n = job_at[name]
                if n >= 8:
                    _, engine, step = jobs[n - 8]
                    if engine == "dve":
                        pe.wait_ge(dve_steps, DVE.at(step))
                    else:
                        pe.wait_ge(act_steps, ACTS.at(step))
                return bank[n % 8]

            pe.wait_ge(ld["ident"], 16)
            pe.wait_ge(ld["g_attn"], 16)
            b = begin("gA")
            PE.done("gA", nc.tensor.transpose(b[:, 0:8], gr_a[:, :], ident[0:8, 0:8]))
            for t in range(TT):
                pe.wait_ge(ld[f"x{t}"], 16)
                for g in range(2):
                    b = begin(f"xT{t}{g}")
                    for j in range(4):
                        last = nc.tensor.transpose(b[:, j * P:(j + 1) * P], xs[:, t, (4 * g + j) * P:(4 * g + j + 1) * P], ident)
                    PE.done(f"xT{t}{g}", last)

            def project(name, t, w, n):
                b = begin(name)
                pe.wait_ge(dve_steps, DVE.at(f"xT{t}1"))
                for k in range(KD):
                    last = nc.tensor.matmul(b[:, 0:n], xT[:, k, t * P:(t + 1) * P], w[:, k, :], start=k == 0, stop=k == KD - 1)
                PE.done(name, last)

            def latent(t):
                pe.wait_ge(dve_steps, DVE.at(f"cT{t}"))
                for name, k0, w, n0, n in (("qba", 0, wqb, 0, 384), ("qbb", 0, wqb, 384, 384), ("kva", 2, wkvb, 0, 512), ("kvb", 2, wkvb, 512, 512)):
                    b = begin(f"{name}{t}")
                    for k in range(2):
                        last = nc.tensor.matmul(b[:, 0:n], cT[:, k0 + k, t * P:(t + 1) * P], w[:, k, n0:n0 + n], start=k == 0, stop=k == 1)
                    PE.done(f"{name}{t}", last)

            pe.wait_ge(ld["wC"], 32)
            for t in range(TT):
                project(f"pC{t}", t, w_c, 512)
                project(f"pE{t}", t, w_kpe, ROPE)
            pe.wait_ge(ld["gains"], 16 * GAIN_DMAS)
            b = begin("gB")
            PE.done("gB", nc.tensor.transpose(b[:, 0:16], gr[:, :], ident[0:16, 0:16]))
            pe.wait_ge(ld["wK"], 16)
            project("pK0", 0, w_k, 512)
            for t in range(TT):
                b = begin(f"cT{t}")
                pe.wait_ge(act_steps, ACTS.at(f"pC{t}"))
                for j in range(4):
                    last = nc.tensor.transpose(b[:, j * P:(j + 1) * P], pr[:, t, C_COL + j * P:C_COL + (j + 1) * P], ident)
                PE.done(f"cT{t}", last)
            b = begin("rel")
            pe.wait_ge(ld["rel"], 32)
            PE.done("rel", nc.tensor.matmul(b[0:A_HEADS, 0:384], rel_sb, rel_tab[:, 0:384], start=True, stop=True))
            project("pK1", 1, w_k, 512)
            pe.wait_ge(ld["lora"], 32)
            latent(0)
            pe.wait_ge(ld["wQ"], 16)
            project("pQ0", 0, w_q, 512)
            pe.wait_ge(ld["bias_a"], 16)
            pe.wait_ge(ld["const"], 16)
            for g in range(4):
                b = begin(f"band{g}")
                PE.done(f"band{g}", nc.tensor.matmul(b[:, :], flip, hankel[:, g * 512:(g + 1) * 512], start=True, stop=True))
            latent(1)
            project("pQ1", 1, w_q, 512)
            pe.wait_ge(ld["wV"], 16)
            project("pV0", 0, w_v, 512)
            project("pV1", 1, w_v, 512)

            def turn(name, blocks, rows=P):
                b = begin(name)
                for j, src in enumerate(blocks):
                    last = nc.tensor.transpose(b[0:rows, j * P:(j + 1) * P], src, ident)
                PE.done(name, last)

            for t in range(TT):
                pe.wait_ge(act_steps, ACTS.at(f"qbb{t}"))
                turn(f"tnq{t}", [qb[:, t, h, 0:NOPE] for h in range(B_HEADS)])
                pe.wait_ge(dve_steps, DVE.at(f"nscale{t}"))
                turn(f"tnk{t}", [kvb[:, t, h, 0:NOPE] for h in range(B_HEADS)])
                pe.wait_ge(pool_steps, POOL.at(f"qadd{t}"))
                turn(f"trq{t}", [sq[:, 1024 + t * 512:1024 + t * 512 + 256].rearrange("p (h r) -> p h r", h=4)[:, h, :] for h in range(4)], ROPE)
                pe.wait_ge(dve_steps, DVE.at(f"kscale{t}"))
                turn(f"trk{t}", [sq[:, 1280 + t * 512:1536 + t * 512].rearrange("p (h r) -> p h r", h=4)[:, h, :] for h in range(4)], ROPE)
                turn(f"taq{t}", [pr[:, t, j * P:(j + 1) * P] for j in range(4)])
                turn(f"tak{t}", [pr[:, t, 512 + j * P:512 + (j + 1) * P] for j in range(4)])

            for name, (t, heads) in heads_of.items():
                b = begin(name)
                nk = (t + 1) * P
                pe.wait_ge(act_steps, ACTS.at(f"tak{t}"))
                pe.wait_ge(dve_steps, DVE.at(f"taq{t}"))
                for j, h in enumerate(heads):
                    o = b[:, j * nk:(j + 1) * nk]
                    if h < A_HEADS:
                        r = slice(64 * (h % 2), 64 * (h % 2) + 64)
                        last = nc.tensor.matmul(o, qTa[r, h // 2, t * P:(t + 1) * P], kTa[r, h // 2, 0:nk], start=True, stop=True)
                    else:
                        g = h - A_HEADS
                        nc.tensor.matmul(o, qTn[:, g, t * P:(t + 1) * P], kTn[:, g, 0:nk], start=True, stop=False)
                        last = nc.tensor.matmul(o, qTr[:, g, t * P:(t + 1) * P], kTr[:, g, 0:nk], start=False, stop=True)
                PE.done(name, last)

            def value(h, key_tile):
                if h < A_HEADS:
                    return pr[:, key_tile, 1024 + h * A_DIM:1024 + (h + 1) * A_DIM]
                return kvb[:, key_tile, h - A_HEADS, NOPE:NOPE + V_DIM]

            for g in range(3):
                pe.wait_ge(act_steps, ACTS.at(f"e0{4 * g + 3}"))
                turn(f"P0{g}", [prob[0][:, 4 * g + j, :] for j in range(4)])
            for name, heads, w in (("vA0", range(8), A_DIM), ("vB0", range(8, 12), V_DIM)):
                b = begin(name)
                for j, h in enumerate(heads):
                    pe.wait_ge(dve_steps, DVE.at(f"P0{h // 4}"))
                    last = nc.tensor.matmul(b[:, j * w:(j + 1) * w], probT0[:, (h // 4) * 512 + (h % 4) * P:(h // 4) * 512 + (h % 4 + 1) * P],
                                            value(h, 0), start=True, stop=True)
                PE.done(name, last)
            for g in range(6):
                pe.wait_ge(act_steps, ACTS.at(f"e1{2 * g + 1}"))
                turn(f"P1{g}", [prob[1][:, 2 * g + j // 2, (j % 2) * P:(j % 2 + 1) * P] for j in range(4)])
            for name, heads, w in (("vA1", range(8), A_DIM), ("vB1", range(8, 12), V_DIM)):
                b = begin(name)
                for j, h in enumerate(heads):
                    g = h // 2
                    if g % 2:
                        pe.wait_ge(dve_steps, DVE.at(f"P1{g}"))
                    else:
                        pe.wait_ge(act_steps, ACTS.at(f"P1{g}"))
                    for kt in range(2):
                        o = (h % 2) * 256 + kt * P
                        last = nc.tensor.matmul(b[:, j * w:(j + 1) * w], probT1[g][:, o:o + P], value(h, kt), start=kt == 0, stop=kt == 1)
                PE.done(name, last)
            for t in range(TT):
                pe.wait_ge(dve_steps, DVE.at(f"vB{t}"))
                for g in range(2):
                    turn(f"mT{t}{g}", [mixed[:, t, (4 * g + j) * P:(4 * g + j + 1) * P] for j in range(4)])
            def out_project(t, g):
                pe.wait_ge(ld[f"wout{g}"], 16)
                pe.wait_ge(act_steps, ACTS.at(f"mT{t}1"))
                b = begin(f"oP{t}{g}")
                for k in range(KD):
                    last = nc.tensor.matmul(b[:, :], mixT[:, k, t * P:(t + 1) * P], w_out_sb[g][:, k, :], start=k == 0, stop=k == KD - 1)
                PE.done(f"oP{t}{g}", last)

            def turn_x(t, g):
                pe.wait_ge(dve_steps, DVE.at(f"oP{t}{g}"))
                turn(f"hT{t}{g}", [xs[:, t, (4 * g + j) * P:(4 * g + j + 1) * P] for j in range(4)])

            def logits(t):
                b = begin(f"lg{t}")
                pe.wait_ge(dve_steps, DVE.at(f"hT{t}1"))
                for k in range(KD):
                    last = nc.tensor.matmul(b[:, 0:EXPERTS], h2T[:, k, t * P:(t + 1) * P], w_router[:, k, :], start=k == 0, stop=k == KD - 1)
                PE.done(f"lg{t}", last)

            for t, g in ((0, 0), (1, 0), (0, 1)):
                out_project(t, g)
            for t, g in ((0, 0), (1, 0), (0, 1)):
                turn_x(t, g)
            out_project(1, 1)
            pe.wait_ge(ld["small"], 32)
            logits(0)
            turn_x(1, 1)
            logits(1)
            b = begin("rank0")
            pe.wait_ge(dve_steps, DVE.at("mask0"))
            PE.done("rank0", nc.tensor.matmul(b[:, 0:EXPERTS], before, mask[:, 0, :], start=True, stop=True))
            b = begin("rank1")
            pe.wait_ge(dve_steps, DVE.at("mask1"))
            nc.tensor.matmul(b[:, 0:EXPERTS], ones, mask[:, 0, :], start=True, stop=False)
            PE.done("rank1", nc.tensor.matmul(b[:, 0:EXPERTS], before, mask[:, 1, :], start=False, stop=True))
            b = begin("cnt")
            nc.tensor.matmul(b[0:EXPERTS, 0:1], mask[:, 0, :], ones[:, 0:1], start=True, stop=False)
            PE.done("cnt", nc.tensor.matmul(b[0:EXPERTS, 0:1], mask[:, 1, :], ones[:, 0:1], start=False, stop=True))

            def gather(b, ps):
                for k in range(KD):
                    for t in range(TT):
                        last = nc.tensor.matmul(ps[:, k * SLOT:(k + 1) * SLOT], hn[:, t, k * P:(k + 1) * P], sel[b][:, t, :],
                                                start=t == 0, stop=t == TT - 1)
                last.then_inc(xet_done, 1)

            def scatter(stop):
                for t in range(TT):
                    for h in range(2):
                        last = nc.tensor.matmul(y_acc[t][h][:, :], GT[:, t * P:(t + 1) * P], y_sb[:, h, :],
                                                start=False, stop=stop, skip_group_check=True)
                return last

            b = begin("gather0")
            pe.wait_ge(dve_steps, DVE.at("sel01"))
            pe.wait_ge(act_steps, ACTS.at("hn1"))
            gather(0, b)
            b = begin("cum")
            pe.wait_ge(dve_steps, DVE.at("x3"))
            PE.done("cum", nc.tensor.matmul(b[0:EXPERTS, 0:1], before[0:EXPERTS, 0:EXPERTS], extra[0:EXPERTS, :], start=True, stop=True))
            b = begin("table")
            pe.wait_ge(dve_steps, DVE.at("tE"))
            PE.done("table", nc.tensor.matmul(b[:, 0:3 * MORE], ones[0:EXPERTS, :], table_in, start=True, stop=True))
            b = begin("gateT")
            for t in range(TT):
                last = nc.tensor.transpose(b[0:EXPERTS, t * P:(t + 1) * P], gate[:, t, :], ident)
            PE.done("gateT", last)
            pe.wait_ge(dve_steps, DVE.at("turns"))
            pe.wait_ge(act_steps, ACTS.at("gateT"))
            pe.wait_ge(xet_ready, 1)
            pe.wait_ge(ld["b_dn"], 16)
            for t in range(TT):
                for h in range(2):
                    last = nc.tensor.matmul(y_acc[t][h][:, :], gateT[:, t * P:(t + 1) * P], b_dn[:, h * HALF:(h + 1) * HALF],
                                            start=True, stop=False, skip_group_check=True)
            PE.done("y_start", last)
            pe.wait_ge(pool_steps, POOL.at("onehot0"))
            pe.wait_ge(ld["b_gu"], 16)
            n_turns = pe.value_load(turns[0:1, 0:1], min_val=EXPERTS // 2, max_val=(EXPERTS + MAX_MORE) // 2)
            with pe.Fori(0, n_turns) as i:
                for b in range(2):
                    n = i * 2 + b
                    pe.wait_ge(xet_ready, n + 1)
                    for u, ps in enumerate((ps_gate, ps_up)):
                        for h in range(2):
                            nc.tensor.matmul(ps[64 * h:64 * h + 64, :], onehot[b], b_gu[:, u * FF + h * HALF:u * FF + (h + 1) * HALF],
                                             start=True, stop=False)
                    for c in range(NCHUNK):
                        pe.wait_ge(gu_loaded[b][c], (i + 1) * 16)
                        for k in range(c * KD // NCHUNK, (c + 1) * KD // NCHUNK):
                            for u, ps in enumerate((ps_gate, ps_up)):
                                for h in range(2):
                                    last = nc.tensor.matmul(ps[64 * h:64 * h + 64, :], xeT[b][:, k * SLOT:(k + 1) * SLOT],
                                                            GU[b][:, k, u * FF + h * HALF:u * FF + (h + 1) * HALF],
                                                            start=False, stop=k == KD - 1)
                        last.then_inc(gu_used, 1)
                        if c == 1 and b == 0:
                            pe.wait_ge(y_ready, n + 1)
                            scatter(False)
                        if c == 1 and b == 1:
                            for t in range(TT):
                                last = nc.tensor.transpose(ps_b[:, t * P:(t + 1) * P], selG[:, t].rearrange("p b j -> p (b j)"), ident)
                            last.then_inc(gt_done, 1)
                    pe.wait_ge(y_ready, n + 1)
                    pe.wait_ge(sel_ready, n + 1)
                    gather(1 - b, ps_a)
                    pe.wait_ge(h_ready, n + 1)
                    if b == 1:
                        pe.wait_ge(gt_ready, i + 1)
                    for c in range(4):
                        last = nc.tensor.transpose(ps_b[:, c * P:(c + 1) * P], h_sb[:, c * P:(c + 1) * P], ident)
                    last.then_inc(t_done, 1)
                    pe.wait_ge(hT_ready, n + 1)
                    pe.wait_ge(xet_ready, n + 2)
                    for c in range(DCHUNK):
                        pe.wait_ge(dn_loaded[c], (n + 1) * 16)
                        for k in range(c * KD // DCHUNK, (c + 1) * KD // DCHUNK):
                            o = (k % 4) * P + (k // 4) * SLOT
                            for h in range(2):
                                last = nc.tensor.matmul(ps_a[64 * h:64 * h + 64, :], hT[:, o:o + SLOT], DN[:, k, h * HALF:(h + 1) * HALF],
                                                        start=k == 0, stop=k == KD - 1)
                        last.then_inc(dn_used, 1)
            pe.wait_ge(y_ready, n_turns * 2 + 1)
            scatter(True).then_inc(y_final, 1)

        @block.scalar
        def _(act):
            def own(name):
                act.wait_ge(act_steps, ACTS.at(name))

            act.dma_start(gr_a[:, :], attn_norm_g[0].rearrange("(k p) -> k p", p=P)).then_inc(ld["g_attn"], 16)
            for at, g, n in ((0, ffn_norm_g, 8), (8, q_a_norm_g, 2), (10, kv_a_norm_g, 2)):
                act.dma_start(gr[at:at + n, :], g[0].rearrange("(k p) -> k p", p=P)).then_inc(ld["gains"], 16)
            for at, g in ((12, a_q_norm_g), (13, a_k_norm_g)):
                for h in range(2):
                    act.dma_start(gr[at:at + 1, h * A_DIM:(h + 1) * A_DIM], g[0:1, :]).then_inc(ld["gains"], 16)
            for at, g in ((14, b_q_norm_g), (15, b_k_norm_g)):
                act.dma_start(gr[at:at + 1, :], g[0:1, 0:NOPE]).then_inc(ld["gains"], 16)
            act.dma_start(gq_rope[:, :], b_q_norm_g[0:1, NOPE:QK_DIM].to_broadcast([P, ROPE])).then_inc(ld["gains"], 16)
            act.dma_start(gk_rope[:, :], b_k_norm_g[0:1, NOPE:QK_DIM].to_broadcast([P, ROPE])).then_inc(ld["gains"], 16)
            act.dma_start(rel_tab, c_rel[:, :]).then_inc(ld["rel"], 16)
            act.dma_start(rel_sb, rel_bias[:, :]).then_inc(ld["rel"], 16)
            act.dma_start(router_bias[:, :], router_b[0:1, :].to_broadcast([P, EXPERTS])).then_inc(ld["small"], 16)
            act.dma_start(w_router[:, :, :], router_w[0].rearrange("(k p) e -> p k e", p=P)).then_inc(ld["small"], 16)

            for t in range(TT):
                act.wait_ge(ld[f"x{t}"], 16)
                ACTS.done(f"sqx{t}", nc.scalar.activation(sq[:, 0:D], xs[:, t, :], ACT.Square, scale=float(D) ** -0.5, accum_out=r_x[:, t:t + 1]))
                own(f"sqx{t}")

            def scaled(name, o, n, r):
                act.wait_ge(pe_steps, PE.at(name))
                ACTS.done(name, nc.scalar.activation(o, bank[job_at[name] % 8][:, 0:n], ACT.Copy, scale=r))

            for t in range(TT):
                act.wait_ge(pool_steps, POOL.at(f"px{t}"))
                scaled(f"pC{t}", pr[:, t, C_COL:C_COL + 512], 512, r_x[:, t:t + 1])
                scaled(f"pE{t}", pr[:, t, KPE_COL:IN_W], ROPE, r_x[:, t:t + 1])
                own(f"pE{t}")
                for g, n in ((0, "sqc"), (1, "sqc_b")):
                    ACTS.done(f"{n}{t}", nc.scalar.activation(sq[:, 0:LORA], pr[:, t, C_COL + g * LORA:C_COL + (g + 1) * LORA], ACT.Square,
                                                              scale=float(LORA) ** -0.5, accum_out=r_c[:, t, g:g + 1]))
                    own(f"{n}{t}")
                ACTS.done(f"sqe{t}", nc.scalar.activation(sq[:, 0:ROPE], pr[:, t, KPE_COL:IN_W], ACT.Square, accum_out=s_kpe[:, t:t + 1]))
                own(f"sqe{t}")
            for t in range(TT):
                scaled(f"pK{t}", pr[:, t, 512:1024], 512, r_x[:, t:t + 1])
            act.wait_ge(dve_steps, DVE.at("rel"))
            act.dma_start(dram_bias[:, :], rel_rev).then_inc(st_bias, 16)
            for t in range(TT):
                act.wait_ge(pool_steps, POOL.at(f"pc{t}"))
                q_flat = qb[:, t].rearrange("p h n -> p (h n)")
                k_flat = kvb[:, t].rearrange("p h n -> p (h n)")
                scaled(f"qba{t}", q_flat[:, 0:384], 384, r_c[:, t, 0:1])
                if t == 0:
                    act.wait_ge(st_bias, 16)
                    act.dma_start(hankel.rearrange("p (h k) -> p h k", h=A_HEADS),
                                  bass.AP(dram_bias, 0, [[1, P], [384, A_HEADS], [1, SEQ]])).then_inc(ld["bias_a"], 16)
                scaled(f"qbb{t}", q_flat[:, 384:768], 384, r_c[:, t, 0:1])
                scaled(f"kva{t}", k_flat[:, 0:512], 512, r_c[:, t, 1:2])
                scaled(f"kvb{t}", k_flat[:, 512:1024], 512, r_c[:, t, 1:2])
                own(f"qbb{t}")
                if t:
                    act.wait_ge(dve_steps, DVE.at(f"sumk{t - 1}"))
                ACTS.done(f"sqq{t}", nc.scalar.activation(sqw[:, 0:768], q_flat, ACT.Square))
                own(f"kvb{t}")
                ACTS.done(f"sqk{t}", nc.scalar.activation(sqw[:, 768:1280].rearrange("p (h n) -> p h n", h=4), kvb[:, t, :, 0:NOPE], ACT.Square))
                scaled(f"pQ{t}", pr[:, t, 0:512], 512, r_x[:, t:t + 1])
                own(f"pQ{t}")
                if t:
                    act.wait_ge(dve_steps, DVE.at(f"sumA{t - 1}"))
                ACTS.done(f"sqa{t}", nc.scalar.activation(sq[:, 0:1024], pr[:, t, 0:1024], ACT.Square))
                if t == 0:
                    for g in range(4):
                        act.wait_ge(pe_steps, PE.at(f"band{g}"))
                        ACTS.done(f"band{g}", nc.scalar.activation(bias_a[:, 2 * g:2 * g + 2, :].rearrange("p h k -> p (h k)"),
                                                                   bank[job_at[f"band{g}"] % 8][:, :], ACT.Copy))
            for t in range(TT):
                scaled(f"pV{t}", pr[:, t, 1024:1536], 512, r_x[:, t:t + 1])

            def copied(name, o, i):
                act.wait_ge(pe_steps, PE.at(name))
                ACTS.done(name, nc.scalar.activation(o, i, ACT.Copy))

            def of(name, rows=P):
                return bank[job_at[name] % 8][0:rows, :].rearrange("p (h t) -> p h t", h=4)

            for t in range(TT):
                cols = slice(t * P, (t + 1) * P)
                copied(f"tnk{t}", kTn[:, :, cols], of(f"tnk{t}"))
                copied(f"trq{t}", qTr[:, :, cols], of(f"trq{t}", ROPE))
                copied(f"trk{t}", kTr[:, :, cols], of(f"trk{t}", ROPE))
                copied(f"tak{t}", kTa[:, :, cols], of(f"tak{t}"))
            for t in range(TT):
                act.wait_ge(dve_steps, DVE.at(f"max{t}"))
                for h in range(12):
                    ACTS.done(f"e{t}{h}", nc.scalar.activation(prob[t][:, h, :], prob[t][:, h, :], ACT.Exp, bias=n_max[:, t, h:h + 1],
                                                               accum_out=den[:, t, h:h + 1]))
            for g in range(0, 6, 2):
                copied(f"P1{g}", probT1[g], bank[job_at[f"P1{g}"] % 8][:, :])
            for t in range(TT):
                for g in range(2):
                    copied(f"mT{t}{g}", mixT[:, 4 * g:4 * g + 4, t * P:(t + 1) * P], of(f"mT{t}{g}"))
            act.wait_ge(pool_steps, POOL.at("zero_b"))
            act.dma_start(b_gu[0:EXPERTS, :], b_gate_up[0]).then_inc(ld["b_gu"], 16)
            act.dma_start(b_dn, b_down[0]).then_inc(ld["b_dn"], 16)

            def square(t, g):
                act.wait_ge(dve_steps, DVE.at(f"oP{t}{g}"))
                half = slice(g * HALF, (g + 1) * HALF)
                ACTS.done(f"sq2_{t}{g}", nc.scalar.activation(hn[:, t, half], xs[:, t, half], ACT.Square, scale=float(D) ** -0.5,
                                                              accum_out=ss_2[:, t, g:g + 1]))

            def normalise(t):
                own(f"sq2_{t}1")
                act.wait_ge(pool_steps, POOL.at(f"p2{t}"))
                ACTS.done(f"hn{t}", nc.scalar.activation(hn[:, t, :], xs[:, t, :], ACT.Copy, scale=r_2[:, t:t + 1]))

            for t, g in ((0, 0), (1, 0), (0, 1)):
                square(t, g)
            normalise(0)
            square(1, 1)
            normalise(1)
            for t in range(TT):
                act.wait_ge(dve_steps, DVE.at(f"nm1_{t}"))
                ACTS.done(f"exp{t}", nc.scalar.activation(ex[:, t, :], lg[:, t, 0:EXPERTS], ACT.Exp, bias=n_m1[:, t:t + 1]))
            copied("gateT", gateT, bank[job_at["gateT"] % 8][0:EXPERTS, 0:SEQ])
            act.wait_ge(dve_steps, DVE.at("turns"))
            n_turns = act.value_load(turns[0:1, 0:1], min_val=EXPERTS // 2, max_val=(EXPERTS + MAX_MORE) // 2)
            with act.Fori(0, n_turns) as i:
                for b in range(2):
                    n = i * 2 + b
                    if b == 1:
                        act.wait_ge(gt_done, i + 1)
                        nc.scalar.activation(GT, ps_b[:, 0:SEQ], ACT.Copy).then_inc(gt_ready, 1)
                    act.wait_ge(gate_ready, n + 1)
                    nc.scalar.activation(h_sb, g_sb, ACT.Sigmoid, scale=ALPHA).then_inc(sig_ready, 1)
                    act.wait_ge(t_done, n + 1)
                    nc.scalar.activation(hT, ps_b[:, :], ACT.Copy).then_inc(hT_ready, 1)
                    act.wait_ge(dn_used, (n + 1) * DCHUNK)
                    for h in range(2):
                        last = nc.scalar.activation(y_sb[64 * b:64 * b + 64, h, :], ps_a[64 * h:64 * h + 64, :], ACT.Copy)
                    last.then_inc(y_ready, 1)

        @block.vector
        def _(dve):
            V = nc.vector

            def own(name):
                dve.wait_ge(dve_steps, DVE.at(name))

            def ps(name, rows=P):
                dve.wait_ge(pe_steps, PE.at(name))
                return bank[job_at[name] % 8][0:rows, :]

            def mean(name, r, add, times):
                DVE.done(name, V.tensor_scalar(r, r, add, times, ALU.add, ALU.mult))

            def with_gain(name, o, at, n=4):
                src = ps(name)[:, 0:512].rearrange("p (k t) -> p k t", k=4)
                g = gains[:, at:at + 4].unsqueeze(2).to_broadcast([P, 4, P])
                DVE.done(name, V.tensor_tensor(o, src, g, ALU.mult))

            for t in range(TT):
                dve.wait_ge(act_steps, ACTS.at(f"sqx{t}"))
                mean(f"rx{t}", r_x[:, t:t + 1], EPS, 1.0)
                if t == 0:
                    DVE.done("gA", V.tensor_copy(gains[:, 0:8], ps("gA")[:, 0:8]))
                    own("gA")
                for g in range(2):
                    with_gain(f"xT{t}{g}", xT[:, 4 * g:4 * g + 4, t * P:(t + 1) * P], 4 * g)
            for t in range(TT):
                dve.wait_ge(act_steps, ACTS.at(f"sqc_b{t}"))
                mean(f"rc{t}", r_c[:, t, :], EPS, 1.0)
            DVE.done("gB", V.tensor_copy(gains[:, 8:24], ps("gB")[:, 0:16]))
            own("gB")
            DVE.done("ga", V.tensor_tensor(gain_a, gains[:, 20:21], gains[:, 21:22], ALU.mult))
            DVE.done("gb", V.tensor_tensor(gain_b, gains[:, 22:23], gains[:, 23:24], ALU.mult))
            for t in range(TT):
                with_gain(f"cT{t}", cT[:, :, t * P:(t + 1) * P], 16)
            DVE.done("rel", V.tensor_tensor(rel_rev, ps("rel", A_HEADS)[:, 0:384], rel_tab[0:A_HEADS, 384:768], ALU.add))

            for t in range(TT):
                dve.wait_ge(act_steps, ACTS.at(f"sqk{t}"))
                DVE.done(f"sumq{t}", V.tensor_reduce(r_q[:, t, :], sqw[:, 0:768].rearrange("p (h n) -> p h n", h=4), AX, ALU.add))
                own(f"sumq{t}")
                mean(f"rq{t}", r_q[:, t, :], QK_DIM * EPS, 1.0)
                DVE.done(f"sumk{t}", V.tensor_reduce(r_k[:, t, :], sqw[:, 768:1280].rearrange("p (h n) -> p h n", h=4), AX, ALU.add))
                own(f"sumk{t}")
                DVE.done(f"addk{t}", V.tensor_scalar(r_k[:, t, :], r_k[:, t, :], s_kpe[:, t:t + 1], 1.0 / QK_DIM, ALU.add, ALU.mult))
                own(f"addk{t}")
                mean(f"rk{t}", r_k[:, t, :], EPS, 1.0)
                dve.wait_ge(act_steps, ACTS.at(f"sqa{t}"))
                DVE.done(f"sumA{t}", V.tensor_reduce(r_a[:, t, :], sq[:, 0:1024].rearrange("p (h n) -> p h n", h=16), AX, ALU.add))
                own(f"sumA{t}")
                mean(f"rAq{t}", r_a[:, t, 0:8], A_DIM * EPS, 1.0)
                mean(f"rAk{t}", r_a[:, t, 8:16], A_DIM * EPS, 1.0 / A_DIM)
                kn = kvb[:, t, :, 0:NOPE]
                dve.wait_ge(pool_steps, POOL.at(f"pk{t}"))
                DVE.done(f"nscale{t}", V.tensor_tensor(kn, kn, r_k[:, t, :].unsqueeze(2).to_broadcast([P, 4, NOPE]), ALU.mult))
                dve.wait_ge(pool_steps, POOL.at(f"kadd{t}"))
                kr = sq[:, 1280 + t * 512:1536 + t * 512].rearrange("p (h r) -> p h r", h=4)
                DVE.done(f"kpe{t}", V.tensor_tensor(kr, k_rot[:, t, :].unsqueeze(1).to_broadcast([P, 4, ROPE]),
                                                    r_k[:, t, :].unsqueeze(2).to_broadcast([P, 4, ROPE]), ALU.mult))
                kk = pr[:, t, 512:1024].rearrange("p (h n) -> p h n", h=8)
                dve.wait_ge(pool_steps, POOL.at(f"pa{t}"))
                DVE.done(f"kscale{t}", V.tensor_tensor(kk, kk, r_a[:, t, 8:16].unsqueeze(2).to_broadcast([P, 8, A_DIM]), ALU.mult))
            for t in range(TT):
                cols = slice(t * P, (t + 1) * P)
                DVE.done(f"tnq{t}", V.tensor_scalar(qTn[:, :, cols], ps(f"tnq{t}").rearrange("p (h t) -> p h t", h=4), gain_b, None, ALU.mult))
                DVE.done(f"taq{t}", V.tensor_scalar(qTa[:, :, cols], ps(f"taq{t}").rearrange("p (h t) -> p h t", h=4), gain_a, None, ALU.mult))
            for t in range(TT):
                nk = (t + 1) * P
                for name, (tt, heads) in heads_of.items():
                    if tt != t:
                        continue
                    src = ps(name)
                    for j, h in enumerate(heads):
                        r = r_a[:, t, h:h + 1] if h < 8 else r_q[:, t, h - 8:h - 7]
                        add = bias_a[:, h, SEQ - nk:SEQ] if h < 8 else causal[:, SEQ - nk:SEQ]
                        dve.wait_ge(act_steps, ACTS.at("band3"))
                        DVE.done(f"{name}{h}", V.scalar_tensor_tensor(prob[t][:, h, :], src[:, j * nk:(j + 1) * nk], r, add, ALU.mult, ALU.add))
                own(("s0b", "s1f")[t] + "11")
                DVE.done(f"max{t}", V.tensor_reduce(n_max[:, t, :], prob[t], AX, ALU.max, negate=True))

            def copied(name, o):
                DVE.done(name, V.tensor_copy(o, ps(name)))

            def outputs(t):
                for name, h0, nh, w, c0 in ((f"vA{t}", 0, 8, A_DIM, 0), (f"vB{t}", 8, 4, V_DIM, A_WIDTH)):
                    DVE.done(name, V.tensor_tensor(mixed[:, t, c0:c0 + 512].rearrange("p (h n) -> p h n", h=nh),
                                                   ps(name).rearrange("p (h n) -> p h n", h=nh),
                                                   den[:, t, h0:h0 + nh].unsqueeze(2).to_broadcast([P, nh, w]), ALU.mult))

            dve.wait_ge(act_steps, ACTS.at("e011"))
            DVE.done("rden0", V.reciprocal(den[:, 0, :], den[:, 0, :]))
            for g in range(3):
                copied(f"P0{g}", probT0[:, g * 512:(g + 1) * 512])
            own("rden0")
            outputs(0)
            dve.wait_ge(act_steps, ACTS.at("e111"))
            DVE.done("rden1", V.reciprocal(den[:, 1, :], den[:, 1, :]))
            for g in range(1, 6, 2):
                copied(f"P1{g}", probT1[g])
            own("rden1")
            outputs(1)
            def residual(t, g):
                part = xs[:, t, g * HALF:(g + 1) * HALF]
                DVE.done(f"oP{t}{g}", V.tensor_tensor(part, ps(f"oP{t}{g}"), part, ALU.add))

            def mean2(t):
                dve.wait_ge(act_steps, ACTS.at(f"sq2_{t}1"))
                DVE.done(f"r2{t}", V.tensor_scalar(r_2[:, t:t + 1], ss_2[:, t, 0:1], ss_2[:, t, 1:2], EPS, ALU.add, ALU.add))

            def h2(t, g):
                with_gain(f"hT{t}{g}", h2T[:, 4 * g:4 * g + 4, t * P:(t + 1) * P], 8 + 4 * g)

            def logits(t):
                src = ps(f"lg{t}")
                dve.wait_ge(pool_steps, POOL.at(f"p2{t}"))
                DVE.done(f"lg{t}", V.scalar_tensor_tensor(lg[:, t, 0:EXPERTS], src[:, 0:EXPERTS], r_2[:, t:t + 1], router_bias[:, :],
                                                          ALU.mult, ALU.add))

            def choose(t):
                own(f"lg{t}")
                DVE.done(f"max8_{t}", V.max(m8[:, t, :], lg[:, t, 0:EXPERTS]))
                own(f"max8_{t}")
                DVE.done(f"top{t}", V.tensor_copy(top4[:, t, 0:TOP_K], m8[:, t, 0:TOP_K]))
                DVE.done(f"nm1_{t}", V.tensor_scalar(n_m1[:, t:t + 1], m8[:, t, 0:1], -1.0, None, ALU.mult))
                own(f"top{t}")
                DVE.done(f"rep{t}", V.match_replace(rep[:, t, 0:36], top4[:, t, :], lg[:, t, 0:36], -LOW))
                own(f"rep{t}")
                DVE.done(f"mask{t}", V.tensor_tensor(mask[:, t, :], rep[:, t, 0:EXPERTS], lg[:, t, 0:EXPERTS], ALU.not_equal))

            ffn_gain = gains[:, 8:16].unsqueeze(2).to_broadcast([P, KD, SLOT])

            def take_tokens(b, ps):
                V.tensor_tensor(xeT[b].rearrange("p (k j) -> p k j", k=KD), ps[:, :].rearrange("p (k j) -> p k j", k=KD),
                                ffn_gain, ALU.mult).then_inc(xet_ready, 1)

            residual(0, 0)
            residual(1, 0)
            residual(0, 1)
            mean2(0)
            h2(0, 0)
            h2(1, 0)
            h2(0, 1)
            residual(1, 1)
            mean2(1)
            DVE.done("low", V.memset(lg[:, :, EXPERTS:EXPERTS + 4], LOW))
            DVE.done("low4", V.memset(top4[:, :, TOP_K:8], LOW))
            DVE.done("first0", V.memset(slot_first[:, 0:EXPERTS], 0.0))
            logits(0)
            h2(1, 1)
            choose(0)
            logits(1)
            choose(1)
            for t in range(TT):
                src = ps(f"rank{t}")
                DVE.done(f"posr{t}", V.scalar_tensor_tensor(pos[:, t, :], src[:, 0:EXPERTS], 1.0, mask[:, t, :], ALU.add, ALU.mult))
                own(f"posr{t}")
                DVE.done(f"pos{t}", V.tensor_scalar(pos[:, t, :], pos[:, t, :], -1.0, None, ALU.add))
            own("pos1")
            for t in range(TT):
                DVE.done(f"sel0{t}", V.tensor_scalar(sel[0][:, t, :], iota, pos[:, t, 0:1], None, ALU.is_equal))
            E = EXPERTS
            DVE.done("cnt", V.tensor_copy(cnt[0:E], ps("cnt", E)[:, 0:1]))
            own("cnt")
            DVE.done("x1", V.tensor_scalar(extra[0:E], cnt[0:E], float(SLOT), None, ALU.is_gt))
            own("x1")
            DVE.done("x2", V.scalar_tensor_tensor(extra[0:E], cnt[0:E], 2.0 * SLOT, extra[0:E], ALU.is_gt, ALU.add))
            own("x2")
            DVE.done("x3", V.scalar_tensor_tensor(extra[0:E], cnt[0:E], 3.0 * SLOT, extra[0:E], ALU.is_gt, ALU.add))
            dve.wait_ge(xet_done, 1)
            take_tokens(0, bank[job_at["gather0"] % 8])
            for t in range(TT):
                dve.wait_ge(act_steps, ACTS.at(f"exp{t}"))
                DVE.done(f"gm{t}", V.tensor_tensor(ex[:, t, :], ex[:, t, :], mask[:, t, :], ALU.mult))
                own(f"gm{t}")
                DVE.done(f"gden{t}", V.tensor_reduce(g_den[:, t:t + 1], ex[:, t, :], AX, ALU.add))
                own(f"gden{t}")
                DVE.done(f"grd{t}", V.reciprocal(g_den[:, t:t + 1], g_den[:, t:t + 1]))
                own(f"grd{t}")
                DVE.done(f"gate{t}", V.tensor_scalar(gate[:, t, :], ex[:, t, :], g_den[:, t:t + 1], None, ALU.mult))
            DVE.done("cum", V.tensor_copy(cum[0:E], ps("cum", E)[:, 0:1]))
            own("cum")
            DVE.done("td", V.tensor_scalar(tdist, iota[0:E, 0:MORE], cum[0:E], None, ALU.subtract))
            own("td")
            DVE.done("tge", V.tensor_scalar(tlow, tdist, 0.0, None, ALU.is_ge))
            DVE.done("tlt", V.tensor_scalar(table_in[:, 0:MORE], tdist, extra[0:E], None, ALU.is_lt))
            own("tlt")
            DVE.done("tA", V.tensor_tensor(table_in[:, 0:MORE], table_in[:, 0:MORE], tlow, ALU.mult))
            own("tA")
            DVE.done("tR", V.scalar_tensor_tensor(table_in[:, MORE:2 * MORE], tdist, 1.0, table_in[:, 0:MORE], ALU.add, ALU.mult))
            DVE.done("tE", V.tensor_scalar(table_in[:, 2 * MORE:3 * MORE], table_in[:, 0:MORE], row_id[0:E], None, ALU.mult))
            for t in range(TT):
                DVE.done(f"selG{t}", V.tensor_scalar(selG[:, t, 0, :], iota, pos[:, t, 0:1], gate[:, t, 0:1], ALU.is_equal, ALU.mult))
            DVE.done("table", V.tensor_copy(table, ps("table")[:, 0:3 * MORE]))
            own("table")
            DVE.done("pairsum", V.tensor_reduce(pairs[0:1], table[0:1, 0:MORE].rearrange("p (s two) -> p two s", two=2)[:, 0, :], AX, ALU.add))
            own("pairsum")
            DVE.done("turns", V.tensor_scalar(turns[0:1, 0:1], pairs[0:1], float(EXPERTS // 2), None, ALU.add))
            DVE.done("slots_e", V.tensor_copy(slot_e[0:1, EXPERTS:SLOTS], table[0:1, 2 * MORE:3 * MORE]))
            DVE.done("main_e", V.tensor_copy(slot_e[0:1, 0:EXPERTS], expert_id[0:1, :]))
            DVE.done("first_m", V.tensor_scalar(slot_first[:, EXPERTS:SLOTS], table[:, 0:MORE], -8.0 * SLOT, 8.0 * SLOT, ALU.mult, ALU.add))
            own("first_m")
            DVE.done("first", V.scalar_tensor_tensor(slot_first[:, EXPERTS:SLOTS], table[:, MORE:2 * MORE], float(SLOT), slot_first[:, EXPERTS:SLOTS], ALU.mult, ALU.add))

            def select(b, steps, pair_read=None):
                dve.wait_ge(select_steps, steps)
                if pair_read is not None:
                    dve.wait_ge(gt_done, pair_read)
                for t in range(TT):
                    V.tensor_scalar(sel[b][:, t, :], iota, rel_pos[b][:, t:t + 1], None, ALU.is_equal)
                    last = V.tensor_scalar(selG[:, t, b, :], iota, rel_pos[b][:, t:t + 1], slot_gate[b][:, t:t + 1],
                                           ALU.is_equal, ALU.mult)
                last.then_inc(sel_ready, 1)

            n_turns = dve.value_load(turns[0:1, 0:1], min_val=EXPERTS // 2, max_val=(EXPERTS + MAX_MORE) // 2)
            with dve.Fori(0, n_turns) as i:
                for b in range(2):
                    n = i * 2 + b
                    select(1 - b, (n + 1) * SEL_OPS, pair_read=i + 1 if b == 1 else None)
                    dve.wait_ge(gu_used, (n + 1) * NCHUNK)
                    V.tensor_scalar(g_sb, ps_gate[:, :], LIMIT, None, ALU.min).then_inc(gate_ready, 1)
                    V.tensor_scalar(u_sb, ps_up[:, :], LIMIT, -LIMIT, ALU.min, ALU.max).then_inc(up_ready, 1)
                    dve.wait_ge(gate_ready, n + 1)
                    dve.wait_ge(up_ready, n + 1)
                    V.scalar_tensor_tensor(u_sb, u_sb, 1.0, g_sb, ALU.add, ALU.mult).then_inc(upgate_ready, 1)
                    dve.wait_ge(upgate_ready, n + 1)
                    dve.wait_ge(sig_ready, n + 1)
                    V.tensor_tensor(h_sb, h_sb, u_sb, ALU.mult).then_inc(h_ready, 1)
                    dve.wait_ge(xet_done, n + 2)
                    take_tokens(1 - b, ps_a)
            dve.wait_ge(y_final, 1)
            for t in range(TT):
                for h in range(2):
                    V.tensor_tensor(y_out[:, t, h * HALF:(h + 1) * HALF], y_acc[t][h][:, :], xs[:, t, h * HALF:(h + 1) * HALF],
                                    ALU.add).then_inc(out_ready, 1)

        @block.gpsimd
        def _(pool):
            G = nc.gpsimd

            def own(name):
                pool.wait_ge(pool_steps, POOL.at(name))

            def rotate(kind, t, o, scratch, cos, sin):
                POOL.done(f"{kind}c{t}", G.tensor_tensor(scratch[0], o, cos, ALU.mult))
                POOL.done(f"{kind}s1{t}", G.tensor_tensor(scratch[1][..., 0:32], o[..., 32:64], sin[..., 0:32], ALU.mult))
                POOL.done(f"{kind}s2{t}", G.tensor_tensor(scratch[1][..., 32:64], o[..., 0:32], sin[..., 32:64], ALU.mult))
                own(f"{kind}s2{t}")
                return G.tensor_tensor(o, scratch[0], scratch[1], ALU.add)

            def root(name, r, n, made):
                pool.wait_ge(dve_steps, DVE.at(made))
                POOL.done(name, G.tensor_tensor(r, r, minus_half[:, :].to_broadcast([P, n]), ALU.pow))

            POOL.done("half", G.memset(minus_half[:, :], -0.5))
            own("half")
            for t in range(TT):
                root(f"px{t}", r_x[:, t:t + 1], 1, f"rx{t}")
            for t in range(TT):
                root(f"pc{t}", r_c[:, t, :], 2, f"rc{t}")
            pool.wait_ge(ld["const"], 16)
            pool.wait_ge(ld["gains"], 16 * GAIN_DMAS)
            for t in range(TT):
                k = k_rot[:, t, :]
                pool.wait_ge(act_steps, ACTS.at(f"pE{t}"))
                POOL.done(f"gk{t}", G.tensor_tensor(k, pr[:, t, KPE_COL:IN_W], gk_rope[:, :], ALU.mult))
                own(f"gk{t}")
                last = rotate("k", t, k, (rs0[:, 0, :], rs1[:, 0, :]), cos2[:, t, :], sin2[:, t, :])
                POOL.done(f"kadd{t}", last)
                own(f"kadd{t}")
            for t in range(TT):
                q = sq[:, 1024 + t * 512:1280 + t * 512].rearrange("p (h r) -> p h r", h=4)
                pool.wait_ge(act_steps, ACTS.at(f"qbb{t}"))
                POOL.done(f"gq{t}", G.tensor_tensor(q, qb[:, t, :, NOPE:QK_DIM], gq_rope[:, :].unsqueeze(1).to_broadcast([P, 4, ROPE]), ALU.mult))
                own(f"gq{t}")
                last = rotate("q", t, q, (rs0[:, :, :], rs1[:, :, :]), cos2[:, t, :].unsqueeze(1).to_broadcast([P, 4, ROPE]),
                              sin2[:, t, :].unsqueeze(1).to_broadcast([P, 4, ROPE]))
                POOL.done(f"qadd{t}", last)
                own(f"qadd{t}")
                root(f"pq{t}", r_q[:, t, :], 4, f"rq{t}")
                root(f"pk{t}", r_k[:, t, :], 4, f"rk{t}")
                root(f"pa{t}", r_a[:, t, :], 16, f"rAk{t}")
            pool.wait_ge(pe_steps, PE.at("mT11"))
            POOL.done("zero_b", G.memset(b_gu, 0.0))
            POOL.done("zero_G", G.memset(GT, 0.0))
            POOL.done("onehot0", G.tensor_copy(onehot[0], ident[:, 0:1].to_broadcast([P, SLOT])))
            for t in range(TT):
                root(f"p2{t}", r_2[:, t:t + 1], 1, f"r2{t}")
            pool.wait_ge(pe_steps, PE.at("lg1"))
            G.memset(y_sb, 0.0).then_inc(y_ready, 1)

            def select(b, n):
                e = pool.value_load(slot_e[0:1, bass.ds(n, 1)], min_val=0, max_val=EXPERTS - 1)
                first = slot_first[:, bass.ds(n, 1)]
                G.tensor_tensor(rel_pos[b].unsqueeze(2), pos[:, :, bass.ds(e, 1)], first.unsqueeze(1).to_broadcast([P, TT, 1]),
                                ALU.subtract).then_inc(select_steps, 1)
                G.tensor_copy(slot_gate[b].unsqueeze(2), gate[:, :, bass.ds(e, 1)]).then_inc(select_steps, 1)
                G.tensor_copy(onehot[b], ident[:, bass.ds(e, 1)].to_broadcast([P, SLOT])).then_inc(select_steps, 1)

            pool.wait_ge(dve_steps, DVE.at("first"))
            n_turns = pool.value_load(turns[0:1, 0:1], min_val=EXPERTS // 2, max_val=(EXPERTS + MAX_MORE) // 2)
            with pool.Fori(0, n_turns) as i:
                for b in range(2):
                    pool.wait_ge(xet_done, i * 2 + b + 1)
                    select(1 - b, i * 2 + b + 1)


_INS = ['x', 'attn_norm_g', 'w_in', 'a_q_norm_g', 'a_k_norm_g', 'rel_bias', 'q_a_norm_g', 'w_q_b', 'kv_a_norm_g', 'w_kv_b',
        'b_q_norm_g', 'b_k_norm_g', 'w_out', 'ffn_norm_g', 'router_w', 'router_b', 'w_gate_up', 'b_gate_up', 'w_down', 'b_down']


def kernel(**inputs):
    import numpy as _np
    import concourse.bacc as _bacc
    from concourse import mybir as _mybir
    from concourse.bass_utils import run_bass_kernel_spmd as _run

    nc = _bacc.Bacc("TRN2", target_bir_lowering=False, num_devices=1, dynamic_dma_scratch_size=1024)
    c_all, c_rel = constants()
    arrays, args = {}, []
    for name, a in [(n, inputs[n]) for n in _INS] + [("c_all", c_all), ("c_rel", c_rel)]:
        a = _np.ascontiguousarray(a)
        arrays[f"in_{name}_dram"] = a
        args.append(nc.dram_tensor(f"in_{name}_dram", a.shape, _mybir.dt.from_np(a.dtype), kind="ExternalInput").ap())
    args.append(nc.dram_tensor("out_0_dram", (1, SEQ, D), _mybir.dt.float32, kind="ExternalOutput").ap())
    for i, name in enumerate(_INS):
        if name in ("w_gate_up", "w_down"):
            args[i] = args[i][0]
    layer_kernel(nc, *args)
    r = _run(nc, [arrays], core_ids=[0])
    return r.results[0]["out_0_dram"]
```

```python
from contextlib import ExitStack

import numpy as np

import concourse.bass as bass
from concourse import mybir

F32 = mybir.dt.float32
I32 = mybir.dt.int32
ALU = mybir.AluOpType
ACT = mybir.ActivationFunctionType
AX = mybir.AxisListType.X

P = 128
SEQ, D = 256, 1024
TT = SEQ // P
KD = D // P
HALF = 512
A_HEADS, A_DIM, A_WIDTH = 8, 64, 512
B_HEADS, NOPE, ROPE, V_DIM = 4, 128, 64, 128
QK_DIM = NOPE + ROPE
LORA = 256
C_COL = 3 * A_WIDTH
KPE_COL = C_COL + 2 * LORA
IN_W = KPE_COL + ROPE
EXPERTS, TOP_K, FF = 32, 4, 1024
LIMIT, ALPHA = 7.0, 1.702
EPS = 1e-6
BUCKETS, MAX_DIST = 32, 2048
NEG = -1e30
LOW = -3e38
SLOT = 64
MAX_MORE = 16
MORE = MAX_MORE + 2
SLOTS = EXPERTS + MORE
GAIN_DMAS = 9
NCHUNK, DCHUNK = 8, 4


def constants():
    eye = np.eye(P, dtype=np.float32)
    iota = np.tile(np.arange(64, dtype=np.float32), (P, 1))
    before = np.triu(np.ones((P, P), np.float32), 1)
    ones = np.ones((P, P), np.float32)
    q, k = np.arange(P)[:, None], np.arange(P)[None, :]
    causal = np.concatenate([np.zeros((P, P)), np.where(k <= q, 0.0, NEG)], 1).astype(np.float32)
    inv = (np.float32(10000.0) ** (-np.arange(0, ROPE, 2, dtype=np.float32) / np.float32(ROPE))).astype(np.float32)
    ang = np.arange(SEQ, dtype=np.float32)[:, None] * inv[None, :]
    cos, sin = np.cos(ang).astype(np.float32), np.sin(ang).astype(np.float32)
    cc = np.concatenate([cos, cos], 1).reshape(TT, P, ROPE).transpose(1, 0, 2).reshape(P, TT * ROPE)
    ss = np.concatenate([-sin, sin], 1).reshape(TT, P, ROPE).transpose(1, 0, 2).reshape(P, TT * ROPE)
    row = np.arange(P, dtype=np.float32)[:, None]
    slot_expert = np.tile(np.arange(EXPERTS, dtype=np.float32), (P, 1))
    c_all = np.concatenate([eye, iota, before, ones, causal, cc, ss, row, slot_expert], 1)
    d = 255 - np.arange(384)
    df = np.maximum(d, 1).astype(np.float32)
    half = BUCKETS // 2
    log_b = half + (np.log(df / half) / np.float32(np.log(MAX_DIST / half)) * half).astype(np.int32)
    bucket = np.where(d < half, np.maximum(d, 0), np.minimum(log_b, BUCKETS - 1))
    count = sum(((d >= 0) & (d <= w) & (d % r == 0)).astype(np.float32) for w, r in ((128, 1), (512, 4), (2048, 16)))
    onehot = (bucket[None, :] == np.arange(BUCKETS)[:, None]).astype(np.float32)
    lnc = np.where(count > 0, np.log(np.maximum(count, 1)), NEG).astype(np.float32)
    c_rel = np.concatenate([onehot, np.tile(lnc, (BUCKETS, 1))], 1)
    return np.ascontiguousarray(c_all, np.float32), np.ascontiguousarray(c_rel, np.float32)


C_ALL_W = P + 64 + P + P + 2 * P + TT * ROPE * 2 + 1 + EXPERTS


class Steps:

    def __init__(self, sem, names):
        self.sem, self.names, self.next = sem, list(names), 0
        assert len(set(self.names)) == len(self.names)

    def at(self, name):
        return self.names.index(name) + 1

    def done(self, name, instruction):
        assert self.names[self.next] == name, (self.names[self.next], name)
        self.next += 1
        instruction.then_inc(self.sem, 1)


def layer_kernel(nc, x, attn_norm_g, w_in, a_q_norm_g, a_k_norm_g, rel_bias, q_a_norm_g, w_q_b, kv_a_norm_g,
                 w_kv_b, b_q_norm_g, b_k_norm_g, w_out, ffn_norm_g, router_w, router_b, w_gate_up, b_gate_up,
                 w_down, b_down, c_all, c_rel, out):
    with ExitStack() as ctx:
        def sb(name, shape, dt=F32):
            return ctx.enter_context(nc.sbuf_tensor(name, shape, dt))

        def sem(name):
            return ctx.enter_context(nc.semaphore(name))

        ring = sb("ring", [P, 2 * KD * 2 * FF])
        dring = sb("dring", [P, KD * D])
        GU = [ring[:, b * KD * 2 * FF:(b + 1) * KD * 2 * FF].rearrange("p (k n) -> p k n", k=KD) for b in range(2)]
        DN = dring[:, :].rearrange("p (k n) -> p k n", k=KD)
        xs = sb("xs", [P, TT, D])
        hn = sb("hn", [P, TT, D])
        mt = sb("mt", [P, 7040])
        ca = sb("ca", [P, C_ALL_W])
        st = sb("st", [P, 256])
        rt = sb("rt", [P, 320])
        gains = sb("gains", [P, 24])
        gr_a = sb("gr_a", [8, P])
        gr = sb("gr", [16, P])
        gq_rope = sb("gq_rope", [P, ROPE])
        gk_rope = sb("gk_rope", [P, ROPE])
        router_bias = sb("router_bias", [P, EXPERTS])
        sqw = sb("sqw", [P, 1280])
        k_rot = sb("k_rot", [P, TT, ROPE])
        short = sb("short", [P, KD * ROPE + 2 * B_HEADS * ROPE])
        w_kpe = short[:, 0:512].rearrange("p (k n) -> p k n", k=KD)
        rs0 = short[:, 512:768].rearrange("p (h r) -> p h r", h=B_HEADS)
        rs1 = short[:, 768:1024].rearrange("p (h r) -> p h r", h=B_HEADS)
        y_sb = short[:, :].rearrange("p (h n) -> p h n", h=2)
        w_router = sb("w_router", [P, KD, EXPERTS])
        minus_half = sb("minus_half", [P, 1])
        slot_e = sb("slot_e", [1, SLOTS], I32)
        turns = sb("turns", [1, 2], I32)
        dram_bias = nc.dram_tensor("dram_bias", (A_HEADS, P, 384), F32)

        def cut(t, at, n):
            return t[:, at:at + n]

        c0 = 0
        ident = cut(ca, c0, P); c0 += P
        iota = cut(ca, c0, 64); c0 += 64
        before = cut(ca, c0, P); c0 += P
        ones = cut(ca, c0, P); c0 += P
        causal = cut(ca, c0, 2 * P); c0 += 2 * P
        cos2 = cut(ca, c0, TT * ROPE).rearrange("p (t r) -> p t r", t=TT); c0 += TT * ROPE
        sin2 = cut(ca, c0, TT * ROPE).rearrange("p (t r) -> p t r", t=TT); c0 += TT * ROPE
        row_id = cut(ca, c0, 1); c0 += 1
        expert_id = cut(ca, c0, EXPERTS); c0 += EXPERTS
        assert c0 == C_ALL_W

        GROUPS = 4
        GROUP = KD * 2 * FF // GROUPS

        def chunks_of(g, chunks=NCHUNK, groups=GROUPS):
            return range(g * chunks // groups, (g + 1) * chunks // groups)

        def group(t, g):
            return t[:, g * GROUP:(g + 1) * GROUP].rearrange("p (k n) -> p k n", k=KD)

        w_c, w_k, w_q, w_v = (group(ring, g) for g in range(4))
        w_out_sb = [group(dring, g) for g in range(2)]
        T = ring[:, KD * 2 * FF:]
        t0 = 0

        def tcut(n):
            nonlocal t0
            t0 += n
            return T[:, t0 - n:t0]

        qTa_at = t0
        qTa = tcut(4 * SEQ).rearrange("p (h t) -> p h t", h=4)
        kTa = tcut(4 * SEQ).rearrange("p (h t) -> p h t", h=4)
        qTn = tcut(4 * SEQ).rearrange("p (h t) -> p h t", h=4)
        kTn = tcut(4 * SEQ).rearrange("p (h t) -> p h t", h=4)
        qTr = tcut(4 * SEQ)[0:ROPE].rearrange("p (h t) -> p h t", h=4)
        kTr = tcut(4 * SEQ)[0:ROPE].rearrange("p (h t) -> p h t", h=4)
        bias_a = tcut(A_HEADS * SEQ).rearrange("p (h t) -> p h t", h=A_HEADS)
        assert t0 <= 2 * GROUP
        pr = tcut(TT * IN_W).rearrange("p (t n) -> p t n", t=TT)
        qb = tcut(TT * B_HEADS * QK_DIM).rearrange("p (t h n) -> p t h n", t=TT, h=B_HEADS)
        kvb = tcut(TT * B_HEADS * 256).rearrange("p (t h n) -> p t h n", t=TT, h=B_HEADS)
        assert t0 <= KD * 2 * FF
        rel_tab = T[0:BUCKETS, qTa_at:qTa_at + 768]
        rel_rev = T[0:A_HEADS, qTa_at + 768:qTa_at + 1152]
        rel_sb = T[0:BUCKETS, qTa_at + 1152:qTa_at + 1160]
        xT = mt[:, 0:2048].rearrange("p (k t) -> p k t", k=KD)
        wqb = mt[:, 2048:3584].rearrange("p (k n) -> p k n", k=2)
        wkvb = mt[:, 3584:5632].rearrange("p (k n) -> p k n", k=2)
        cT = mt[:, 5632:6656].rearrange("p (k t) -> p k t", k=4)
        prob = [mt[:, 2048:3584].rearrange("p (h k) -> p h k", h=12), mt[:, 3584:6656].rearrange("p (h k) -> p h k", h=12)]
        mixed = mt[:, 0:2048].rearrange("p (t n) -> p t n", t=TT)
        mixT = mt[:, 2048:4096].rearrange("p (k t) -> p k t", k=KD)
        h2T = mt[:, 0:2048].rearrange("p (k t) -> p k t", k=KD)
        sq = hn[:, :, :].rearrange("p t n -> p (t n)")
        probT0 = hn[:, :, :].rearrange("p t n -> p (t n)")
        probT1 = [pr[:, 0, 0:512], pr[:, 0, 512:1024], pr[:, 1, 0:512], pr[:, 1, 512:1024],
                  sq[:, 1536:2048], qb[:, 0].rearrange("p h n -> p (h n)")[:, 0:512]]
        s0 = 0

        def scut(n):
            nonlocal s0
            s0 += n
            return st[:, s0 - n:s0]

        r_x, r_2 = scut(TT), scut(TT)
        ss_2 = scut(2 * TT).rearrange("p (t g) -> p t g", t=TT)
        r_a = scut(TT * 16).rearrange("p (t n) -> p t n", t=TT)
        r_c = scut(TT * 2).rearrange("p (t n) -> p t n", t=TT)
        r_q = scut(TT * 4).rearrange("p (t n) -> p t n", t=TT)
        s_kpe = scut(TT)
        r_k = scut(TT * 4).rearrange("p (t n) -> p t n", t=TT)
        n_max = scut(TT * 12).rearrange("p (t n) -> p t n", t=TT)
        den = scut(TT * 12).rearrange("p (t n) -> p t n", t=TT)
        g_den = scut(TT)
        n_m1 = scut(TT)
        gain_a, gain_b = scut(1), scut(1)
        cnt, extra, cum = scut(1), scut(1), scut(1)
        assert s0 <= 256
        r0 = 0

        def rcut(n):
            nonlocal r0
            r0 += n
            return rt[:, r0 - n:r0]

        pos = rcut(TT * EXPERTS).rearrange("p (t e) -> p t e", t=TT)
        gate = rcut(TT * EXPERTS).rearrange("p (t e) -> p t e", t=TT)
        slot_first = rcut(SLOTS)
        rel_pos = [rcut(TT) for _ in range(2)]
        slot_gate = [rcut(TT) for _ in range(2)]
        R = sqw
        lg = R[:, 0:80].rearrange("p (t e) -> p t e", t=TT)
        rep = R[:, 80:160].rearrange("p (t e) -> p t e", t=TT)
        m8 = R[:, 160:176].rearrange("p (t e) -> p t e", t=TT)
        top4 = R[:, 176:192].rearrange("p (t e) -> p t e", t=TT)
        mask = R[:, 192:256].rearrange("p (t e) -> p t e", t=TT)
        ex = R[:, 256:320].rearrange("p (t e) -> p t e", t=TT)
        table_in = R[0:EXPERTS, 320:320 + 3 * MORE]
        tdist = R[0:EXPERTS, 400:400 + MORE]
        tlow = R[0:EXPERTS, 440:440 + MORE]
        table = R[:, 480:480 + 3 * MORE]
        pairs = R[:, 560:561]
        xeT = [mt[:, 0:512], mt[:, 512:1024]]
        g_sb, u_sb, h_sb = mt[:, 1024:1536], mt[:, 1536:2048], mt[:, 2048:2560]
        hT = mt[:, 2560:3072]
        GT = mt[:, 4608:4864]
        sel = [mt[:, 4096 + 128 * b:4224 + 128 * b].rearrange("p (t j) -> p t j", t=TT) for b in range(2)]
        selG = mt[:, 4352:4608].rearrange("p (t b j) -> p t b j", t=TT, b=2)
        onehot = [mt[:, 4864 + 64 * b:4928 + 64 * b] for b in range(2)]
        b_gu = mt[:, 4992:7040]
        y_out = xs

        bank = [ctx.enter_context(nc.psum_tensor(f"bank{i}", [P, HALF], F32)) for i in range(8)]
        ps_gate, ps_up, ps_a, ps_b = bank[0:4]
        y_banks = bank[4:8]
        y_acc = [y_banks[0:2], y_banks[2:4]]

        jobs = [("gA", "dve", "gA")]
        jobs += [(f"xT{t}{g}", "dve", f"xT{t}{g}") for t in range(2) for g in range(2)]
        jobs += [(f"{n}{t}", "act", f"{n}{t}") for t in range(2) for n in ("pC", "pE")]
        jobs += [("gB", "dve", "gB"), ("pK0", "act", "pK0"), ("cT0", "dve", "cT0"), ("cT1", "dve", "cT1"), ("rel", "dve", "rel"),
                 ("pK1", "act", "pK1")]
        jobs += [(f"{n}0", "act", f"{n}0") for n in ("qba", "qbb", "kva", "kvb", "pQ")]
        jobs += [(f"{n}1", "act", f"{n}1") for n in ("qba", "qbb", "kva", "kvb", "pQ")]
        jobs += [("pV0", "act", "pV0")]
        for t in range(2):
            jobs += [(f"tnq{t}", "dve", f"tnq{t}"), (f"tnk{t}", "act", f"tnk{t}"),
                     (f"trq{t}", "act", f"trq{t}"), (f"trk{t}", "act", f"trk{t}"),
                     (f"taq{t}", "dve", f"taq{t}"), (f"tak{t}", "act", f"tak{t}")]
        heads_of = {"s0e": (0, [0, 2, 4, 6]), "s0o": (0, [1, 3, 5, 7]), "s0b": (0, [8, 9, 10, 11]),
                    "s1a": (1, [0, 2]), "s1b": (1, [1, 3]), "s1c": (1, [4, 6]), "s1d": (1, [5, 7]),
                    "s1e": (1, [8, 9]), "s1f": (1, [10, 11])}
        jobs += [(n, "dve", f"{n}{hs[-1]}") for n, (_, hs) in heads_of.items()]
        jobs += [("pV1", "act", "pV1")]
        jobs += [(f"P0{g}", "dve", f"P0{g}") for g in range(3)]
        jobs += [("vA0", "dve", "vA0"), ("vB0", "dve", "vB0")]
        jobs += [(f"P1{g}", "dve" if g % 2 else "act", f"P1{g}") for g in range(6)]
        jobs += [("vA1", "dve", "vA1"), ("vB1", "dve", "vB1")]
        jobs += [(f"mT{t}{g}", "act", f"mT{t}{g}") for t in range(2) for g in range(2)]
        jobs += [(f"oP{t}{g}", "dve", f"oP{t}{g}") for t, g in ((0, 0), (1, 0), (0, 1))]
        jobs += [(f"hT{t}{g}", "dve", f"hT{t}{g}") for t, g in ((0, 0), (1, 0), (0, 1))]
        jobs += [("oP11", "dve", "oP11"), ("lg0", "dve", "lg0"), ("hT11", "dve", "hT11"), ("lg1", "dve", "lg1")]
        jobs += [("rank0", "dve", "posr0"), ("rank1", "dve", "posr1"), ("cnt", "dve", "cnt")]
        jobs += [("y_zero2", "", ""), ("y_zero3", "", "")]
        jobs += [("gather0", "", ""), ("cum", "dve", "cum"), ("table", "dve", "table"), ("gateT", "", "")]
        job_at = {n: i for i, (n, _, _) in enumerate(jobs)}
        assert bank[job_at["y_zero2"] % 8] is y_banks[2]

        pe_steps, dve_steps, act_steps, pool_steps = sem("pe_steps"), sem("dve_steps"), sem("act_steps"), sem("pool_steps")
        PE = Steps(pe_steps, [n for n, _, _ in jobs if n not in ("y_zero2", "y_zero3", "gather0")])
        ACTS = Steps(act_steps,
                     ["sqx0", "sqx1"]
                     + [f"{n}{t}" for t in range(2) for n in ("pC", "pE", "sqc", "sqc_b", "sqe")]
                     + ["pK0", "pK1"]
                     + [f"{n}0" for n in ("qba", "qbb", "kva", "kvb", "sqq", "sqk", "pQ", "sqa")]
                     + [f"{n}1" for n in ("qba", "qbb", "kva", "kvb", "sqq", "sqk", "pQ", "sqa")]
                     + ["pV0"]
                     + [f"{n}{t}" for t in range(2) for n in ("tnk", "trq", "trk", "tak")]
                     + [f"e{t}{h}" for t in range(2) for h in range(12)] + ["pV1"]
                     + [f"P1{g}" for g in range(0, 6, 2)]
                     + [f"mT{t}{g}" for t in range(2) for g in range(2)]
                     + ["sq2_00", "sq2_10", "sq2_01", "hn0", "sq2_11", "hn1", "exp0", "exp1"])
        DVE = Steps(dve_steps,
                    ["gA", "xT00", "xT01", "xT10", "xT11", "rx0", "rx1", "rc0", "rc1", "gB", "ga", "gb", "cT0", "cT1", "rel"]
                    + [f"{n}{t}" for t in range(2) for n in ("sumq", "rq", "sumk", "addk", "rk", "sumA", "rAq", "rAk", "nscale", "kpe", "kscale")]
                    + [f"{n}{t}" for t in range(2) for n in ("tnq", "taq")]
                    + [x for n, (t, hs) in heads_of.items() if t == 0 for x in [f"{n}{h}" for h in hs]] + ["max0"]
                    + [x for n, (t, hs) in heads_of.items() if t == 1 for x in [f"{n}{h}" for h in hs]] + ["max1"]
                    + ["rden0", "P00", "P01", "P02", "vA0", "vB0", "rden1", "P11", "P13", "P15", "vA1", "vB1"]
                    + ["oP00", "oP10", "oP01", "r20", "hT00", "hT10", "hT01", "oP11", "r21", "low", "low4", "first0", "lg0", "hT11"]
                    + [f"{n}0" for n in ("max8_", "top", "nm1_", "rep", "mask")] + ["lg1"]
                    + [f"{n}1" for n in ("max8_", "top", "nm1_", "rep", "mask")]
                    + ["posr0", "pos0", "posr1", "pos1", "sel00", "sel01", "cnt", "x1", "x2", "x3"]
                    + [f"{n}{t}" for t in range(2) for n in ("gm", "gden", "grd", "gate")]
                    + ["cum", "td", "tge", "tlt", "tA", "tR", "tE", "selG0", "selG1"] + [f"y_zero{n}" for n in range(4)]
                    + ["table", "pairsum", "turns_less", "turns",
                       "slots_e", "main_e", "first_m", "first"])
        POOL = Steps(pool_steps,
                     ["half", "px0", "px1", "pc0", "pc1"]
                     + [f"{n}{t}" for t in range(2) for n in ("gk", "kc", "ks1", "ks2", "kadd")]
                     + [f"{n}{t}" for t in range(2) for n in ("gq", "qc", "qs1", "qs2", "qadd", "pq", "pk", "pa")]
                     + ["zero_y", "zero_b", "zero_G", "onehot0", "p20", "p21"])

        ld = {n: sem("ld_" + n) for n in ("x0", "x1", "g_attn", "gains", "ident", "const", "wC0", "wC1", "wE", "wK0", "wK1", "wQ", "wV", "lora", "rel", "small", "wout0", "wout1",
                                          "bias_a", "b_gu", "b_dn")}
        st_bias = sem("st_bias")
        st_out = sem("st_out")
        gu_loaded = [[sem(f"gu_loaded{b}{c}") for c in range(NCHUNK)] for b in range(2)]
        dn_loaded = [sem(f"dn_loaded{c}") for c in range(DCHUNK)]
        gu_used, dn_used = sem("gu_used"), sem("dn_used")
        select_steps, sel_ready = sem("select_steps"), sem("sel_ready")
        xet_done, xet_ready = sem("xet_done"), sem("xet_ready")
        gt_done, gt_ready = sem("gt_done"), sem("gt_ready")
        gate_ready, up_ready, upgate_ready = sem("gate_ready"), sem("up_ready"), sem("upgate_ready")
        sig_ready, h_ready = sem("sig_ready"), sem("h_ready")
        t_done, hT_ready = sem("t_done"), sem("hT_ready")
        y_ready, y_final, out_ready = sem("y_ready"), sem("y_final"), sem("out_ready")
        SEL_OPS = 3

        def fill(t, c):
            return t[:, c * (KD // NCHUNK):(c + 1) * (KD // NCHUNK), :]

        def gu_dram(e, c):
            rows = D // NCHUNK
            w = w_gate_up[e] if isinstance(e, int) else w_gate_up[bass.ds(e, 1)].rearrange("a d f -> (a d) f")
            return w[c * rows:(c + 1) * rows, :].rearrange("(k p) f -> p k f", p=P)

        def dn_dram(e, c):
            rows = FF // DCHUNK
            w = w_down[e] if isinstance(e, int) else w_down[bass.ds(e, 1)].rearrange("a d f -> (a d) f")
            return w[c * rows:(c + 1) * rows, :].rearrange("(k p) f -> p k f", p=P)

        def dn_fill(c):
            return DN[:, c * (KD // DCHUNK):(c + 1) * (KD // DCHUNK), :]

        block = ctx.enter_context(nc.Block())

        @block.sync
        def _(sp):
            w_rows = w_in[0].rearrange("(k p) n -> p k n", p=P)
            w_out_rows = w_out[0].rearrange("(k p) n -> p k n", p=P)
            sp.dma_start(xs[:, 0, :], x[0, 0:P, :]).then_inc(ld["x0"], 16)
            sp.dma_start(ca[:, 0:P], c_all[:, 0:P]).then_inc(ld["ident"], 16)
            sp.dma_start(xs[:, 1, :], x[0, P:SEQ, :]).then_inc(ld["x1"], 16)
            for k in range(0, KD, KD // 2):
                sp.dma_start(w_c[:, k:k + KD // 2], w_rows[:, k:k + KD // 2, C_COL:C_COL + 512]).then_inc(ld[f"wC{2 * k // KD}"], 16)
            sp.dma_start(w_kpe, w_rows[:, :, KPE_COL:KPE_COL + ROPE]).then_inc(ld["wE"], 16)
            for k in range(0, KD, KD // 2):
                sp.dma_start(w_k[:, k:k + KD // 2], w_rows[:, k:k + KD // 2, 512:1024]).then_inc(ld[f"wK{2 * k // KD}"], 16)
            sp.dma_start(ca[:, P:], c_all[:, P:]).then_inc(ld["const"], 16)
            sp.dma_start(wqb, w_q_b[0].rearrange("(k p) n -> p k n", p=P)).then_inc(ld["lora"], 16)
            sp.dma_start(wkvb, w_kv_b[0].rearrange("(k p) n -> p k n", p=P)).then_inc(ld["lora"], 16)
            sp.dma_start(w_q, w_rows[:, :, 0:512]).then_inc(ld["wQ"], 16)
            sp.dma_start(w_v, w_rows[:, :, 1024:1536]).then_inc(ld["wV"], 16)
            sp.wait_ge(dve_steps, DVE.at("rel"))
            sp.dma_start(dram_bias[:, :, :], rel_rev.unsqueeze(1).to_broadcast([A_HEADS, P, 384])).then_inc(st_bias, 16)
            sp.dma_start(w_out_sb[0], w_out_rows[:, :, 0:HALF]).then_inc(ld["wout0"], 16)
            sp.wait_ge(st_bias, 16)
            sp.dma_start(bias_a, bass.AP(dram_bias, P - 1, [[384 - 1, P], [P * 384, A_HEADS], [1, SEQ]])).then_inc(ld["bias_a"], 16)
            sp.dma_start(w_out_sb[1], w_out_rows[:, :, HALF:D]).then_inc(ld["wout1"], 16)
            for g, done in enumerate(("pE1", "pK1", "pQ1")):
                sp.wait_ge(pe_steps, PE.at(done))
                for c in chunks_of(g):
                    sp.dma_start(fill(GU[0], c), gu_dram(0, c)).then_inc(gu_loaded[0][c], 16)
            for g in range(GROUPS):
                if g == 0:
                    sp.wait_ge(dve_steps, DVE.at("max1"))
                if g == 2:
                    sp.wait_ge(pe_steps, PE.at("pV1"))
                    for c in chunks_of(3):
                        sp.dma_start(fill(GU[0], c), gu_dram(0, c)).then_inc(gu_loaded[0][c], 16)
                    sp.wait_ge(pe_steps, PE.at("vB1"))
                for c in chunks_of(g):
                    sp.dma_start(fill(GU[1], c), gu_dram(1, c)).then_inc(gu_loaded[1][c], 16)
            for g in range(2):
                sp.wait_ge(pe_steps, PE.at(f"oP1{g}"))
                for c in chunks_of(g, DCHUNK, 2):
                    sp.dma_start(dn_fill(c), dn_dram(0, c)).then_inc(dn_loaded[c], 16)

            def expert(slot):
                if isinstance(slot, int):
                    return slot
                return sp.value_load(slot_e[0:1, bass.ds(slot, 1)], min_val=0, max_val=EXPERTS - 1)

            def fetch_gate_up(i, b, chunks=range(NCHUNK)):
                e = expert(i * 2 + (b + 2))
                for c in chunks:
                    sp.wait_ge(gu_used, i * (2 * NCHUNK) + (b * NCHUNK + c + 1))
                    sp.dma_start(fill(GU[b], c), gu_dram(e, c)).then_inc(gu_loaded[b][c], 16)

            def fetch_down(i, b):
                e = expert(i * 2 + (b + 1))
                for c in range(DCHUNK):
                    sp.wait_ge(dn_used, i * (2 * DCHUNK) + (b * DCHUNK + c + 1))
                    sp.dma_start(dn_fill(c), dn_dram(e, c)).then_inc(dn_loaded[c], 16)

            for b in range(2):
                fetch_gate_up(0, b)
                fetch_down(0, b)
            fetch_gate_up(1, 0)
            fetch_down(1, 0)
            fetch_gate_up(1, 1, range(0, NCHUNK // 2))
            fetch_down(1, 1)
            fetch_gate_up(1, 1, range(NCHUNK // 2, NCHUNK))
            sp.wait_ge(dve_steps, DVE.at("main_e"))
            more_turns = sp.value_load(turns[0:1, 1:2], min_val=EXPERTS // 2 - 1, max_val=(EXPERTS + MAX_MORE) // 2 - 1)
            with sp.Fori(2, more_turns) as i:
                for b in range(2):
                    fetch_gate_up(i, b, range(0, NCHUNK // 4))
                    fetch_down(i, b)
                    fetch_gate_up(i, b, range(NCHUNK // 4, NCHUNK))
            fetch_down(more_turns, 0)
            for t in range(TT):
                for h in range(2):
                    sp.wait_ge(out_ready, 2 * t + h + 1)
                    half = slice(h * HALF, (h + 1) * HALF)
                    sp.dma_start(out[0, t * P:(t + 1) * P, half], y_out[:, t, half]).then_inc(st_out, 16)
            sp.wait_ge(st_out, 16 * 2 * TT)

        @block.tensor
        def _(pe):
            def begin(name):
                n = job_at[name]
                if n >= 8:
                    _, engine, step = jobs[n - 8]
                    if engine == "dve":
                        pe.wait_ge(dve_steps, DVE.at(step))
                    else:
                        pe.wait_ge(act_steps, ACTS.at(step))
                return bank[n % 8]

            pe.wait_ge(ld["ident"], 16)
            pe.wait_ge(ld["g_attn"], 16)
            b = begin("gA")
            PE.done("gA", nc.tensor.transpose(b[:, 0:8], gr_a[:, :], ident[0:8, 0:8]))
            for t in range(TT):
                pe.wait_ge(ld[f"x{t}"], 16)
                for g in range(2):
                    b = begin(f"xT{t}{g}")
                    for j in range(4):
                        last = nc.tensor.transpose(b[:, j * P:(j + 1) * P], xs[:, t, (4 * g + j) * P:(4 * g + j + 1) * P], ident)
                    PE.done(f"xT{t}{g}", last)

            def project(name, t, w, n, halves=None):
                b = begin(name)
                pe.wait_ge(dve_steps, DVE.at(f"xT{t}1"))
                for k in range(KD):
                    if halves and k % (KD // 2) == 0:
                        pe.wait_ge(ld[f"{halves}{2 * k // KD}"], 16)
                    last = nc.tensor.matmul(b[:, 0:n], xT[:, k, t * P:(t + 1) * P], w[:, k, :], start=k == 0, stop=k == KD - 1)
                PE.done(name, last)

            def latent(t):
                pe.wait_ge(dve_steps, DVE.at(f"cT{t}"))
                for name, k0, w, n0, n in (("qba", 0, wqb, 0, 384), ("qbb", 0, wqb, 384, 384), ("kva", 2, wkvb, 0, 512), ("kvb", 2, wkvb, 512, 512)):
                    b = begin(f"{name}{t}")
                    for k in range(2):
                        last = nc.tensor.matmul(b[:, 0:n], cT[:, k0 + k, t * P:(t + 1) * P], w[:, k, n0:n0 + n], start=k == 0, stop=k == 1)
                    PE.done(f"{name}{t}", last)

            for t in range(TT):
                project(f"pC{t}", t, w_c, 512, "wC")
                pe.wait_ge(ld["wE"], 16)
                project(f"pE{t}", t, w_kpe, ROPE)
            pe.wait_ge(ld["gains"], 16 * GAIN_DMAS)
            b = begin("gB")
            PE.done("gB", nc.tensor.transpose(b[:, 0:16], gr[:, :], ident[0:16, 0:16]))
            project("pK0", 0, w_k, 512, "wK")
            for t in range(TT):
                b = begin(f"cT{t}")
                pe.wait_ge(act_steps, ACTS.at(f"pC{t}"))
                for j in range(4):
                    last = nc.tensor.transpose(b[:, j * P:(j + 1) * P], pr[:, t, C_COL + j * P:C_COL + (j + 1) * P], ident)
                PE.done(f"cT{t}", last)
            b = begin("rel")
            pe.wait_ge(ld["rel"], 32)
            PE.done("rel", nc.tensor.matmul(b[0:A_HEADS, 0:384], rel_sb, rel_tab[:, 0:384], start=True, stop=True))
            project("pK1", 1, w_k, 512, "wK")
            pe.wait_ge(ld["lora"], 32)
            latent(0)
            pe.wait_ge(ld["wQ"], 16)
            project("pQ0", 0, w_q, 512)
            latent(1)
            project("pQ1", 1, w_q, 512)
            pe.wait_ge(ld["wV"], 16)
            project("pV0", 0, w_v, 512)

            def turn(name, blocks, rows=P):
                b = begin(name)
                for j, src in enumerate(blocks):
                    last = nc.tensor.transpose(b[0:rows, j * P:(j + 1) * P], src, ident)
                PE.done(name, last)

            for t in range(TT):
                pe.wait_ge(act_steps, ACTS.at(f"qbb{t}"))
                turn(f"tnq{t}", [qb[:, t, h, 0:NOPE] for h in range(B_HEADS)])
                pe.wait_ge(dve_steps, DVE.at(f"nscale{t}"))
                turn(f"tnk{t}", [kvb[:, t, h, 0:NOPE] for h in range(B_HEADS)])
                pe.wait_ge(pool_steps, POOL.at(f"qadd{t}"))
                turn(f"trq{t}", [sq[:, 1024 + t * 512:1024 + t * 512 + 256].rearrange("p (h r) -> p h r", h=4)[:, h, :] for h in range(4)], ROPE)
                pe.wait_ge(dve_steps, DVE.at(f"kscale{t}"))
                turn(f"trk{t}", [sq[:, 1280 + t * 512:1536 + t * 512].rearrange("p (h r) -> p h r", h=4)[:, h, :] for h in range(4)], ROPE)
                turn(f"taq{t}", [pr[:, t, j * P:(j + 1) * P] for j in range(4)])
                turn(f"tak{t}", [pr[:, t, 512 + j * P:512 + (j + 1) * P] for j in range(4)])

            for name, (t, heads) in heads_of.items():
                b = begin(name)
                nk = (t + 1) * P
                pe.wait_ge(act_steps, ACTS.at(f"tak{t}"))
                pe.wait_ge(dve_steps, DVE.at(f"taq{t}"))
                for j, h in enumerate(heads):
                    o = b[:, j * nk:(j + 1) * nk]
                    if h < A_HEADS:
                        r = slice(64 * (h % 2), 64 * (h % 2) + 64)
                        last = nc.tensor.matmul(o, qTa[r, h // 2, t * P:(t + 1) * P], kTa[r, h // 2, 0:nk], start=True, stop=True)
                    else:
                        g = h - A_HEADS
                        nc.tensor.matmul(o, qTn[:, g, t * P:(t + 1) * P], kTn[:, g, 0:nk], start=True, stop=False)
                        last = nc.tensor.matmul(o, qTr[:, g, t * P:(t + 1) * P], kTr[:, g, 0:nk], start=False, stop=True)
                PE.done(name, last)

            def value(h, key_tile):
                if h < A_HEADS:
                    return pr[:, key_tile, 1024 + h * A_DIM:1024 + (h + 1) * A_DIM]
                return kvb[:, key_tile, h - A_HEADS, NOPE:NOPE + V_DIM]

            project("pV1", 1, w_v, 512)
            for g in range(3):
                pe.wait_ge(act_steps, ACTS.at(f"e0{4 * g + 3}"))
                turn(f"P0{g}", [prob[0][:, 4 * g + j, :] for j in range(4)])
            for name, heads, w in (("vA0", range(8), A_DIM), ("vB0", range(8, 12), V_DIM)):
                b = begin(name)
                for j, h in enumerate(heads):
                    pe.wait_ge(dve_steps, DVE.at(f"P0{h // 4}"))
                    last = nc.tensor.matmul(b[:, j * w:(j + 1) * w], probT0[:, (h // 4) * 512 + (h % 4) * P:(h // 4) * 512 + (h % 4 + 1) * P],
                                            value(h, 0), start=True, stop=True)
                PE.done(name, last)
            for g in range(6):
                pe.wait_ge(act_steps, ACTS.at(f"e1{2 * g + 1}"))
                turn(f"P1{g}", [prob[1][:, 2 * g + j // 2, (j % 2) * P:(j % 2 + 1) * P] for j in range(4)])
            for name, heads, w in (("vA1", range(8), A_DIM), ("vB1", range(8, 12), V_DIM)):
                b = begin(name)
                for j, h in enumerate(heads):
                    g = h // 2
                    if g % 2:
                        pe.wait_ge(dve_steps, DVE.at(f"P1{g}"))
                    else:
                        pe.wait_ge(act_steps, ACTS.at(f"P1{g}"))
                    for kt in range(2):
                        o = (h % 2) * 256 + kt * P
                        last = nc.tensor.matmul(b[:, j * w:(j + 1) * w], probT1[g][:, o:o + P], value(h, kt), start=kt == 0, stop=kt == 1)
                PE.done(name, last)
            for t in range(TT):
                pe.wait_ge(dve_steps, DVE.at(f"vB{t}"))
                for g in range(2):
                    turn(f"mT{t}{g}", [mixed[:, t, (4 * g + j) * P:(4 * g + j + 1) * P] for j in range(4)])
            def out_project(t, g):
                pe.wait_ge(ld[f"wout{g}"], 16)
                pe.wait_ge(act_steps, ACTS.at(f"mT{t}1"))
                b = begin(f"oP{t}{g}")
                for k in range(KD):
                    last = nc.tensor.matmul(b[:, :], mixT[:, k, t * P:(t + 1) * P], w_out_sb[g][:, k, :], start=k == 0, stop=k == KD - 1)
                PE.done(f"oP{t}{g}", last)

            def turn_x(t, g):
                pe.wait_ge(dve_steps, DVE.at(f"oP{t}{g}"))
                turn(f"hT{t}{g}", [xs[:, t, (4 * g + j) * P:(4 * g + j + 1) * P] for j in range(4)])

            def logits(t):
                b = begin(f"lg{t}")
                for k in range(KD):
                    if k % 4 == 0:
                        pe.wait_ge(dve_steps, DVE.at(f"hT{t}{k // 4}"))
                    last = nc.tensor.matmul(b[:, 0:EXPERTS], h2T[:, k, t * P:(t + 1) * P], w_router[:, k, :], start=k == 0, stop=k == KD - 1)
                PE.done(f"lg{t}", last)

            for t, g in ((0, 0), (1, 0), (0, 1)):
                out_project(t, g)
            for t, g in ((0, 0), (1, 0), (0, 1)):
                turn_x(t, g)
            out_project(1, 1)
            pe.wait_ge(ld["small"], 32)
            logits(0)
            turn_x(1, 1)
            logits(1)
            b = begin("rank0")
            pe.wait_ge(dve_steps, DVE.at("mask0"))
            PE.done("rank0", nc.tensor.matmul(b[:, 0:EXPERTS], before, mask[:, 0, :], start=True, stop=True))
            b = begin("rank1")
            nc.tensor.matmul(b[:, 0:EXPERTS], ones, mask[:, 0, :], start=True, stop=False)
            pe.wait_ge(dve_steps, DVE.at("mask1"))
            PE.done("rank1", nc.tensor.matmul(b[:, 0:EXPERTS], before, mask[:, 1, :], start=False, stop=True))
            b = begin("cnt")
            nc.tensor.matmul(b[0:EXPERTS, 0:1], mask[:, 0, :], ones[:, 0:1], start=True, stop=False)
            PE.done("cnt", nc.tensor.matmul(b[0:EXPERTS, 0:1], mask[:, 1, :], ones[:, 0:1], start=False, stop=True))

            def gather(b, ps, blocks=range(KD)):
                for k in blocks:
                    for t in range(TT):
                        last = nc.tensor.matmul(ps[:, k * SLOT:(k + 1) * SLOT], hn[:, t, k * P:(k + 1) * P], sel[b][:, t, :],
                                                start=t == 0, stop=t == TT - 1)
                return last

            def scatter(stop):
                for t in range(TT):
                    for h in range(2):
                        last = nc.tensor.matmul(y_acc[t][h][:, :], GT[:, t * P:(t + 1) * P], y_sb[:, h, :],
                                                start=False, stop=stop, skip_group_check=True)
                        if stop:
                            last.then_inc(y_final, 1)

            slot0 = begin("gather0")
            pe.wait_ge(dve_steps, DVE.at("sel01"))
            pe.wait_ge(act_steps, ACTS.at("hn1"))
            gather(0, slot0, range(0, 2))
            b = begin("cum")
            pe.wait_ge(dve_steps, DVE.at("x3"))
            PE.done("cum", nc.tensor.matmul(b[0:EXPERTS, 0:1], before[0:EXPERTS, 0:EXPERTS], extra[0:EXPERTS, :], start=True, stop=True))
            gather(0, slot0, range(2, 5))
            b = begin("table")
            pe.wait_ge(dve_steps, DVE.at("tE"))
            PE.done("table", nc.tensor.matmul(b[:, 0:3 * MORE], ones[0:EXPERTS, :], table_in, start=True, stop=True))
            b = begin("gateT")
            for t in range(TT):
                last = nc.tensor.transpose(b[0:EXPERTS, t * P:(t + 1) * P], gate[:, t, :], ident)
            PE.done("gateT", last)
            gather(0, slot0, range(5, KD)).then_inc(xet_done, 1)
            pe.wait_ge(dve_steps, DVE.at("turns"))
            pe.wait_ge(ld["b_dn"], 16)
            pe.wait_ge(pool_steps, POOL.at("onehot0"))
            pe.wait_ge(ld["b_gu"], 16)
            n_turns = pe.value_load(turns[0:1, 0:1], min_val=EXPERTS // 2, max_val=(EXPERTS + MAX_MORE) // 2)
            with pe.Fori(0, n_turns) as i:
                for b in range(2):
                    n = i * 2 + b
                    pe.wait_ge(xet_ready, n + 1)
                    for c in range(NCHUNK):
                        pe.wait_ge(gu_loaded[b][c], (i + 1) * 16)
                        for k in range(c * KD // NCHUNK, (c + 1) * KD // NCHUNK):
                            for u, ps in enumerate((ps_gate, ps_up)):
                                for h in range(2):
                                    last = nc.tensor.matmul(ps[64 * h:64 * h + 64, :], xeT[b][:, k * SLOT:(k + 1) * SLOT],
                                                            GU[b][:, k, u * FF + h * HALF:u * FF + (h + 1) * HALF],
                                                            start=k == 0, stop=k == KD - 1)
                        last.then_inc(gu_used, 1)
                        if c == NCHUNK // 2 - 1:
                            for u, ps in enumerate((ps_gate, ps_up)):
                                for h in range(2):
                                    nc.tensor.matmul(ps[64 * h:64 * h + 64, :], onehot[b], b_gu[:, u * FF + h * HALF:u * FF + (h + 1) * HALF],
                                                     start=False, stop=False)
                        if c == NCHUNK // 2 - 1 and b == 0:
                            pe.wait_ge(y_ready, n + 1)
                            scatter(False)
                        if c == NCHUNK // 2 - 1 and b == 1:
                            for t in range(TT):
                                last = nc.tensor.transpose(ps_b[:, t * P:(t + 1) * P], selG[:, t].rearrange("p b j -> p (b j)"), ident)
                            last.then_inc(gt_done, 1)
                    pe.wait_ge(y_ready, n + 1)
                    pe.wait_ge(sel_ready, n + 1)
                    gather(1 - b, ps_a).then_inc(xet_done, 1)
                    pe.wait_ge(h_ready, n + 1)
                    if b == 1:
                        pe.wait_ge(gt_ready, i + 1)
                    for c in range(4):
                        last = nc.tensor.transpose(ps_b[:, c * P:(c + 1) * P], h_sb[:, c * P:(c + 1) * P], ident)
                    last.then_inc(t_done, 1)
                    pe.wait_ge(hT_ready, n + 1)
                    pe.wait_ge(xet_ready, n + 2)
                    for c in range(DCHUNK):
                        pe.wait_ge(dn_loaded[c], (n + 1) * 16)
                        for k in range(c * KD // DCHUNK, (c + 1) * KD // DCHUNK):
                            o = (k % 4) * P + (k // 4) * SLOT
                            for h in range(2):
                                last = nc.tensor.matmul(ps_a[64 * h:64 * h + 64, :], hT[:, o:o + SLOT], DN[:, k, h * HALF:(h + 1) * HALF],
                                                        start=k == 0, stop=k == KD - 1)
                        last.then_inc(dn_used, 1)
            pe.wait_ge(y_ready, n_turns * 2 + 1)
            scatter(True)

        @block.scalar
        def _(act):
            def own(name):
                act.wait_ge(act_steps, ACTS.at(name))

            act.dma_start(gr_a[:, :], attn_norm_g[0].rearrange("(k p) -> k p", p=P)).then_inc(ld["g_attn"], 16)
            for at, g, n in ((0, ffn_norm_g, 8), (8, q_a_norm_g, 2), (10, kv_a_norm_g, 2)):
                act.dma_start(gr[at:at + n, :], g[0].rearrange("(k p) -> k p", p=P)).then_inc(ld["gains"], 16)
            for at, g in ((12, a_q_norm_g), (13, a_k_norm_g)):
                act.dma_start(gr[at:at + 1, :].rearrange("p (h n) -> p h n", h=2),
                              g[0:1, :].unsqueeze(1).to_broadcast([1, 2, A_DIM])).then_inc(ld["gains"], 16)
            for at, g in ((14, b_q_norm_g), (15, b_k_norm_g)):
                act.dma_start(gr[at:at + 1, :], g[0:1, 0:NOPE]).then_inc(ld["gains"], 16)
            act.dma_start(gq_rope[:, :], b_q_norm_g[0:1, NOPE:QK_DIM].to_broadcast([P, ROPE])).then_inc(ld["gains"], 16)
            act.dma_start(gk_rope[:, :], b_k_norm_g[0:1, NOPE:QK_DIM].to_broadcast([P, ROPE])).then_inc(ld["gains"], 16)
            act.dma_start(rel_tab, c_rel[:, :]).then_inc(ld["rel"], 16)
            act.dma_start(rel_sb, rel_bias[:, :]).then_inc(ld["rel"], 16)
            act.dma_start(router_bias[:, :], router_b[0:1, :].to_broadcast([P, EXPERTS])).then_inc(ld["small"], 16)
            act.dma_start(w_router[:, :, :], router_w[0].rearrange("(k p) e -> p k e", p=P)).then_inc(ld["small"], 16)

            for t in range(TT):
                act.wait_ge(ld[f"x{t}"], 16)
                ACTS.done(f"sqx{t}", nc.scalar.activation(sq[:, 0:D], xs[:, t, :], ACT.Square, scale=float(D) ** -0.5, accum_out=r_x[:, t:t + 1]))
                own(f"sqx{t}")

            def scaled(name, o, n, r):
                act.wait_ge(pe_steps, PE.at(name))
                ACTS.done(name, nc.scalar.activation(o, bank[job_at[name] % 8][:, 0:n], ACT.Copy, scale=r))

            for t in range(TT):
                act.wait_ge(pool_steps, POOL.at(f"px{t}"))
                scaled(f"pC{t}", pr[:, t, C_COL:C_COL + 512], 512, r_x[:, t:t + 1])
                scaled(f"pE{t}", pr[:, t, KPE_COL:IN_W], ROPE, r_x[:, t:t + 1])
                own(f"pE{t}")
                for g, n in ((0, "sqc"), (1, "sqc_b")):
                    ACTS.done(f"{n}{t}", nc.scalar.activation(sq[:, 0:LORA], pr[:, t, C_COL + g * LORA:C_COL + (g + 1) * LORA], ACT.Square,
                                                              scale=float(LORA) ** -0.5, accum_out=r_c[:, t, g:g + 1]))
                    own(f"{n}{t}")
                ACTS.done(f"sqe{t}", nc.scalar.activation(sq[:, 0:ROPE], pr[:, t, KPE_COL:IN_W], ACT.Square, accum_out=s_kpe[:, t:t + 1]))
                own(f"sqe{t}")
            for t in range(TT):
                scaled(f"pK{t}", pr[:, t, 512:1024], 512, r_x[:, t:t + 1])
            for t in range(TT):
                act.wait_ge(pool_steps, POOL.at(f"pc{t}"))
                q_flat = qb[:, t].rearrange("p h n -> p (h n)")
                k_flat = kvb[:, t].rearrange("p h n -> p (h n)")
                scaled(f"qba{t}", q_flat[:, 0:384], 384, r_c[:, t, 0:1])
                scaled(f"qbb{t}", q_flat[:, 384:768], 384, r_c[:, t, 0:1])
                scaled(f"kva{t}", k_flat[:, 0:512], 512, r_c[:, t, 1:2])
                scaled(f"kvb{t}", k_flat[:, 512:1024], 512, r_c[:, t, 1:2])
                own(f"qbb{t}")
                if t:
                    act.wait_ge(dve_steps, DVE.at(f"sumk{t - 1}"))
                ACTS.done(f"sqq{t}", nc.scalar.activation(sqw[:, 0:768], q_flat, ACT.Square))
                own(f"kvb{t}")
                ACTS.done(f"sqk{t}", nc.scalar.activation(sqw[:, 768:1280].rearrange("p (h n) -> p h n", h=4), kvb[:, t, :, 0:NOPE], ACT.Square))
                scaled(f"pQ{t}", pr[:, t, 0:512], 512, r_x[:, t:t + 1])
                own(f"pQ{t}")
                if t:
                    act.wait_ge(dve_steps, DVE.at(f"sumA{t - 1}"))
                ACTS.done(f"sqa{t}", nc.scalar.activation(sq[:, 0:1024], pr[:, t, 0:1024], ACT.Square))
            scaled("pV0", pr[:, 0, 1024:1536], 512, r_x[:, 0:1])

            def copied(name, o, i):
                act.wait_ge(pe_steps, PE.at(name))
                ACTS.done(name, nc.scalar.activation(o, i, ACT.Copy))

            def of(name, rows=P):
                return bank[job_at[name] % 8][0:rows, :].rearrange("p (h t) -> p h t", h=4)

            act.wait_ge(ld["bias_a"], 16)
            for t in range(TT):
                cols = slice(t * P, (t + 1) * P)
                copied(f"tnk{t}", kTn[:, :, cols], of(f"tnk{t}"))
                copied(f"trq{t}", qTr[:, :, cols], of(f"trq{t}", ROPE))
                copied(f"trk{t}", kTr[:, :, cols], of(f"trk{t}", ROPE))
                copied(f"tak{t}", kTa[:, :, cols], of(f"tak{t}"))
            for t in range(TT):
                act.wait_ge(dve_steps, DVE.at(f"max{t}"))
                for h in range(12):
                    ACTS.done(f"e{t}{h}", nc.scalar.activation(prob[t][:, h, :], prob[t][:, h, :], ACT.Exp, bias=n_max[:, t, h:h + 1],
                                                               accum_out=den[:, t, h:h + 1]))
            scaled("pV1", pr[:, 1, 1024:1536], 512, r_x[:, 1:2])
            for g in range(0, 6, 2):
                copied(f"P1{g}", probT1[g], bank[job_at[f"P1{g}"] % 8][:, :])
            for t in range(TT):
                for g in range(2):
                    copied(f"mT{t}{g}", mixT[:, 4 * g:4 * g + 4, t * P:(t + 1) * P], of(f"mT{t}{g}"))
            act.wait_ge(pool_steps, POOL.at("zero_b"))
            act.dma_start(b_gu[0:EXPERTS, :], b_gate_up[0]).then_inc(ld["b_gu"], 16)
            act.dma_start(short[0:EXPERTS, :], b_down[0]).then_inc(ld["b_dn"], 16)

            def square(t, g):
                act.wait_ge(dve_steps, DVE.at(f"oP{t}{g}"))
                half = slice(g * HALF, (g + 1) * HALF)
                ACTS.done(f"sq2_{t}{g}", nc.scalar.activation(hn[:, t, half], xs[:, t, half], ACT.Square, scale=float(D) ** -0.5,
                                                              accum_out=ss_2[:, t, g:g + 1]))

            def normalise(t):
                own(f"sq2_{t}1")
                act.wait_ge(pool_steps, POOL.at(f"p2{t}"))
                ACTS.done(f"hn{t}", nc.scalar.activation(hn[:, t, :], xs[:, t, :], ACT.Copy, scale=r_2[:, t:t + 1]))

            for t, g in ((0, 0), (1, 0), (0, 1)):
                square(t, g)
            normalise(0)
            square(1, 1)
            normalise(1)
            for t in range(TT):
                act.wait_ge(dve_steps, DVE.at(f"nm1_{t}"))
                ACTS.done(f"exp{t}", nc.scalar.activation(ex[:, t, :], lg[:, t, 0:EXPERTS], ACT.Exp, bias=n_m1[:, t:t + 1]))
            act.wait_ge(pe_steps, PE.at("gateT"))
            nc.scalar.activation(GT[0:EXPERTS, :], bank[job_at["gateT"] % 8][0:EXPERTS, 0:SEQ], ACT.Copy).then_inc(y_ready, 1)
            act.wait_ge(dve_steps, DVE.at("turns"))
            n_turns = act.value_load(turns[0:1, 0:1], min_val=EXPERTS // 2, max_val=(EXPERTS + MAX_MORE) // 2)
            with act.Fori(0, n_turns) as i:
                for b in range(2):
                    n = i * 2 + b
                    if b == 1:
                        act.wait_ge(gt_done, i + 1)
                        nc.scalar.activation(GT, ps_b[:, 0:SEQ], ACT.Copy).then_inc(gt_ready, 1)
                    act.wait_ge(gate_ready, n + 1)
                    nc.scalar.activation(h_sb, g_sb, ACT.Sigmoid, scale=ALPHA).then_inc(sig_ready, 1)
                    act.wait_ge(t_done, n + 1)
                    nc.scalar.activation(hT, ps_b[:, :], ACT.Copy).then_inc(hT_ready, 1)
                    act.wait_ge(dn_used, (n + 1) * DCHUNK)
                    for h in range(2):
                        last = nc.scalar.activation(y_sb[64 * b:64 * b + 64, h, :], ps_a[64 * h:64 * h + 64, :], ACT.Copy)
                    last.then_inc(y_ready, 1)

        @block.vector
        def _(dve):
            V = nc.vector

            def own(name):
                dve.wait_ge(dve_steps, DVE.at(name))

            def ps(name, rows=P):
                dve.wait_ge(pe_steps, PE.at(name))
                return bank[job_at[name] % 8][0:rows, :]

            def mean(name, r, add, times):
                DVE.done(name, V.tensor_scalar(r, r, add, times, ALU.add, ALU.mult))

            def with_gain(name, o, at, n=4):
                src = ps(name)[:, 0:512].rearrange("p (k t) -> p k t", k=4)
                g = gains[:, at:at + 4].unsqueeze(2).to_broadcast([P, 4, P])
                DVE.done(name, V.tensor_tensor(o, src, g, ALU.mult))

            DVE.done("gA", V.tensor_copy(gains[:, 0:8], ps("gA")[:, 0:8]))
            own("gA")
            for t in range(TT):
                for g in range(2):
                    with_gain(f"xT{t}{g}", xT[:, 4 * g:4 * g + 4, t * P:(t + 1) * P], 4 * g)
            for t in range(TT):
                dve.wait_ge(act_steps, ACTS.at(f"sqx{t}"))
                mean(f"rx{t}", r_x[:, t:t + 1], EPS, 1.0)
            for t in range(TT):
                dve.wait_ge(act_steps, ACTS.at(f"sqc_b{t}"))
                mean(f"rc{t}", r_c[:, t, :], EPS, 1.0)
            DVE.done("gB", V.tensor_copy(gains[:, 8:24], ps("gB")[:, 0:16]))
            own("gB")
            DVE.done("ga", V.tensor_tensor(gain_a, gains[:, 20:21], gains[:, 21:22], ALU.mult))
            DVE.done("gb", V.tensor_tensor(gain_b, gains[:, 22:23], gains[:, 23:24], ALU.mult))
            for t in range(TT):
                with_gain(f"cT{t}", cT[:, :, t * P:(t + 1) * P], 16)
            DVE.done("rel", V.tensor_tensor(rel_rev, ps("rel", A_HEADS)[:, 0:384], rel_tab[0:A_HEADS, 384:768], ALU.add))

            for t in range(TT):
                dve.wait_ge(act_steps, ACTS.at(f"sqk{t}"))
                DVE.done(f"sumq{t}", V.tensor_reduce(r_q[:, t, :], sqw[:, 0:768].rearrange("p (h n) -> p h n", h=4), AX, ALU.add))
                own(f"sumq{t}")
                mean(f"rq{t}", r_q[:, t, :], QK_DIM * EPS, 1.0)
                DVE.done(f"sumk{t}", V.tensor_reduce(r_k[:, t, :], sqw[:, 768:1280].rearrange("p (h n) -> p h n", h=4), AX, ALU.add))
                own(f"sumk{t}")
                DVE.done(f"addk{t}", V.tensor_scalar(r_k[:, t, :], r_k[:, t, :], s_kpe[:, t:t + 1], 1.0 / QK_DIM, ALU.add, ALU.mult))
                own(f"addk{t}")
                mean(f"rk{t}", r_k[:, t, :], EPS, 1.0)
                dve.wait_ge(act_steps, ACTS.at(f"sqa{t}"))
                DVE.done(f"sumA{t}", V.tensor_reduce(r_a[:, t, :], sq[:, 0:1024].rearrange("p (h n) -> p h n", h=16), AX, ALU.add))
                own(f"sumA{t}")
                mean(f"rAq{t}", r_a[:, t, 0:8], A_DIM * EPS, 1.0)
                mean(f"rAk{t}", r_a[:, t, 8:16], A_DIM * EPS, 1.0 / A_DIM)
                kn = kvb[:, t, :, 0:NOPE]
                dve.wait_ge(pool_steps, POOL.at(f"pk{t}"))
                DVE.done(f"nscale{t}", V.tensor_tensor(kn, kn, r_k[:, t, :].unsqueeze(2).to_broadcast([P, 4, NOPE]), ALU.mult))
                dve.wait_ge(pool_steps, POOL.at(f"kadd{t}"))
                kr = sq[:, 1280 + t * 512:1536 + t * 512].rearrange("p (h r) -> p h r", h=4)
                DVE.done(f"kpe{t}", V.tensor_tensor(kr, k_rot[:, t, :].unsqueeze(1).to_broadcast([P, 4, ROPE]),
                                                    r_k[:, t, :].unsqueeze(2).to_broadcast([P, 4, ROPE]), ALU.mult))
                kk = pr[:, t, 512:1024].rearrange("p (h n) -> p h n", h=8)
                dve.wait_ge(pool_steps, POOL.at(f"pa{t}"))
                DVE.done(f"kscale{t}", V.tensor_tensor(kk, kk, r_a[:, t, 8:16].unsqueeze(2).to_broadcast([P, 8, A_DIM]), ALU.mult))
            dve.wait_ge(ld["bias_a"], 16)
            for t in range(TT):
                cols = slice(t * P, (t + 1) * P)
                DVE.done(f"tnq{t}", V.tensor_scalar(qTn[:, :, cols], ps(f"tnq{t}").rearrange("p (h t) -> p h t", h=4), gain_b, None, ALU.mult))
                DVE.done(f"taq{t}", V.tensor_scalar(qTa[:, :, cols], ps(f"taq{t}").rearrange("p (h t) -> p h t", h=4), gain_a, None, ALU.mult))
            dve.wait_ge(ld["const"], 16)
            for t in range(TT):
                nk = (t + 1) * P
                for name, (tt, heads) in heads_of.items():
                    if tt != t:
                        continue
                    src = ps(name)
                    for j, h in enumerate(heads):
                        r = r_a[:, t, h:h + 1] if h < 8 else r_q[:, t, h - 8:h - 7]
                        add = bias_a[:, h, SEQ - nk:SEQ] if h < 8 else causal[:, SEQ - nk:SEQ]
                        DVE.done(f"{name}{h}", V.scalar_tensor_tensor(prob[t][:, h, :], src[:, j * nk:(j + 1) * nk], r, add, ALU.mult, ALU.add))
                own(("s0b", "s1f")[t] + "11")
                DVE.done(f"max{t}", V.tensor_reduce(n_max[:, t, :], prob[t], AX, ALU.max, negate=True))

            def copied(name, o):
                DVE.done(name, V.tensor_copy(o, ps(name)))

            def outputs(t):
                for name, h0, nh, w, c0 in ((f"vA{t}", 0, 8, A_DIM, 0), (f"vB{t}", 8, 4, V_DIM, A_WIDTH)):
                    DVE.done(name, V.tensor_tensor(mixed[:, t, c0:c0 + 512].rearrange("p (h n) -> p h n", h=nh),
                                                   ps(name).rearrange("p (h n) -> p h n", h=nh),
                                                   den[:, t, h0:h0 + nh].unsqueeze(2).to_broadcast([P, nh, w]), ALU.mult))

            dve.wait_ge(act_steps, ACTS.at("e011"))
            DVE.done("rden0", V.reciprocal(den[:, 0, :], den[:, 0, :]))
            for g in range(3):
                copied(f"P0{g}", probT0[:, g * 512:(g + 1) * 512])
            own("rden0")
            outputs(0)
            dve.wait_ge(act_steps, ACTS.at("e111"))
            DVE.done("rden1", V.reciprocal(den[:, 1, :], den[:, 1, :]))
            for g in range(1, 6, 2):
                copied(f"P1{g}", probT1[g])
            own("rden1")
            outputs(1)
            def residual(t, g):
                part = xs[:, t, g * HALF:(g + 1) * HALF]
                DVE.done(f"oP{t}{g}", V.tensor_tensor(part, ps(f"oP{t}{g}"), part, ALU.add))

            def mean2(t):
                dve.wait_ge(act_steps, ACTS.at(f"sq2_{t}1"))
                DVE.done(f"r2{t}", V.tensor_scalar(r_2[:, t:t + 1], ss_2[:, t, 0:1], ss_2[:, t, 1:2], EPS, ALU.add, ALU.add))

            def h2(t, g):
                with_gain(f"hT{t}{g}", h2T[:, 4 * g:4 * g + 4, t * P:(t + 1) * P], 8 + 4 * g)

            def logits(t):
                src = ps(f"lg{t}")
                dve.wait_ge(pool_steps, POOL.at(f"p2{t}"))
                DVE.done(f"lg{t}", V.scalar_tensor_tensor(lg[:, t, 0:EXPERTS], src[:, 0:EXPERTS], r_2[:, t:t + 1], router_bias[:, :],
                                                          ALU.mult, ALU.add))

            def choose(t):
                own(f"lg{t}")
                DVE.done(f"max8_{t}", V.max(m8[:, t, :], lg[:, t, 0:EXPERTS]))
                own(f"max8_{t}")
                DVE.done(f"top{t}", V.tensor_copy(top4[:, t, 0:TOP_K], m8[:, t, 0:TOP_K]))
                DVE.done(f"nm1_{t}", V.tensor_scalar(n_m1[:, t:t + 1], m8[:, t, 0:1], -1.0, None, ALU.mult))
                own(f"top{t}")
                DVE.done(f"rep{t}", V.match_replace(rep[:, t, 0:36], top4[:, t, :], lg[:, t, 0:36], -LOW))
                own(f"rep{t}")
                DVE.done(f"mask{t}", V.tensor_tensor(mask[:, t, :], rep[:, t, 0:EXPERTS], lg[:, t, 0:EXPERTS], ALU.not_equal))

            ffn_gain = gains[:, 8:16].unsqueeze(2).to_broadcast([P, KD, SLOT])

            def take_tokens(b, ps):
                V.tensor_tensor(xeT[b].rearrange("p (k j) -> p k j", k=KD), ps[:, :].rearrange("p (k j) -> p k j", k=KD),
                                ffn_gain, ALU.mult).then_inc(xet_ready, 1)

            residual(0, 0)
            residual(1, 0)
            residual(0, 1)
            mean2(0)
            h2(0, 0)
            h2(1, 0)
            h2(0, 1)
            residual(1, 1)
            mean2(1)
            DVE.done("low", V.memset(lg[:, :, EXPERTS:EXPERTS + 4], LOW))
            DVE.done("low4", V.memset(top4[:, :, TOP_K:8], LOW))
            DVE.done("first0", V.memset(slot_first[:, 0:EXPERTS], 0.0))
            logits(0)
            h2(1, 1)
            choose(0)
            logits(1)
            choose(1)
            for t in range(TT):
                src = ps(f"rank{t}")
                DVE.done(f"posr{t}", V.scalar_tensor_tensor(pos[:, t, :], src[:, 0:EXPERTS], 1.0, mask[:, t, :], ALU.add, ALU.mult))
                own(f"posr{t}")
                DVE.done(f"pos{t}", V.tensor_scalar(pos[:, t, :], pos[:, t, :], -1.0, None, ALU.add))
            own("pos1")
            for t in range(TT):
                DVE.done(f"sel0{t}", V.tensor_scalar(sel[0][:, t, :], iota, pos[:, t, 0:1], None, ALU.is_equal))
            E = EXPERTS
            DVE.done("cnt", V.tensor_copy(cnt[0:E], ps("cnt", E)[:, 0:1]))
            own("cnt")
            DVE.done("x1", V.tensor_scalar(extra[0:E], cnt[0:E], float(SLOT), None, ALU.is_gt))
            own("x1")
            DVE.done("x2", V.scalar_tensor_tensor(extra[0:E], cnt[0:E], 2.0 * SLOT, extra[0:E], ALU.is_gt, ALU.add))
            own("x2")
            DVE.done("x3", V.scalar_tensor_tensor(extra[0:E], cnt[0:E], 3.0 * SLOT, extra[0:E], ALU.is_gt, ALU.add))
            for t in range(TT):
                dve.wait_ge(act_steps, ACTS.at(f"exp{t}"))
                DVE.done(f"gm{t}", V.tensor_tensor(ex[:, t, :], ex[:, t, :], mask[:, t, :], ALU.mult))
                own(f"gm{t}")
                DVE.done(f"gden{t}", V.tensor_reduce(g_den[:, t:t + 1], ex[:, t, :], AX, ALU.add))
                own(f"gden{t}")
                DVE.done(f"grd{t}", V.reciprocal(g_den[:, t:t + 1], g_den[:, t:t + 1]))
                own(f"grd{t}")
                DVE.done(f"gate{t}", V.tensor_scalar(gate[:, t, :], ex[:, t, :], g_den[:, t:t + 1], None, ALU.mult))
            DVE.done("cum", V.tensor_copy(cum[0:E], ps("cum", E)[:, 0:1]))
            own("cum")
            DVE.done("td", V.tensor_scalar(tdist, iota[0:E, 0:MORE], cum[0:E], None, ALU.subtract))
            own("td")
            DVE.done("tge", V.tensor_scalar(tlow, tdist, 0.0, None, ALU.is_ge))
            DVE.done("tlt", V.tensor_scalar(table_in[:, 0:MORE], tdist, extra[0:E], None, ALU.is_lt))
            own("tlt")
            DVE.done("tA", V.tensor_tensor(table_in[:, 0:MORE], table_in[:, 0:MORE], tlow, ALU.mult))
            own("tA")
            DVE.done("tR", V.scalar_tensor_tensor(table_in[:, MORE:2 * MORE], tdist, 1.0, table_in[:, 0:MORE], ALU.add, ALU.mult))
            DVE.done("tE", V.tensor_scalar(table_in[:, 2 * MORE:3 * MORE], table_in[:, 0:MORE], row_id[0:E], None, ALU.mult))
            for t in range(TT):
                DVE.done(f"selG{t}", V.tensor_scalar(selG[:, t, 0, :], iota, pos[:, t, 0:1], gate[:, t, 0:1], ALU.is_equal, ALU.mult))
            for n in range(4):
                if n >= 2:
                    _, engine, step = jobs[job_at[f"y_zero{n}"] - 8]
                    if engine == "act":
                        dve.wait_ge(act_steps, ACTS.at(step))
                    else:
                        own(step)
                DVE.done(f"y_zero{n}", V.memset(y_banks[n][:, :], 0.0))
            DVE.done("table", V.tensor_copy(table, ps("table")[:, 0:3 * MORE]))
            own("table")
            DVE.done("pairsum", V.tensor_reduce(pairs[0:1], table[0:1, 0:MORE].rearrange("p (s two) -> p two s", two=2)[:, 0, :], AX, ALU.add))
            own("pairsum")
            DVE.done("turns_less", V.tensor_scalar(turns[0:1, 1:2], pairs[0:1], float(EXPERTS // 2 - 1), None, ALU.add))
            DVE.done("turns", V.tensor_scalar(turns[0:1, 0:1], pairs[0:1], float(EXPERTS // 2), None, ALU.add))
            DVE.done("slots_e", V.tensor_copy(slot_e[0:1, EXPERTS:SLOTS], table[0:1, 2 * MORE:3 * MORE]))
            DVE.done("main_e", V.tensor_copy(slot_e[0:1, 0:EXPERTS], expert_id[0:1, :]))
            DVE.done("first_m", V.tensor_scalar(slot_first[:, EXPERTS:SLOTS], table[:, 0:MORE], -8.0 * SLOT, 8.0 * SLOT, ALU.mult, ALU.add))
            own("first_m")
            DVE.done("first", V.scalar_tensor_tensor(slot_first[:, EXPERTS:SLOTS], table[:, MORE:2 * MORE], float(SLOT), slot_first[:, EXPERTS:SLOTS], ALU.mult, ALU.add))

            def select(b, steps, pair_read=None):
                dve.wait_ge(select_steps, steps)
                if pair_read is not None:
                    dve.wait_ge(gt_done, pair_read)
                for t in range(TT):
                    V.tensor_scalar(sel[b][:, t, :], iota, rel_pos[b][:, t:t + 1], None, ALU.is_equal)
                    last = V.tensor_scalar(selG[:, t, b, :], iota, rel_pos[b][:, t:t + 1], slot_gate[b][:, t:t + 1],
                                           ALU.is_equal, ALU.mult)
                last.then_inc(sel_ready, 1)

            dve.wait_ge(xet_done, 1)
            take_tokens(0, bank[job_at["gather0"] % 8])
            n_turns = dve.value_load(turns[0:1, 0:1], min_val=EXPERTS // 2, max_val=(EXPERTS + MAX_MORE) // 2)
            with dve.Fori(0, n_turns) as i:
                for b in range(2):
                    n = i * 2 + b
                    select(1 - b, (n + 1) * SEL_OPS, pair_read=i + 1 if b == 1 else None)
                    dve.wait_ge(gu_used, (n + 1) * NCHUNK)
                    V.tensor_scalar(g_sb, ps_gate[:, :], LIMIT, None, ALU.min).then_inc(gate_ready, 1)
                    V.tensor_scalar(u_sb, ps_up[:, :], LIMIT, -LIMIT, ALU.min, ALU.max).then_inc(up_ready, 1)
                    dve.wait_ge(gate_ready, n + 1)
                    dve.wait_ge(up_ready, n + 1)
                    V.scalar_tensor_tensor(u_sb, u_sb, 1.0, g_sb, ALU.add, ALU.mult).then_inc(upgate_ready, 1)
                    dve.wait_ge(upgate_ready, n + 1)
                    dve.wait_ge(sig_ready, n + 1)
                    V.tensor_tensor(h_sb, h_sb, u_sb, ALU.mult).then_inc(h_ready, 1)
                    dve.wait_ge(xet_done, n + 2)
                    take_tokens(1 - b, ps_a)
            for t in range(TT):
                for h in range(2):
                    dve.wait_ge(y_final, 2 * t + h + 1)
                    V.tensor_tensor(y_out[:, t, h * HALF:(h + 1) * HALF], y_acc[t][h][:, :], xs[:, t, h * HALF:(h + 1) * HALF],
                                    ALU.add).then_inc(out_ready, 1)

        @block.gpsimd
        def _(pool):
            G = nc.gpsimd

            def own(name):
                pool.wait_ge(pool_steps, POOL.at(name))

            def rotate(kind, t, o, scratch, cos, sin):
                POOL.done(f"{kind}c{t}", G.tensor_tensor(scratch[0], o, cos, ALU.mult))
                POOL.done(f"{kind}s1{t}", G.tensor_tensor(scratch[1][..., 0:32], o[..., 32:64], sin[..., 0:32], ALU.mult))
                POOL.done(f"{kind}s2{t}", G.tensor_tensor(scratch[1][..., 32:64], o[..., 0:32], sin[..., 32:64], ALU.mult))
                own(f"{kind}s2{t}")
                return G.tensor_tensor(o, scratch[0], scratch[1], ALU.add)

            def root(name, r, n, made):
                pool.wait_ge(dve_steps, DVE.at(made))
                POOL.done(name, G.tensor_tensor(r, r, minus_half[:, :].to_broadcast([P, n]), ALU.pow))

            POOL.done("half", G.memset(minus_half[:, :], -0.5))
            own("half")
            for t in range(TT):
                root(f"px{t}", r_x[:, t:t + 1], 1, f"rx{t}")
            for t in range(TT):
                root(f"pc{t}", r_c[:, t, :], 2, f"rc{t}")
            pool.wait_ge(ld["const"], 16)
            pool.wait_ge(ld["gains"], 16 * GAIN_DMAS)
            for t in range(TT):
                k = k_rot[:, t, :]
                pool.wait_ge(act_steps, ACTS.at(f"pE{t}"))
                POOL.done(f"gk{t}", G.tensor_tensor(k, pr[:, t, KPE_COL:IN_W], gk_rope[:, :], ALU.mult))
                own(f"gk{t}")
                last = rotate("k", t, k, (rs0[:, 0, :], rs1[:, 0, :]), cos2[:, t, :], sin2[:, t, :])
                POOL.done(f"kadd{t}", last)
                own(f"kadd{t}")
            for t in range(TT):
                q = sq[:, 1024 + t * 512:1280 + t * 512].rearrange("p (h r) -> p h r", h=4)
                pool.wait_ge(act_steps, ACTS.at(f"qbb{t}"))
                POOL.done(f"gq{t}", G.tensor_tensor(q, qb[:, t, :, NOPE:QK_DIM], gq_rope[:, :].unsqueeze(1).to_broadcast([P, 4, ROPE]), ALU.mult))
                own(f"gq{t}")
                last = rotate("q", t, q, (rs0[:, :, :], rs1[:, :, :]), cos2[:, t, :].unsqueeze(1).to_broadcast([P, 4, ROPE]),
                              sin2[:, t, :].unsqueeze(1).to_broadcast([P, 4, ROPE]))
                POOL.done(f"qadd{t}", last)
                own(f"qadd{t}")
                root(f"pq{t}", r_q[:, t, :], 4, f"rq{t}")
                root(f"pk{t}", r_k[:, t, :], 4, f"rk{t}")
                root(f"pa{t}", r_a[:, t, :], 16, f"rAk{t}")
            POOL.done("zero_y", G.memset(short[:, :], 0.0))
            pool.wait_ge(pe_steps, PE.at("mT11"))
            POOL.done("zero_b", G.memset(b_gu, 0.0))
            POOL.done("zero_G", G.memset(GT, 0.0))
            POOL.done("onehot0", G.tensor_copy(onehot[0], ident[:, 0:1].to_broadcast([P, SLOT])))
            for t in range(TT):
                root(f"p2{t}", r_2[:, t:t + 1], 1, f"r2{t}")

            def select(b, n):
                e = pool.value_load(slot_e[0:1, bass.ds(n, 1)], min_val=0, max_val=EXPERTS - 1)
                first = slot_first[:, bass.ds(n, 1)]
                G.tensor_tensor(rel_pos[b].unsqueeze(2), pos[:, :, bass.ds(e, 1)], first.unsqueeze(1).to_broadcast([P, TT, 1]),
                                ALU.subtract).then_inc(select_steps, 1)
                G.tensor_copy(slot_gate[b].unsqueeze(2), gate[:, :, bass.ds(e, 1)]).then_inc(select_steps, 1)
                G.tensor_copy(onehot[b], ident[:, bass.ds(e, 1)].to_broadcast([P, SLOT])).then_inc(select_steps, 1)

            pool.wait_ge(dve_steps, DVE.at("first"))
            n_turns = pool.value_load(turns[0:1, 0:1], min_val=EXPERTS // 2, max_val=(EXPERTS + MAX_MORE) // 2)
            with pool.Fori(0, n_turns) as i:
                for b in range(2):
                    pool.wait_ge(xet_done, i * 2 + b + 1)
                    select(1 - b, i * 2 + b + 1)


_INS = ['x', 'attn_norm_g', 'w_in', 'a_q_norm_g', 'a_k_norm_g', 'rel_bias', 'q_a_norm_g', 'w_q_b', 'kv_a_norm_g', 'w_kv_b',
        'b_q_norm_g', 'b_k_norm_g', 'w_out', 'ffn_norm_g', 'router_w', 'router_b', 'w_gate_up', 'b_gate_up', 'w_down', 'b_down']


def kernel(**inputs):
    import numpy as _np
    import concourse.bacc as _bacc
    from concourse import mybir as _mybir
    from concourse.bass_utils import run_bass_kernel_spmd as _run

    nc = _bacc.Bacc("TRN2", target_bir_lowering=False, num_devices=1, dynamic_dma_scratch_size=1024)
    c_all, c_rel = constants()
    arrays, args = {}, []
    for name, a in [(n, inputs[n]) for n in _INS] + [("c_all", c_all), ("c_rel", c_rel)]:
        a = _np.ascontiguousarray(a)
        arrays[f"in_{name}_dram"] = a
        args.append(nc.dram_tensor(f"in_{name}_dram", a.shape, _mybir.dt.from_np(a.dtype), kind="ExternalInput").ap())
    args.append(nc.dram_tensor("out_0_dram", (1, SEQ, D), _mybir.dt.float32, kind="ExternalOutput").ap())
    for i, name in enumerate(_INS):
        if name in ("w_gate_up", "w_down"):
            args[i] = args[i][0]
    layer_kernel(nc, *args)
    r = _run(nc, [arrays], core_ids=[0])
    return r.results[0]["out_0_dram"]
```
